# Optimizing a Trainium2 kernel written in Bass

```python
import jax
import jax.numpy as jnp
from jax import lax
import numpy as np
import jax, jax.numpy as jnp

D_MODEL = 1024
BATCH = 1
SEQ = 256
DEPTH = 2

CTX_LEN = 256
GRID_W = 64
HEAD_DIM = 64
NA_WIDTH = D_MODEL // 2
NA_HEADS = NA_WIDTH // HEAD_DIM
NA_WIN_ROWS = 8
NA_WIN_COLS = 16
NA_QCB = 16
NA_KCB = 32
RW_WIDTH = D_MODEL // 4
RW_HEADS = RW_WIDTH // HEAD_DIM
RW_DECAY_RANK = 64
RW_A_RANK = 64
RW_GATE_RANK = 128
RW_LORA = RW_DECAY_RANK + RW_A_RANK + RW_GATE_RANK
RW_IN = 3 * RW_WIDTH + 2 * RW_LORA
RW_GN_EPS = 64e-5
CV_WIDTH = D_MODEL // 4
CV_CONV_LEN = 31
MIX_WIDTH = NA_WIDTH + RW_WIDTH + CV_WIDTH
IN_WIDTH = 3 * NA_WIDTH + RW_IN + 2 * CV_WIDTH
D_FF = 2816
N_EXPERTS = 8
TOP_K = 2
D_FF_EXPERT = 3584
MOE_BLOCK = 128
N_DENSE_LAYERS = (DEPTH + 1) // 2
N_MOE_LAYERS = DEPTH // 2
RMS_EPS = 1e-6
LN_EPS = 1e-5


def _rmsnorm(x, g):
    xf = x.astype(jnp.float32)
    y = xf * lax.rsqrt(jnp.mean(xf * xf, axis=-1, keepdims=True) + RMS_EPS)
    return (y * g.astype(jnp.float32)).astype(x.dtype)

def _layernorm(x, g, b):
    xf = x.astype(jnp.float32)
    mu = jnp.mean(xf, axis=-1, keepdims=True)
    var = jnp.mean(jnp.square(xf - mu), axis=-1, keepdims=True)
    y = (xf - mu) * lax.rsqrt(var + LN_EPS)
    return (y * g.astype(jnp.float32) + b.astype(jnp.float32)).astype(x.dtype)

def _modulate(h, shift, scale):
    return h * (1 + scale) + shift

def _swiglu(h, w_gate, w_up, w_down):
    return (jax.nn.silu(h @ w_gate) * (h @ w_up)) @ w_down

def _moe_swiglu(h, router, w_gate, w_up, w_down):
    shp = h.shape
    d = shp[-1]
    xt = h.reshape(-1, d)
    n_tok = xt.shape[0]
    n_asg = n_tok * TOP_K
    logits = (xt @ router).astype(jnp.float32)
    top_logit, top_e = lax.top_k(logits, TOP_K)
    gates = jax.nn.softmax(top_logit, axis=-1)
    flat_e = top_e.reshape(-1)
    flat_tok = jnp.arange(n_asg, dtype=jnp.int32) // TOP_K
    order = jnp.argsort(flat_e)
    s_e = flat_e[order]
    s_tok = flat_tok[order]
    s_gate = gates.reshape(-1)[order]
    counts = jnp.bincount(flat_e, length=N_EXPERTS)
    padded = (counts + MOE_BLOCK - 1) // MOE_BLOCK * MOE_BLOCK
    pad_end = jnp.cumsum(padded)
    pad_start = pad_end - padded
    start = jnp.cumsum(counts) - counts
    dest = pad_start[s_e] + jnp.arange(n_asg, dtype=jnp.int32) - start[s_e]
    n_blocks = (n_asg + MOE_BLOCK - 1) // MOE_BLOCK + N_EXPERTS
    slot_tok = jnp.full((n_blocks * MOE_BLOCK,), n_tok, jnp.int32).at[dest].set(s_tok)
    block_e = jnp.minimum(jnp.searchsorted(pad_end, jnp.arange(n_blocks) * MOE_BLOCK, side='right'), N_EXPERTS - 1)
    x_pad = jnp.concatenate([xt, jnp.zeros((1, d), xt.dtype)], axis=0)
    xb = x_pad[slot_tok].reshape(n_blocks, MOE_BLOCK, d)

    def expert_block(args):
        x_blk, e = args
        return _swiglu(x_blk, w_gate[e], w_up[e], w_down[e])

    yb = lax.map(expert_block, (xb, block_e)).reshape(-1, d)
    y = jnp.zeros_like(xt).at[s_tok].add(yb[dest] * s_gate[:, None].astype(xt.dtype))
    return y.reshape(shp)

def _na_column_layout():
    n_cb = GRID_W // NA_QCB
    q_cols = np.arange(GRID_W).reshape(n_cb, NA_QCB)
    blk_start = np.clip(np.arange(n_cb) * NA_QCB - NA_WIN_COLS // 2, 0, GRID_W - NA_KCB)
    key_cols = blk_start[:, None] + np.arange(NA_KCB)[None, :]
    win_start = np.clip(q_cols - NA_WIN_COLS // 2, 0, GRID_W - NA_WIN_COLS)
    kcol = key_cols[:, None, :]
    ws = win_start[:, :, None]
    mask = (kcol >= ws) & (kcol < ws + NA_WIN_COLS)
    rel_idx = np.clip(kcol - q_cols[:, :, None] + NA_WIN_COLS - 1, 0, 2 * NA_WIN_COLS - 2)
    return key_cols, mask, rel_idx

def _neighbourhood_attention(q, k, v, kc, vc, rpb):
    B, N, H, dh = q.shape
    rows = N // GRID_W
    kr = min(NA_WIN_ROWS, rows)
    n_cb = GRID_W // NA_QCB
    key_cols, col_mask, rel_idx = _na_column_layout()
    qg = (q * dh ** -0.5).reshape(B, rows, GRID_W, H, dh).transpose(1, 0, 3, 2, 4)
    kg = k.reshape(B, rows, GRID_W, H, dh).transpose(0, 3, 1, 2, 4)
    vg = v.reshape(B, rows, GRID_W, H, dh).transpose(0, 3, 1, 2, 4)
    kct = kc.transpose(0, 2, 1, 3)
    vct = vc.transpose(0, 2, 1, 3)
    rpb_cols = rpb[:, :, rel_idx]
    n_win = kr * NA_KCB

    def one_row(args):
        i, qi = args
        rs = jnp.clip(i - kr // 2, 0, rows - kr)
        ks = lax.dynamic_slice_in_dim(kg, rs, kr, axis=2)[:, :, :, key_cols]
        vs = lax.dynamic_slice_in_dim(vg, rs, kr, axis=2)[:, :, :, key_cols]
        qb = qi.reshape(B, H, n_cb, NA_QCB, dh)
        s_win = jnp.einsum('bhcqd,bhrckd->bhcqrk', qb, ks).astype(jnp.float32)
        bias = lax.dynamic_slice_in_dim(rpb_cols, rs - i + NA_WIN_ROWS - 1, kr, axis=1)
        bias = bias.transpose(0, 2, 3, 1, 4).astype(jnp.float32)
        s_win = jnp.where(col_mask[:, :, None, :], s_win + bias, -jnp.inf)
        s_ctx = jnp.einsum('bhcqd,bhld->bhcql', qb, kct).astype(jnp.float32)
        s = jnp.concatenate([s_win.reshape(B, H, n_cb, NA_QCB, n_win), s_ctx], axis=-1)
        p = jax.nn.softmax(s, axis=-1).astype(v.dtype)
        p_win = p[..., :n_win].reshape(B, H, n_cb, NA_QCB, kr, NA_KCB)
        o = (jnp.einsum('bhcqrk,bhrckd->bhcqd', p_win, vs)
             + jnp.einsum('bhcql,bhld->bhcqd', p[..., n_win:], vct))
        return o.reshape(B, H, GRID_W, dh)

    out = lax.map(one_row, (jnp.arange(rows), qg))
    return out.transpose(1, 0, 3, 2, 4).reshape(B, N, H * dh)

def _context_attention(q, k, v):
    B, L, H, dh = q.shape
    s = jnp.einsum('blhd,bmhd->bhlm', q, k).astype(jnp.float32) * (dh ** -0.5)
    p = jax.nn.softmax(s, axis=-1).astype(v.dtype)
    return jnp.einsum('bhlm,bmhd->blhd', p, v).reshape(B, L, H * dh)

def _token_shift(u, mu_prev, mu_next):
    zero = jnp.zeros_like(u[:, :1])
    prev = jnp.concatenate([zero, u[:, :-1]], axis=1)
    nxt = jnp.concatenate([u[:, 1:], zero], axis=1)
    return u + mu_prev * (prev - u) + mu_next * (nxt - u)

def _head_norm(y, g, b):
    mu = jnp.mean(y, axis=-1, keepdims=True)
    var = jnp.mean(jnp.square(y - mu), axis=-1, keepdims=True)
    yn = (y - mu) * lax.rsqrt(var + RW_GN_EPS)
    return yn.reshape(y.shape[0], y.shape[1], -1) * g + b

def _rwkv7_scan(r, w, k, v, z, b):
    G, H, dh = r.shape[1:]

    def step(S, inp):
        r_t, w_t, k_t, v_t, z_t, b_t = inp
        s_z = jnp.einsum('ghvk,ghk->ghv', S, z_t)
        S = S * w_t[:, :, None, :] + s_z[..., None] * b_t[:, :, None, :] + v_t[..., None] * k_t[:, :, None, :]
        return S, jnp.einsum('ghvk,ghk->ghv', S, r_t)

    _, y = lax.scan(step, jnp.zeros((G, H, dh, dh), jnp.float32), (r, w, k, v, z, b))
    return y

def _bi_rwkv7(ul, uc, mu_prev, mu_next, w0, w2, a0, a2, g2, k_k, k_a, r_k, gn_g, gn_b, need_ctx_out):
    B, N, _ = ul.shape
    L = uc.shape[1]
    T = L + N
    u = jnp.concatenate([_token_shift(uc, mu_prev, mu_next), _token_shift(ul, mu_prev, mu_next)],
                        axis=1).astype(jnp.float32)
    heads = lambda t: t.reshape(B, T, RW_HEADS, HEAD_DIM)
    r = u[..., :RW_WIDTH]
    k = u[..., RW_WIDTH:2 * RW_WIDTH]
    v = u[..., 2 * RW_WIDTH:3 * RW_WIDTH]
    kk = heads(k * k_k)
    kk = kk * lax.rsqrt(jnp.sum(kk * kk, axis=-1, keepdims=True) + 1e-12)
    rh, vh = heads(r), heads(v)
    per_dir = []
    for d in range(2):
        lo = 3 * RW_WIDTH + d * RW_LORA
        wd = u[..., lo:lo + RW_DECAY_RANK]
        ad = u[..., lo + RW_DECAY_RANK:lo + RW_DECAY_RANK + RW_A_RANK]
        gd = u[..., lo + RW_DECAY_RANK + RW_A_RANK:lo + RW_LORA]
        log_w = -jax.nn.softplus(-(w0[d] + jnp.tanh(wd) @ w2[d])) - 0.5
        decay = jnp.exp(-jnp.exp(log_w))
        a = jax.nn.sigmoid(a0[d] + ad @ a2[d])
        g = jax.nn.sigmoid(gd) @ g2[d]
        kd = heads(k * (1.0 + (a - 1.0) * k_a))
        per_dir.append((heads(decay), kd, kk * heads(a), g))
    perm = np.concatenate([np.arange(L)[::-1], L + np.arange(N)[::-1]])

    def stack(t_f, t_b):
        return jnp.concatenate([t_f, t_b[:, perm]], axis=0).swapaxes(0, 1)

    (w_f, k_f, b_f, _), (w_b, k_b, b_b, _) = per_dir
    y = _rwkv7_scan(stack(rh, rh), stack(w_f, w_b), stack(k_f, k_b), stack(vh, vh),
                    stack(-kk, -kk), stack(b_f, b_b)).swapaxes(0, 1)
    t0 = 0 if need_ctx_out else L
    y_dirs = (y[:B, t0:], y[B:][:, perm][:, t0:])
    outs = []
    for (_, kd, _, g), yd in zip(per_dir, y_dirs):
        bonus = (jnp.sum(rh * kd * r_k, axis=-1, keepdims=True) * vh)[:, t0:].reshape(B, T - t0, RW_WIDTH)
        outs.append((_head_norm(yd, gn_g, gn_b) + bonus) * g[:, t0:])
    out = (outs[0] + outs[1]).astype(ul.dtype)
    out_l = out[:, L - t0:]
    out_c = out[:, :L] if need_ctx_out else None
    return out_l, out_c

def _conformer_conv(u, dw_w, dw_b, ln_g, ln_b):
    h = u[..., :CV_WIDTH] * jax.nn.sigmoid(u[..., CV_WIDTH:])
    h = lax.conv_general_dilated(h, dw_w[:, None, :], (1,), [(CV_CONV_LEN // 2, CV_CONV_LEN // 2)],
                                 dimension_numbers=('NWC', 'WIO', 'NWC'),
                                 feature_group_count=CV_WIDTH) + dw_b
    return jax.nn.silu(_layernorm(h, ln_g, ln_b))

def _mixers(hl, hc, w_in, w_out, na_rpb, rw_mu_prev, rw_mu_next, rw_w0, rw_w2, rw_a0, rw_a2, rw_g2,
            rw_k_k, rw_k_a, rw_r_k, rw_gn_g, rw_gn_b, cv_dw_w, cv_dw_b, cv_ln_g, cv_ln_b, need_ctx_out):
    o_rw = 3 * NA_WIDTH
    o_cv = o_rw + RW_IN
    heads = lambda t: t.reshape(t.shape[0], t.shape[1], NA_HEADS, HEAD_DIM)
    pl = hl @ w_in
    c_off = 0 if need_ctx_out else NA_WIDTH
    pc = hc @ (w_in if need_ctx_out else w_in[:, NA_WIDTH:o_cv])
    kc = heads(pc[..., NA_WIDTH - c_off:2 * NA_WIDTH - c_off])
    vc = heads(pc[..., 2 * NA_WIDTH - c_off:o_rw - c_off])
    na_l = _neighbourhood_attention(heads(pl[..., :NA_WIDTH]), heads(pl[..., NA_WIDTH:2 * NA_WIDTH]),
                                    heads(pl[..., 2 * NA_WIDTH:o_rw]), kc, vc, na_rpb)
    rw_l, rw_c = _bi_rwkv7(pl[..., o_rw:o_cv], pc[..., o_rw - c_off:o_cv - c_off], rw_mu_prev, rw_mu_next,
                           rw_w0, rw_w2, rw_a0, rw_a2, rw_g2, rw_k_k, rw_k_a, rw_r_k, rw_gn_g, rw_gn_b,
                           need_ctx_out)
    cv_l = _conformer_conv(pl[..., o_cv:], cv_dw_w, cv_dw_b, cv_ln_g, cv_ln_b)
    out_l = jnp.concatenate([na_l, rw_l, cv_l], axis=-1) @ w_out
    if not need_ctx_out:
        return out_l, None
    na_c = _context_attention(heads(pc[..., :NA_WIDTH]), kc, vc)
    cv_c = _conformer_conv(pc[..., o_cv:], cv_dw_w, cv_dw_b, cv_ln_g, cv_ln_b)
    out_c = jnp.concatenate([na_c, rw_c, cv_c], axis=-1) @ w_out
    return out_l, out_c

def first_inputs(seed: int = 0) -> dict:
    key = jax.random.key(seed)
    ks = iter(jax.random.split(key, 40))
    f32 = jnp.float32

    def nrm(shape, std):
        return jax.random.normal(next(ks), shape, f32) * std

    def uni(shape, lo, hi):
        return jax.random.uniform(next(ks), shape, f32, lo, hi)

    D = D_MODEL
    return {
        'x': nrm((BATCH, SEQ, D), 1.0),
        'c': nrm((BATCH, D), 1.0),
        'ctx': nrm((BATCH, CTX_LEN, D), 1.0),
        'c_ctx': nrm((D,), 1.0),
        'norm1_g': 1.0 + nrm((DEPTH, D), 0.02),
        'norm2_g': 1.0 + nrm((DEPTH, D), 0.02),
        'mod_w': nrm((DEPTH, D, 6 * D), 0.5 * D ** -0.5),
        'mod_b': nrm((DEPTH, 6 * D), 0.02),
        'w_in': nrm((DEPTH, D, IN_WIDTH), D ** -0.5),
        'w_out': nrm((DEPTH, MIX_WIDTH, D), MIX_WIDTH ** -0.5),
        'na_rpb': nrm((DEPTH, NA_HEADS, 2 * NA_WIN_ROWS - 1, 2 * NA_WIN_COLS - 1), 0.1),
        'rw_mu_prev': uni((DEPTH, RW_IN), 0.0, 0.5),
        'rw_mu_next': uni((DEPTH, RW_IN), 0.0, 0.5),
        'rw_w0': uni((DEPTH, 2, RW_WIDTH), -6.0, 1.0),
        'rw_w2': nrm((DEPTH, 2, RW_DECAY_RANK, RW_WIDTH), 0.5 * RW_DECAY_RANK ** -0.5),
        'rw_a0': nrm((DEPTH, 2, RW_WIDTH), 0.3),
        'rw_a2': nrm((DEPTH, 2, RW_A_RANK, RW_WIDTH), 0.5 * RW_A_RANK ** -0.5),
        'rw_g2': nrm((DEPTH, 2, RW_GATE_RANK, RW_WIDTH), RW_GATE_RANK ** -0.5),
        'rw_k_k': 0.85 + nrm((DEPTH, RW_WIDTH), 0.02),
        'rw_k_a': 1.0 + nrm((DEPTH, RW_WIDTH), 0.02),
        'rw_r_k': nrm((DEPTH, RW_HEADS, HEAD_DIM), 0.1),
        'rw_gn_g': 1.0 + nrm((DEPTH, RW_WIDTH), 0.02),
        'rw_gn_b': nrm((DEPTH, RW_WIDTH), 0.02),
        'cv_dw_w': nrm((DEPTH, CV_CONV_LEN, CV_WIDTH), CV_CONV_LEN ** -0.5),
        'cv_dw_b': nrm((DEPTH, CV_WIDTH), 0.02),
        'cv_ln_g': 1.0 + nrm((DEPTH, CV_WIDTH), 0.02),
        'cv_ln_b': nrm((DEPTH, CV_WIDTH), 0.02),
        'ffn_w_gate': nrm((N_DENSE_LAYERS, D, D_FF), D ** -0.5),
        'ffn_w_up': nrm((N_DENSE_LAYERS, D, D_FF), D ** -0.5),
        'ffn_w_down': nrm((N_DENSE_LAYERS, D_FF, D), D_FF ** -0.5),
        'moe_router': nrm((N_MOE_LAYERS, D, N_EXPERTS), D ** -0.5),
        'moe_w_gate': nrm((N_MOE_LAYERS, N_EXPERTS, D, D_FF_EXPERT), D ** -0.5),
        'moe_w_up': nrm((N_MOE_LAYERS, N_EXPERTS, D, D_FF_EXPERT), D ** -0.5),
        'moe_w_down': nrm((N_MOE_LAYERS, N_EXPERTS, D_FF_EXPERT, D), D_FF_EXPERT ** -0.5),
        'final_g': 1.0 + nrm((D,), 0.02),
    }

def first_block(x, c, ctx, c_ctx, norm1_g, norm2_g, mod_w, mod_b, w_in, w_out, na_rpb, rw_mu_prev, rw_mu_next,
              rw_w0, rw_w2, rw_a0, rw_a2, rw_g2, rw_k_k, rw_k_a, rw_r_k, rw_gn_g, rw_gn_b, cv_dw_w, cv_dw_b,
              cv_ln_g, cv_ln_b, ffn_w_gate, ffn_w_up, ffn_w_down, moe_router, moe_w_gate, moe_w_up, moe_w_down,
              final_g):
    c_sil = jax.nn.silu(c)
    cc_sil = jax.nn.silu(c_ctx)
    xl, xc = x, ctx
    for layer in range(DEPTH):
        need_ctx = layer < DEPTH - 1
        sh1, sc1, g1, sh2, sc2, g2 = jnp.split((c_sil @ mod_w[layer] + mod_b[layer])[:, None, :], 6, axis=-1)
        csh1, csc1, cg1, csh2, csc2, cg2 = jnp.split(cc_sil @ mod_w[layer] + mod_b[layer], 6, axis=-1)
        hl = _modulate(_rmsnorm(xl, norm1_g[layer]), sh1, sc1)
        hc = _modulate(_rmsnorm(xc, norm1_g[layer]), csh1, csc1)
        mix_l, mix_c = _mixers(hl, hc, w_in[layer], w_out[layer], na_rpb[layer], rw_mu_prev[layer],
                               rw_mu_next[layer], rw_w0[layer], rw_w2[layer], rw_a0[layer], rw_a2[layer],
                               rw_g2[layer], rw_k_k[layer], rw_k_a[layer], rw_r_k[layer], rw_gn_g[layer],
                               rw_gn_b[layer], cv_dw_w[layer], cv_dw_b[layer], cv_ln_g[layer], cv_ln_b[layer],
                               need_ctx)
        xl = xl + g1 * mix_l
        hl = _modulate(_rmsnorm(xl, norm2_g[layer]), sh2, sc2)
        j = layer // 2
        if layer % 2 == 0:
            xl = xl + g2 * _swiglu(hl, ffn_w_gate[j], ffn_w_up[j], ffn_w_down[j])
        else:
            xl = xl + g2 * _moe_swiglu(hl, moe_router[j], moe_w_gate[j], moe_w_up[j], moe_w_down[j])
        if need_ctx:
            xc = xc + cg1 * mix_c
            hc = _modulate(_rmsnorm(xc, norm2_g[layer]), csh2, csc2)
            if layer % 2 == 0:
                xc = xc + cg2 * _swiglu(hc, ffn_w_gate[j], ffn_w_up[j], ffn_w_down[j])
            else:
                xc = xc + cg2 * _moe_swiglu(hc, moe_router[j], moe_w_gate[j], moe_w_up[j], moe_w_down[j])
    return _rmsnorm(xl, final_g)


D_MIX = D_MODEL
N_Q_HEADS = 8
N_KV_HEADS = 2
GQA_GROUP = N_Q_HEADS // N_KV_HEADS
ATTN_W = N_Q_HEADS * HEAD_DIM
KV_W = N_KV_HEADS * HEAD_DIM
N_SG_HEADS = 4
SG_W = N_SG_HEADS * HEAD_DIM
SG_CHUNK = 128
N_CONV_GROUPS = 4
CONV_W = N_CONV_GROUPS * HEAD_DIM
CONV_K = 3
Q_BLOCK = 128
ROPE_THETA = 10000.0
AXIS_DIM = HEAD_DIM // 2
EPS = 1e-6
PROJ_SPLITS = (ATTN_W, KV_W, KV_W, SG_W, SG_W, CONV_W, CONV_W, CONV_W)
PROJ_W = sum(PROJ_SPLITS)


def _rmsnorm_2(x, g):
    x32 = x.astype(jnp.float32)
    y = x32 * lax.rsqrt(jnp.mean(x32 * x32, axis=-1, keepdims=True) + EPS)
    return y.astype(x.dtype) * g

def _dwconv3(x, w):
    xp = jnp.pad(x, ((0, 0), (1, 1), (0, 0)))
    return xp[:, :-2] * w[0] + xp[:, 1:-1] * w[1] + xp[:, 2:] * w[2]

def _axial_angles(seq):
    rows = seq // GRID_W
    row = jnp.broadcast_to(jnp.arange(rows)[:, None], (rows, GRID_W)).reshape(-1)
    col = jnp.broadcast_to(jnp.arange(GRID_W)[None, :], (rows, GRID_W)).reshape(-1)
    inv = 1.0 / (ROPE_THETA ** (jnp.arange(AXIS_DIM // 2, dtype=jnp.float32) * 2.0 / AXIS_DIM))
    ang_r = row.astype(jnp.float32)[:, None] * inv[None, :]
    ang_c = col.astype(jnp.float32)[:, None] * inv[None, :]
    return ang_r, ang_c

def _rotate(x, cos, sin):
    x1, x2 = jnp.split(x, 2, axis=-1)
    return jnp.concatenate([x1 * cos - x2 * sin, x1 * sin + x2 * cos], axis=-1)

def _axial_rope(x, tabs):
    cr, sr, cc, sc = tabs
    return jnp.concatenate([_rotate(x[..., :AXIS_DIM], cr, sr),
                            _rotate(x[..., AXIS_DIM:], cc, sc)], axis=-1)

def _block_attention(q, k, v):
    b, s = q.shape[0], q.shape[1]
    nblk = s // Q_BLOCK
    scale = HEAD_DIM ** -0.5
    qb = q.reshape(b, nblk, Q_BLOCK, N_KV_HEADS, GQA_GROUP, HEAD_DIM).transpose(1, 0, 2, 3, 4, 5)

    def one_block(qblk):
        sc = jnp.einsum('bqgrd,bkgd->bgrqk', qblk, k).astype(jnp.float32) * scale
        p = jax.nn.softmax(sc, axis=-1).astype(v.dtype)
        return jnp.einsum('bgrqk,bkgd->bqgrd', p, v)

    out = lax.map(one_block, qb)
    return out.transpose(1, 0, 2, 3, 4, 5).reshape(b, s, ATTN_W)

def _spatial_gating(u, v, g_v, w_s, b_s):
    b, s = u.shape[0], u.shape[1]
    nchunk = s // SG_CHUNK
    vn = _rmsnorm_2(v, g_v).reshape(b, nchunk, SG_CHUNK, N_SG_HEADS, HEAD_DIM)
    mixed = jnp.einsum('hpq,bnqhc->bnphc', w_s, vn) + b_s.T[:, :, None]
    return u * mixed.reshape(b, s, SG_W)

def second_inputs(seed: int = 0) -> dict:
    key = jax.random.key(seed)
    ks = jax.random.split(key, 16)
    f32 = jnp.float32
    nrm = lambda k, shape, s: jax.random.normal(k, shape, f32) * s
    res_scale = (2.0 * DEPTH) ** -0.5
    return {
        "x": jax.random.normal(ks[0], (BATCH, SEQ, D_MODEL), f32),
        "norm1_g": 1.0 + nrm(ks[1], (DEPTH, D_MODEL), 0.02),
        "w_in": nrm(ks[2], (DEPTH, D_MODEL, PROJ_W), D_MODEL ** -0.5),
        "q_norm_g": 1.0 + nrm(ks[3], (DEPTH, HEAD_DIM), 0.02),
        "k_norm_g": 1.0 + nrm(ks[4], (DEPTH, HEAD_DIM), 0.02),
        "sg_norm_g": 1.0 + nrm(ks[5], (DEPTH, SG_W), 0.02),
        "sg_w": nrm(ks[6], (DEPTH, N_SG_HEADS, SG_CHUNK, SG_CHUNK), 0.5 * SG_CHUNK ** -0.5),
        "sg_b": 1.0 + nrm(ks[7], (DEPTH, N_SG_HEADS, SG_CHUNK), 0.1),
        "conv_w": nrm(ks[8], (DEPTH, CONV_K, CONV_W), CONV_K ** -0.5),
        "w_out": nrm(ks[9], (DEPTH, D_MIX, D_MODEL), D_MIX ** -0.5 * res_scale),
        "norm2_g": 1.0 + nrm(ks[10], (DEPTH, D_MODEL), 0.02),
        "ffn_w_up": nrm(ks[11], (DEPTH, D_MODEL, 2 * D_FF), D_MODEL ** -0.5),
        "ffn_conv_w": nrm(ks[12], (DEPTH, CONV_K, 2 * D_FF), CONV_K ** -0.5),
        "ffn_w_down": nrm(ks[13], (DEPTH, D_FF, D_MODEL), D_FF ** -0.5 * res_scale),
    }

def second_block(x, norm1_g, w_in, q_norm_g, k_norm_g, sg_norm_g, sg_w, sg_b, conv_w,
              w_out, norm2_g, ffn_w_up, ffn_conv_w, ffn_w_down):
    b, s, _ = x.shape
    ang_r, ang_c = _axial_angles(s)
    dt = x.dtype
    tabs = (jnp.cos(ang_r)[:, None, :].astype(dt), jnp.sin(ang_r)[:, None, :].astype(dt),
            jnp.cos(ang_c)[:, None, :].astype(dt), jnp.sin(ang_c)[:, None, :].astype(dt))
    split_at = np.cumsum(PROJ_SPLITS)[:-1].tolist()

    for l in range(DEPTH):
        h = _rmsnorm_2(x, norm1_g[l])
        p = h @ w_in[l]
        q, k, v, su, sv, cb, cc, cx = jnp.split(p, split_at, axis=-1)

        q = _rmsnorm_2(q.reshape(b, s, N_Q_HEADS, HEAD_DIM), q_norm_g[l])
        k = _rmsnorm_2(k.reshape(b, s, N_KV_HEADS, HEAD_DIM), k_norm_g[l])
        q = _axial_rope(q, tabs)
        k = _axial_rope(k, tabs)
        a_out = _block_attention(q, k, v.reshape(b, s, N_KV_HEADS, HEAD_DIM))

        g_out = _spatial_gating(su, sv, sg_norm_g[l], sg_w[l], sg_b[l])

        c_out = cb * _dwconv3(cc * cx, conv_w[l])

        mix = jnp.concatenate([a_out, g_out, c_out], axis=-1)
        x = x + mix @ w_out[l]

        h2 = _rmsnorm_2(x, norm2_g[l])
        up = _dwconv3(h2 @ ffn_w_up[l], ffn_conv_w[l])
        gate, val = jnp.split(up, 2, axis=-1)
        x = x + (jax.nn.silu(gate) * val) @ ffn_w_down[l]
    return x


def setup_inputs(seed=0):
    out = dict(first_inputs(seed))
    for name, value in second_inputs(seed + 1).items():
        if name != "x":
            out[name + "_2"] = value
    return out


def reference(
    x, c, ctx, c_ctx, norm1_g, norm2_g, mod_w, mod_b, w_in, w_out, na_rpb, rw_mu_prev,
    rw_mu_next, rw_w0, rw_w2, rw_a0, rw_a2, rw_g2, rw_k_k, rw_k_a, rw_r_k, rw_gn_g, rw_gn_b,
    cv_dw_w, cv_dw_b, cv_ln_g, cv_ln_b, ffn_w_gate, ffn_w_up, ffn_w_down, moe_router,
    moe_w_gate, moe_w_up, moe_w_down, final_g, norm1_g_2, w_in_2, q_norm_g_2, k_norm_g_2,
    sg_norm_g_2, sg_w_2, sg_b_2, conv_w_2, w_out_2, norm2_g_2, ffn_w_up_2, ffn_conv_w_2,
    ffn_w_down_2,
):
    x = first_block(
        x, c, ctx, c_ctx, norm1_g, norm2_g, mod_w, mod_b, w_in, w_out, na_rpb, rw_mu_prev,
        rw_mu_next, rw_w0, rw_w2, rw_a0, rw_a2, rw_g2, rw_k_k, rw_k_a, rw_r_k, rw_gn_g, rw_gn_b,
        cv_dw_w, cv_dw_b, cv_ln_g, cv_ln_b, ffn_w_gate, ffn_w_up, ffn_w_down, moe_router,
        moe_w_gate, moe_w_up, moe_w_down, final_g,
    )
    return second_block(
        x, norm1_g_2, w_in_2, q_norm_g_2, k_norm_g_2, sg_norm_g_2, sg_w_2, sg_b_2, conv_w_2,
        w_out_2, norm2_g_2, ffn_w_up_2, ffn_conv_w_2, ffn_w_down_2,
    )


_drawn_inputs = setup_inputs


def setup_inputs(seed=0):
    import zlib

    import numpy as np

    out = dict(_drawn_inputs(seed))
    spreads = {}
    factors = {'norm1_g': 4.32,
     'na_rpb': 8.0,
     'rw_w2': 3.552,
     'rw_k_k': 3.847,
     'rw_k_a': 3.358,
     'rw_gn_g': 5.64,
     'rw_gn_b': 5.291,
     'cv_dw_b': 4.106,
     'cv_ln_g': 8.0,
     'cv_ln_b': 6.199,
     'norm1_g_2': 3.796,
     'q_norm_g_2': 86.993,
     'k_norm_g_2': 83.574,
     'sg_norm_g_2': 45.24,
     'norm2_g_2': 19.362,
     'norm2_g': 3.282,
     'sg_b_2': 4.489}
    for name, (base, spread) in spreads.items():
        noise = np.random.default_rng([zlib.crc32(name.encode()), seed]).standard_normal(out[name].shape)
        drawn = base * np.exp(spread * noise) if base else spread * noise
        out[name] = jnp.asarray(drawn.astype(out[name].dtype))
    for name, factor in factors.items():
        out[name] = (out[name] * factor).astype(out[name].dtype)
    return out
```

```python
from contextlib import ExitStack

import numpy as np

import concourse.bass as bass
from concourse import mybir

F32 = mybir.dt.float32
ACT = mybir.ActivationFunctionType
ALU = mybir.AluOpType
AX = mybir.AxisListType

P = 128
D = 1024
KT = D // P
CTX, LAT = 256, 256
T = CTX + LAT
DH = 64
DEPTH = 2
NA_H, NA_W = 8, 512
RW_W, RW_IN = 256, 1280
CV_TAPS, CV_PAD = 31, 15
D_FF, D_FFE, N_EXP = 2816, 3584, 8
UNIT = 256
PART = KT * UNIT
RING = 6
CH = 64
NCH = T // CH
NEG = -1.0e30
FF_UNITS, FFE_UNITS = D_FF // UNIT, D_FFE // UNIT
MOD_PARTS = 6 * D // UNIT
SG_CHUNK = 128

CHUNKS = [list(range(NCH)), [3, 2, 1, 0, 7, 6, 5, 4]]

P1 = {}
_at = 0
for _name, _n in [("norm1_g", 8), ("norm2_g", 8), ("mod_b", 48), ("mu_prev", 10), ("mu_next", 10),
                  ("w0", 4), ("a0", 4), ("k_k", 2), ("k_a", 2), ("r_k", 2), ("gn_g", 2), ("gn_b", 2),
                  ("cv_b", 2), ("cv_g", 2), ("cv_beta", 2), ("cv_w", 2 * CV_TAPS), ("final_g", 8)]:
    P1[_name] = (_at, _at + _n)
    _at += _n
P1_COLS = _at
P2 = {}
_at = 0
for _name, _n in [("norm1_g", 8), ("norm2_g", 8), ("q_g", 1), ("k_g", 1), ("sg_g", 2), ("conv_w", 6),
                  ("ffn_w", 3 * 44)]:
    P2[_name] = (_at, _at + _n)
    _at += _n
P2_COLS = _at

CON = {}
_at = 0
for _name, _n in [("mean_d", 128), ("head_sum", 128), ("ident", 128), ("eye64", 64), ("mask_zr", 512),
                  ("mask_d", 256), ("mask_l", 256), ("mask_dt", 256), ("not_first", 512), ("swap", 128),
                  ("cos", 256), ("sin", 256), ("win", 64), ("out_win", 64), ("sel", 1024),
                  ("eps", 8), ("iota", 8), ("mean_cv", 128)]:
    CON[_name] = (_at, _at + _n)
    _at += _n
CON_COLS = _at
EPS_RMS, EPS_LN, EPS_GN, EPS_KK = 0, 1, 2, 3


def constants():
    c = np.zeros((P, CON_COLS), np.float32)

    def put(name, a):
        lo, hi = CON[name]
        c[:a.shape[0], lo:hi] = a
    p = np.arange(P)
    put("mean_d", np.full((P, P), 1.0 / D))
    put("head_sum", (p[:, None] // DH == p[None, :] // DH) * 1.0)
    put("ident", np.eye(P))
    put("eye64", (p[:, None] % CH == np.arange(CH)[None, :]) * 1.0)
    row = (p % CH)[:, None]
    col = np.arange(CH)[None, :]
    fwd_st, bwd_st = (row < col) * 1.0, (row > col) * 1.0
    fwd_in, bwd_in = (row <= col) * 1.0, (row >= col) * 1.0
    same = (row // 16 == col // 16) * 1.0
    two = lambda f, b: [f, f, b, b]
    put("mask_zr", np.concatenate([np.concatenate(x, 1) for x in
                                   [(fwd_st, fwd_in)] * 2 + [(bwd_st, bwd_in)] * 2], 1))
    put("mask_dt", np.concatenate(two(fwd_st * same, bwd_st * same), 1))
    put("mask_d", np.concatenate(two(bwd_st * same, fwd_st * same), 1))
    put("mask_l", np.concatenate(two(bwd_st * (1 - same), fwd_st * (1 - same)), 1))
    put("not_first", np.tile((np.arange(T) % CH != 0) * 1.0, (P, 1)))
    f = p % DH
    axis, half, freq = f // 32, (f % 32) // 16, f % 16
    inv = (1.0 / (10000.0 ** (np.arange(16, dtype=np.float32) * np.float32(2.0) / np.float32(32)))).astype(np.float32)
    tok = np.arange(LAT)
    pos = np.where(axis[:, None] == 0, tok[None, :] // 64, tok[None, :] % 64).astype(np.float32)
    ang = pos * inv[freq][:, None]
    put("cos", np.cos(ang).astype(np.float32))
    put("sin", (np.sin(ang) * np.where(half == 0, -1.0, 1.0)[:, None]).astype(np.float32))
    partner = np.where(half == 0, p + 16, p - 16)
    put("swap", (p[:, None] == partner[None, :]) * 1.0)
    qc, kc = (p % 64)[:, None], np.arange(64)[None, :]
    ws = np.clip(qc - 8, 0, 48)
    inside = (kc >= ws) & (kc < ws + 16)
    put("win", inside * 1.0)
    put("out_win", np.where(inside, 0.0, NEG))
    put("sel", np.concatenate([(p[0:8, None] == e) * np.ones((1, P)) for e in range(8)], 1))
    lo, _ = CON["eps"]
    for at, v in ((EPS_RMS, 1e-6), (EPS_LN, 1e-5), (EPS_GN, 64e-5), (EPS_KK, 1e-12)):
        c[:, lo + at] = v
    put("mean_cv", np.full((P, P), 1.0 / 256))
    put("iota", np.tile(np.arange(8.0), (P, 1)))
    return c


class Steps:

    def __init__(self, signal, names):
        self.s, self.names, self.i = signal, names, 0

        self.h = signal.h

    def one(self, name):
        assert self.names[self.i] == name, (self.names[self.i], name)
        self.i += 1
        return self.s.one()

    def at(self, name):
        return self.s.at(self.names.index(name) + 1)


class Signal:

    def __init__(self, handle):
        self.h, self.n, self.m = handle, 0, 0

    def one(self, times=1):
        self.m += times
        return 1

    def at(self, k):
        return max(self.n + k, 0) if isinstance(k, int) else k + self.n


def build(nc, parts, xt_in, ct_in, con_in, par1_in, par2_in, lora_in, gate2_in, router_in, bias_in,
          sgw_in, sgb_in, out):
    ctx = ExitStack()
    sb = lambda name, cols: ctx.enter_context(nc.sbuf_tensor(name, [P, cols], F32))
    sems = {}

    def S(name):
        if name not in sems:
            sems[name] = Signal(ctx.enter_context(nc.semaphore(name)))
        return sems[name]

    x_buf = sb("x_buf", KT * T)
    h_buf = sb("h_buf", KT * T)
    mix_buf = sb("mix_buf", KT * T)
    ring = sb("ring", RING * PART)
    con = sb("constants", CON_COLS)
    par1 = [sb(f"par1_{l}", P1_COLS) for l in range(DEPTH)]
    par2 = [sb(f"par2_{l}", P2_COLS) for l in range(DEPTH)]
    modv = sb("modv", 48 * 2)
    scal = sb("scal", 64)
    ct = sb("condition_buf", KT * 2)
    arena = sb("arena", 22560)
    banks = ctx.enter_context(nc.psum_tensor("banks", [P, 8 * 512], F32))

    v3 = lambda a, n: a.rearrange("p (a b) -> p a b", a=n)
    xT, hT, mixT = (v3(b[:, :], KT) for b in (x_buf, h_buf, mix_buf))
    bank = lambda i: banks[:, i * 512:(i + 1) * 512]
    C = lambda name: con[:, CON[name][0]:CON[name][1]]
    Q1 = lambda l, name, i: par1[l][:, P1[name][0] + i:P1[name][0] + i + 1]
    Q2 = lambda l, name, i: par2[l][:, P2[name][0] + i:P2[name][0] + i + 1]
    eps = lambda i: con[:, CON["eps"][0] + i:CON["eps"][0] + i + 1]
    mod3 = v3(modv[:, :], 48)
    slots = v3(ring[:, :], RING)

    class Arena:

        def __init__(self, at=0, buf=None, size=22560):
            self.at, self.buf, self.size = at, buf or arena, size

        def take(self, cols, n=None):
            a = self.buf[:, self.at:self.at + cols]
            self.at += cols
            assert self.at <= self.size, self.at
            return v3(a, n) if n else a

    block = ctx.enter_context(nc.Block())
    loaded = [S(f"part_loaded_{i}") for i in range(RING)]
    used = S("parts_used")
    stream = {"put": 0, "got": 0, "skew": 0}

    phase = {"n": 0}

    def end_phase():
        phase["n"] += 1
        met = S("phase_met")
        goal = 4 * phase["n"]

        def meet(eng):
            eng.drain().then_inc(met.h, met.one())
            eng.wait_ge(met.h, goal)

        @block.tensor
        def _(pe):
            meet(pe)

        @block.scalar
        def _(act):
            meet(act)

        @block.vector
        def _(dve):
            meet(dve)

        @block.gpsimd
        def _(pool):
            meet(pool)
        for s in sems.values():
            if s not in loaded and s is not used:
                s.n = s.m

    def load_parts(sp, count):
        for _ in range(count):
            n = stream["put"]
            if n >= RING:
                sp.wait_ge(used.h, n - RING + 1)
            sp.dma_start(slots[:, n % RING, :], parts[n - stream["skew"], :, :]).then_inc(loaded[n % RING].h, 16)
            stream["put"] += 1

    def load_looped(sp, trips):
        n0 = stream["put"]
        with sp.Fori(0, trips) as i:
            for j in range(RING):
                n = n0 + j
                sp.wait_ge(used.h, i * RING + (n - RING + 1))
                sp.dma_start(slots[:, n % RING, :], parts[bass.ds(i * RING + (n - stream["skew"]), 1), :, :]
                             .rearrange("a p n -> p (a n)")).then_inc(loaded[n % RING].h, 16)
        stream["put"] += trips * RING

    def take_part(pe, n, i=None):
        goal = 16 * (n // RING + 1)
        pe.wait_ge(loaded[n % RING].h, goal if i is None else i * 16 + goal)
        return slots[:, n % RING, :]

    def norm(src, dst, cols, gain, shift, name):
        lo, hi = cols
        n = hi - lo
        streams = [s for s in range(2) if lo <= s * CTX < hi]
        a = Arena()
        sq, sd, rs = a.take(KT * n, KT), a.take(n), a.take(n)
        sq_done, ms_done, sd_done, rs_done, t_done, h_done = (
            S(f"norm_{x}") for x in ("squared", "mean", "root", "inverse", "scaled", "shifted"))

        @block.scalar
        def _(act):
            for k in range(KT):
                act.activation(sq[:, k, :], src[:, k, lo:hi], ACT.Square).then_inc(sq_done.h, sq_done.one())
            act.wait_ge(ms_done.h, ms_done.at(1))
            act.activation(sd, bank(0)[:, 0:n], ACT.Sqrt, bias=eps(EPS_RMS)).then_inc(sd_done.h, sd_done.one())
            if shift:
                for k in range(KT):
                    for j, s in enumerate(streams):
                        act.wait_ge(t_done.h, t_done.at(k * len(streams) + j + 1))
                        y = dst[:, k, s * CTX:(s + 1) * CTX]
                        act.activation(y, y, ACT.Identity, bias=shift(k, s)).then_inc(h_done.h, h_done.one())

        @block.tensor
        def _(pe):
            for k in range(KT):
                pe.wait_ge(sq_done.h, sq_done.at(k + 1))
                mm = pe.matmul(bank(0)[:, 0:n], C("mean_d"), sq[:, k, :], start=k == 0, stop=k == KT - 1)
            mm.then_inc(ms_done.h, ms_done.one())

        @block.vector
        def _(dve):
            dve.wait_ge(sd_done.h, sd_done.at(1))
            dve.reciprocal(rs, sd).then_inc(rs_done.h, rs_done.one())
            dve.wait_ge(rs_done.h, rs_done.at(1))
            for k in range(KT):
                for s in streams:
                    c = slice(s * CTX, (s + 1) * CTX)
                    r = slice(s * CTX - lo, (s + 1) * CTX - lo)
                    dve.scalar_tensor_tensor(dst[:, k, c], src[:, k, c], gain(k, s), rs[:, r],
                                                        ALU.mult, ALU.mult).then_inc(t_done.h, t_done.one())
        end_phase()

    def modulation(l):
        b_done, g_done = S("mod_biased"), S("mod_gains")
        acc = v3(bank(0)[:, 0:96], 48)

        @block.sync
        def _(sp):
            load_parts(sp, MOD_PARTS)

        @block.tensor
        def _(pe):
            for m in range(MOD_PARTS):
                w = v3(take_part(pe, stream["got"]), KT)
                for j in range(2):
                    for k in range(KT):
                        mm = pe.matmul(acc[:, 2 * m + j, :], w[:, k, j * P:(j + 1) * P], v3(ct[:, :], KT)[:, k, :],
                                       start=k == 0, stop=k == KT - 1)
                mm.then_inc(used.h, used.one())
                stream["got"] += 1

        @block.vector
        def _(dve):
            dve.wait_ge(used.h, stream["got"])
            b = par1[l][:, P1["mod_b"][0]:P1["mod_b"][1]]
            for s in range(2):
                dve.tensor_tensor(mod3[:, :, s], acc[:, :, s], b, ALU.add).then_inc(b_done.h, b_done.one())
            dve.wait_ge(b_done.h, b_done.at(2))
            for i, name in enumerate(("norm1_g", "norm2_g")):
                g = par1[l][:, P1[name][0]:P1[name][1]]
                for s in range(2):
                    o = v3(scal[:, i * 16:(i + 1) * 16], 8)[:, :, s]
                    dve.scalar_tensor_tensor(o, mod3[:, 24 * i + 8:24 * i + 16, s], 1.0, g,
                                                        ALU.add, ALU.mult).then_inc(g_done.h, g_done.one())
            c0 = scal[:, 32:42]
            mp = par1[l][:, P1["mu_prev"][0]:P1["mu_prev"][1]]
            mn = par1[l][:, P1["mu_next"][0]:P1["mu_next"][1]]
            dve.tensor_tensor(c0, mp, mn, ALU.add).then_inc(b_done.h, b_done.one())
            dve.wait_ge(b_done.h, b_done.at(3))
            dve.tensor_scalar(c0, c0, -1.0, 1.0, ALU.mult, ALU.add).then_inc(g_done.h, g_done.one())
            ka = par1[l][:, P1["k_a"][0]:P1["k_a"][1]]
            dve.tensor_scalar(scal[:, 42:44], ka, -1.0, 1.0, ALU.mult, ALU.add).then_inc(g_done.h, g_done.one())
        end_phase()

    gain1 = lambda k, s: scal[:, 2 * k + s:2 * k + s + 1]
    gain2 = lambda k, s: scal[:, 16 + 2 * k + s:16 + 2 * k + s + 1]
    modc = lambda t, s: mod3[:, t, s:s + 1]

    def project(tiles):
        ready, free = S("tile_ready"), {"act": S("tile_free_act"), "dve": S("tile_free_dve")}
        first = stream["got"]
        n_parts = tiles[-1]["part"] + 1
        closes = [t + 1 == len(tiles) or tiles[t + 1]["part"] != tiles[t]["part"] for t in range(len(tiles))]

        @block.sync
        def _(sp):
            load_parts(sp, n_parts)

        @block.tensor
        def _(pe):
            freed = {"act": 0, "dve": 0}
            part = -1
            for t, tile in enumerate(tiles):
                if tile["part"] != part:
                    part = tile["part"]
                    w = v3(take_part(pe, first + part), KT)
                if t >= 8:
                    o = tiles[t - 8]["owner"]
                    freed[o] += 1
                    pe.wait_ge(free[o].h, free[o].at(freed[o]))
                for k in range(KT):
                    if "tok" in tile:
                        tk, wd = tile["tok"], tile.get("wide", UNIT)
                        mm = pe.matmul(bank(t % 8)[:, 0:wd], tile["src"][:, k, tk * P:(tk + 1) * P],
                                       w[:, k, UNIT - wd:UNIT], start=k == 0, stop=k == KT - 1)
                    else:
                        lo, hi = tile["cols"]
                        mm = pe.matmul(bank(t % 8)[:, 0:hi - lo], w[:, k, tile["j"] * P:(tile["j"] + 1) * P],
                                       tile["src"][:, k, lo:hi], start=k == 0, stop=k == KT - 1)
                mm.then_inc((used if closes[t] else ready).h, (used if closes[t] else ready).one())
        stream["got"] += n_parts

        def tile_done(t):
            if closes[t]:
                return used.h, first + tiles[t]["part"] + 1
            return ready.h, ready.at(sum(not c for c in closes[:t + 1]))
        return tile_done, free

    def attention(units, q, k, v, scale, qwide, k_tile, v_col, at):
        per = qwide // P
        a = Arena(at)
        nk_max = max(len(u[4]) for u in units) * P
        pr = a.take(2 * nk_max, 2)
        ptr = [v3(x, nk_max // P) for x in (a.take(nk_max // P * qwide), a.take(nk_max // P * qwide))]
        st = a.take(2 * 4, 2)
        s_ok, m_ok, e_ok, n_ok, t_ok, c_ok, o_ok, w_ok, mm_ok, ri_ok = (S(f"attn_{x}") for x in (
            "scores", "max", "exp", "probs", "probs_turned", "turned_copied", "out", "out_copied",
            "rowmax", "inverse"))
        N = len(units)

        @block.tensor
        def _(pe):
            def scores(i):
                tile, half, qc, kcols, vt, bias, _ = units[i]
                hs = slice(half * DH, half * DH + DH)
                if i >= 2:
                    pe.wait_ge(e_ok.h, e_ok.at(i - 1))
                at = 0
                for lo, hi in kcols:
                    b = bias if at == 0 else None
                    mm = pe.matmul(bank(i % 2)[:, at:at + hi - lo], q[hs, tile, qc:qc + P], k[hs, k_tile(tile), lo:hi],
                                   start=True, stop=b is None)
                    if b is not None:
                        mm = pe.matmul(bank(i % 2)[:, at:at + hi - lo], C("ident"), b, start=False, stop=True)
                    at += hi - lo
                mm.then_inc(s_ok.h, s_ok.one())

            def turn(i):
                pe.wait_ge(n_ok.h, n_ok.at(i + 1))
                if i >= 2:
                    pe.wait_ge(c_ok.h, c_ok.at(i - 1))
                for t in range(len(units[i][4])):
                    mm = pe.transpose(bank(2 + i % 2)[:, t * P:(t + 1) * P], pr[:, i % 2, t * P:(t + 1) * P], C("ident"))
                mm.then_inc(t_ok.h, t_ok.one())

            def values(g):
                tile, half, _, _, vt, _, _ = units[g * per]
                hs = slice(half * DH, half * DH + DH)
                pe.wait_ge(c_ok.h, c_ok.at((g + 1) * per))
                if g >= 2:
                    pe.wait_ge(w_ok.h, w_ok.at(g - 1))
                for t, tv in enumerate(vt):
                    vc = v_col(tile, half)
                    mm = pe.matmul(bank(4 + g % 2)[hs, 0:qwide], v[:, tv, vc:vc + DH], ptr[g % 2][:, t, :],
                                   start=t == 0, stop=t == len(vt) - 1)
                mm.then_inc(o_ok.h, o_ok.one())

            for i in range(N + 2):
                if i < N:
                    scores(i)
                if 1 <= i <= N:
                    turn(i - 1)
                if i >= 2 and (i - 2) % per == per - 1:
                    values((i - 2) // per)

        @block.vector
        def _(dve):
            def top(i):
                nk = len(units[i][4]) * P
                dve.wait_ge(s_ok.h, s_ok.at(i + 1))
                if i >= 2:
                    dve.wait_ge(e_ok.h, e_ok.at(i - 1))
                dve.tensor_reduce(st[:, i % 2, 0:1], bank(i % 2)[:, 0:nk], AX.X, ALU.max).then_inc(mm_ok.h, mm_ok.one())
                dve.wait_ge(mm_ok.h, mm_ok.at(i + 1))
                dve.tensor_scalar(st[:, i % 2, 1:2], st[:, i % 2, 0:1], -scale, None, ALU.mult).then_inc(m_ok.h, m_ok.one())

            def normalise(i):
                nk = len(units[i][4]) * P
                dve.wait_ge(e_ok.h, e_ok.at(i + 1))
                dve.reciprocal(st[:, i % 2, 3:4], st[:, i % 2, 2:3]).then_inc(ri_ok.h, ri_ok.one())
                dve.wait_ge(ri_ok.h, ri_ok.at(i + 1))
                dve.tensor_scalar(pr[:, i % 2, 0:nk], pr[:, i % 2, 0:nk], st[:, i % 2, 3:4], None, ALU.mult).then_inc(n_ok.h, n_ok.one())

            def copy_out(g):
                tile, half, _, _, _, _, oc = units[g * per]
                hs = slice(half * DH, half * DH + DH)
                dve.wait_ge(o_ok.h, o_ok.at(g + 1))
                dve.tensor_copy(mixT[hs, tile, oc:oc + qwide], bank(4 + g % 2)[hs, 0:qwide]).then_inc(w_ok.h, w_ok.one())

            for i in range(N + 4):
                if i < N:
                    top(i)
                if 1 <= i <= N:
                    normalise(i - 1)
                if i >= 3 and (i - 3) % per == per - 1 and (i - 3) // per < N // per:
                    copy_out((i - 3) // per)

        @block.scalar
        def _(act):
            def exp(i):
                nk = len(units[i][4]) * P
                act.wait_ge(m_ok.h, m_ok.at(i + 1))
                if i >= 2:
                    act.wait_ge(t_ok.h, t_ok.at(i - 1))
                    act.wait_ge(ri_ok.h, ri_ok.at(i - 1))
                act.activation(pr[:, i % 2, 0:nk], bank(i % 2)[:, 0:nk], ACT.Exp, bias=st[:, i % 2, 1:2],
                                        scale=scale, accum_out=st[:, i % 2, 2:3]).then_inc(e_ok.h, e_ok.one())

            def copy_turned(i):
                nt = len(units[i][4])
                g, j = i // per, i % per
                act.wait_ge(t_ok.h, t_ok.at(i + 1))
                if g >= 2:
                    act.wait_ge(o_ok.h, o_ok.at(g - 1))
                act.activation(ptr[g % 2][:, 0:nt, j * P:(j + 1) * P], v3(bank(2 + i % 2)[:, 0:nt * P], nt),
                                        ACT.Copy).then_inc(c_ok.h, c_ok.one())

            for i in range(N + 1):
                if i < N:
                    exp(i)
                if i >= 1:
                    copy_turned(i - 1)
        end_phase()

    def out_project(src, cols, gate, n_parts=4):
        tiles = [dict(part=p, j=j, cols=cols, src=src, owner="dve") for p in range(n_parts) for j in range(2)]
        tile_done, free = project(tiles)
        lo, hi = cols

        @block.vector
        def _(dve):
            for t in range(len(tiles)):
                dve.wait_ge(*tile_done(t))
                for s in range(2):
                    a, b = s * CTX, (s + 1) * CTX
                    if not lo <= a < hi:
                        continue
                    ps = bank(t % 8)[:, a - lo:b - lo]
                    if gate:
                        ins = dve.scalar_tensor_tensor(xT[:, t, a:b], ps, gate(t, s), xT[:, t, a:b], ALU.mult, ALU.add)
                    else:
                        ins = dve.tensor_tensor(xT[:, t, a:b], ps, xT[:, t, a:b], ALU.add)
                ins.then_inc(free["dve"].h, free["dve"].one())
        end_phase()

    def feed_forward(kind, groups, n_units, src, c0, residual, gates=None, taps=None, at=0):
        a = Arena(at)
        sg, hid = a.take(2 * 512, 2), a.take(2 * 512, 2)
        cen = a.take(2 * 1024, 2) if kind == "conv" else None
        si, ac, tp, ce, tq = (S(f"ff_{x}") for x in ("silu", "hidden", "product", "centre_tap", "side_taps"))
        N = groups * n_units
        B = stream["got"]
        y = lambda m: bank(4 + m // 2)[:, (m % 2) * 256:(m % 2 + 1) * 256]
        gate_bank, up_bank = (lambda u: bank(u % 2)), (lambda u: bank(2 + u % 2))
        looped = kind != "conv"

        gate_of = lambda U: B + 3 * U if U else B + 1
        up_of = lambda U: B + 3 * U + 1 if U else B + 2

        def over_units(eng, body, lead):
            for g in range(groups):
                if not looped:
                    for u in range(n_units):
                        body(g * n_units + u, 0, 1)
                    continue
                start = 0 if lead else 1
                if not lead:
                    body(g * n_units, 0, 1)
                trips = (n_units - 1) // 2
                with eng.Fori(0, trips) as i:
                    for j in range(2):
                        body(g * n_units + start + j, i, trips)
                for u in range(start + 2 * trips, n_units):
                    body(g * n_units + u, 0, 1)

        @block.sync
        def _(sp):
            load_parts(sp, 2)
            for g in range(groups):
                if looped:
                    trips = (n_units - 1) // 2
                    load_looped(sp, trips)
                    load_parts(sp, 3 * (n_units - 2 * trips) - (2 if g == groups - 1 else 0))
                else:
                    load_parts(sp, 3 * n_units - 2)

        @block.tensor
        def _(pe):
            def products(U, n, i, times):
                for which, bk in enumerate((gate_bank(U), up_bank(U))):
                    w = v3(take_part(pe, n + which, i), KT)
                    if which == 0:
                        pe.wait_ge(ac.h, ac.at(i * 2 + (U + 1)))
                    for j in range(2):
                        for k in range(KT):
                            mm = pe.matmul(bk[:, j * 256:(j + 1) * 256], w[:, k, j * P:(j + 1) * P],
                                           src[:, k, c0:c0 + 256], start=k == 0, stop=k == KT - 1)
                    mm.then_inc(used.h, used.one(times))

            def down(U, n, i, times):
                w = v3(take_part(pe, n, i), 2)
                pe.wait_ge(ac.h, ac.at(i * 2 + (U + 3)))
                for j in range(2):
                    for m in range(KT):
                        mm = pe.matmul(y(m), w[:, j, m * P:(m + 1) * P], hid[:, U % 2, j * 256:(j + 1) * 256],
                                       start=False, stop=False, skip_group_check=True)
                mm.then_inc(used.h, used.one(times))

            pe.wait_ge(ac.h, ac.at(1))
            for b in range(4):
                pe.matmul(bank(4 + b), C("ident"), hid[:, 0, :], start=True, stop=False, skip_group_check=True)
            products(0, B, 0, 1)

            def body(U, i, times):
                n = B + 2 + 3 * U
                if U < N - 1:
                    products(U + 1, n, i, times)
                    down(U, n + 2, i, times)
                else:
                    down(U, n, i, times)
            over_units(pe, body, 1)

        @block.scalar
        def _(act):
            def body(U, i, times):
                since = lambda v: i * 6 + v if times > 1 else v
                if kind == "conv":
                    act.wait_ge(used.h, since(gate_of(U)))
                    act.wait_ge(ac.h, ac.at(U + 1))
                    for h in range(2):
                        if h:
                            act.wait_ge(used.h, since(up_of(U)))
                        for j in range(2):
                            bk = (gate_bank(U), up_bank(U))[h]
                            act.activation(cen[:, U % 2, (2 * h + j) * 256:(2 * h + j + 1) * 256],
                                                  bk[:, j * 256:(j + 1) * 256], ACT.Copy,
                                                  scale=taps(1, 22 * h + 2 * U + j)).then_inc(ce.h, ce.one())
                    act.wait_ge(tq.h, tq.at(8 * U + 4))
                    act.activation(sg[:, U % 2, :], cen[:, U % 2, 0:512], ACT.Silu).then_inc(si.h, si.one())
                    return
                act.wait_ge(used.h, since(gate_of(U)))
                act.wait_ge(ac.h, ac.at(i * 2 + (U + 1)))
                act.activation(sg[:, U % 2, :], gate_bank(U), ACT.Silu).then_inc(si.h, si.one(times))
            over_units(act, body, 0)

        @block.vector
        def _(dve):
            for j in range(2):
                dve.memset(hid[:, j, :], 0.0).then_inc(ac.h, ac.one())

            def body(U, i, times):
                since = lambda v: i * 6 + v if times > 1 else v
                if kind == "conv":
                    dve.wait_ge(used.h, since(up_of(U)))
                    for h in range(2):
                        dve.wait_ge(ce.h, ce.at(4 * U + 2 * h + 2))
                        bk = (gate_bank(U), up_bank(U))[h]
                        for side in range(2):
                            if side:
                                dve.wait_ge(tq.h, tq.at(8 * U + 4 * h + 2))
                            for j in range(2):
                                c = cen[:, U % 2, (2 * h + j) * 256:(2 * h + j + 1) * 256]
                                p = bk[:, j * 256:(j + 1) * 256]
                                o, q = (c[:, 1:256], p[:, 0:255]) if side == 0 else (c[:, 0:255], p[:, 1:256])
                                dve.scalar_tensor_tensor(o, q, taps(2 * side, 22 * h + 2 * U + j), o,
                                                                ALU.mult, ALU.add).then_inc(tq.h, tq.one())
                    dve.wait_ge(si.h, si.at(U + 1))
                    dve.wait_ge(tq.h, tq.at(8 * U + 8))
                    dve.tensor_tensor(hid[:, U % 2, :], cen[:, U % 2, 512:1024], sg[:, U % 2, :], ALU.mult).then_inc(ac.h, ac.one())
                    return
                dve.wait_ge(used.h, since(up_of(U)))
                dve.wait_ge(si.h, si.at(i * 2 + (U + 1)))
                if kind == "silu":
                    dve.tensor_tensor(hid[:, U % 2, :], up_bank(U), sg[:, U % 2, :], ALU.mult).then_inc(ac.h, ac.one(times))
                    return
                e = U // n_units
                dve.tensor_tensor(hid[:, U % 2, :], up_bank(U), sg[:, U % 2, :], ALU.mult).then_inc(tp.h, tp.one(times))
                dve.wait_ge(tp.h, tp.at(i * 2 + (U + 1)))
                h = v3(hid[:, U % 2, :], 2)
                dve.tensor_tensor(h, h, gates[:, e:e + 1, :].broadcast_to((P, 2, 256)), ALU.mult).then_inc(ac.h, ac.one(times))
            over_units(dve, body, 0)
            dve.wait_ge(used.h, B + 3 * N)
            for m in range(KT):
                residual(dve, m, y(m))
        stream["got"] += 3 * N
        end_phase()

    def recurrence(l, us, at):
        big, hb = Arena(at), Arena(0, h_buf, KT * T)
        zr = big.take(4 * T * 2).rearrange("p (q c w t) -> p q c w t", q=4, c=NCH, w=2)
        bt, kt = hb.take(4 * T, 4), hb.take(4 * T, 4)
        gg, bon, pc = big.take(4 * T, 4), big.take(2 * T, 2), big.take(4 * NCH, 4)
        tmp_at = big.at
        lora, g2w, tw, sgd = big.take(512, 2), big.take(512, 2), big.take(T), big.take(T)
        lw, av, kk, ci, ce, ex, kd = (big.take(2 * T, 2) for _ in range(7))
        r, k, v = us[:, 0:2, :], us[:, 2:4, :], us[:, 4:6, :]
        by_chunk = lambda a: a.rearrange("p (c t) -> p c t", t=CH)
        chunks_of = lambda a: a.rearrange("p h (c t) -> p (h c) t", t=CH)
        lo_in = S("lora_loaded")

        @block.scalar
        def _(sp):
            sp.dma_start(lora, lora_in[l, :, :].rearrange("p (d n) -> p d n", d=2)).then_inc(lo_in.h, 16)
            sp.dma_start(g2w, gate2_in[l, :, :].rearrange("p (d n) -> p d n", d=2)).then_inc(lo_in.h, 16)

        an = ["sq0", "sq1", "root0", "root1"]
        vn = ["kk0", "kk1", "inv0", "inv1", "kkn0", "kkn1"]
        pn = ["kksum"]
        for d in range(2):
            an += [f"{x}{d}" for x in ("tanh", "sgd", "sw0", "sw1", "a0", "a1", "g", "ex", "ep", "en", "pc")]
            pn += [f"{x}{d}" for x in ("w", "g", "bonus")]
            vn += [f"{x}{d}" for x in ("lw", "scan0", "scan1", "excl", "incl", "z0", "z1", "r0", "r1", "b1", "b",
                                       "ka0", "ka1", "kd", "k", "rk0", "rk1", "bv", "bg")]
            vn += ["badd1"] * d
        A_, V_, P_ = Steps(S("rw_act"), an), Steps(S("rw_dve"), vn), Steps(S("rw_pe"), pn)

        @block.tensor
        def _(pe):
            pe.wait_ge(A_.h, A_.at("sq1"))
            for hp in range(2):
                mm = pe.matmul(bank(hp), C("head_sum"), ex[:, hp, :], start=True, stop=True)
            mm.then_inc(P_.h, P_.one("kksum"))
            pe.wait_ge(lo_in.h, 32 * (l + 1))
            for d in range(2):
                pe.wait_ge(A_.h, A_.at(f"tanh{d}"))
                for hp in range(2):
                    c = slice(hp * P, (hp + 1) * P)
                    pe.matmul(bank(2 + hp), lora[0:64, d, c], tw[0:64, :], start=True, stop=True)
                    mm = pe.matmul(bank(4 + hp), lora[64:128, d, c], us[64:128, 6 + 2 * d, :], start=True, stop=True)
                mm.then_inc(P_.h, P_.one(f"w{d}"))
                pe.wait_ge(A_.h, A_.at(f"sgd{d}"))
                for hp in range(2):
                    mm = pe.matmul(bank(6 + hp), g2w[:, d, hp * P:(hp + 1) * P], sgd, start=True, stop=True)
                mm.then_inc(P_.h, P_.one(f"g{d}"))
                pe.wait_ge(V_.h, V_.at(f"rk1{d}"))
                for hp in range(2):
                    mm = pe.matmul(bank(hp), C("head_sum"), av[:, hp, :], start=True, stop=True)
                mm.then_inc(P_.h, P_.one(f"bonus{d}"))

        @block.scalar
        def _(act):
            for hp in range(2):
                act.wait_ge(V_.h, V_.at(f"kk{hp}"))
                act.activation(ex[:, hp, :], kk[:, hp, :], ACT.Square).then_inc(A_.h, A_.one(f"sq{hp}"))
            act.wait_ge(P_.h, P_.at("kksum"))
            for hp in range(2):
                act.activation(ce[:, hp, :], bank(hp), ACT.Sqrt, bias=eps(EPS_KK)).then_inc(A_.h, A_.one(f"root{hp}"))
            for d in range(2):
                if d:
                    act.wait_ge(P_.h, P_.at("g0"))
                    act.wait_ge(V_.h, V_.at("bg0"))
                act.activation(tw[0:64, :], us[0:64, 6 + 2 * d, :], ACT.Tanh).then_inc(A_.h, A_.one(f"tanh{d}"))
                act.activation(sgd, us[:, 7 + 2 * d, :], ACT.Sigmoid).then_inc(A_.h, A_.one(f"sgd{d}"))
                act.wait_ge(P_.h, P_.at(f"w{d}"))
                for hp in range(2):
                    act.activation(lw[:, hp, :], bank(2 + hp), ACT.Sigmoid,
                                                         bias=Q1(l, "w0", 2 * d + hp)).then_inc(A_.h, A_.one(f"sw{hp}{d}"))
                for hp in range(2):
                    act.activation(av[:, hp, :], bank(4 + hp), ACT.Sigmoid,
                                                        bias=Q1(l, "a0", 2 * d + hp)).then_inc(A_.h, A_.one(f"a{hp}{d}"))
                act.wait_ge(P_.h, P_.at(f"g{d}"))
                act.activation(gg[:, 2 * d:2 * d + 2, :], v3(banks[:, 6 * 512:8 * 512], 2), ACT.Copy).then_inc(A_.h, A_.one(f"g{d}"))
                act.wait_ge(V_.h, V_.at(f"incl{d}"))
                act.activation(ex, ce, ACT.Exp).then_inc(A_.h, A_.one(f"ex{d}"))
                act.wait_ge(A_.h, A_.at(f"ex{d}"))
                act.activation(ce, ci, ACT.Exp).then_inc(A_.h, A_.one(f"ep{d}"))
                act.wait_ge(V_.h, V_.at(f"z1{d}"))
                act.activation(ex, ci, ACT.Exp, scale=-1.0).then_inc(A_.h, A_.one(f"en{d}"))
                edge = CH - 1 if d == 0 else 0
                act.activation(pc[:, 2 * d:2 * d + 2, :],
                                                 ci.rearrange("p h (c t) -> p h c t", t=CH)[:, :, :, edge], ACT.Exp).then_inc(A_.h, A_.one(f"pc{d}"))

        @block.vector
        def _(dve):
            me = V_.s
            for hp in range(2):
                dve.tensor_scalar(kk[:, hp, :], k[:, hp, :], Q1(l, "k_k", hp), None, ALU.mult).then_inc(V_.h, V_.one(f"kk{hp}"))
            for hp in range(2):
                dve.wait_ge(A_.h, A_.at(f"root{hp}"))
                dve.reciprocal(ce[:, hp, :], ce[:, hp, :]).then_inc(V_.h, V_.one(f"inv{hp}"))
            dve.wait_ge(me.h, me.m)
            for hp in range(2):
                dve.tensor_tensor(kk[:, hp, :], kk[:, hp, :], ce[:, hp, :], ALU.mult).then_inc(V_.h, V_.one(f"kkn{hp}"))
            for d in range(2):
                dve.wait_ge(A_.h, A_.at(f"sw1{d}"))
                dve.tensor_scalar(lw, lw, -float(np.exp(-0.5)), None, ALU.mult).then_inc(V_.h, V_.one(f"lw{d}"))
                dve.wait_ge(me.h, me.m)
                for hp in range(2):
                    dve.tensor_tensor_scan(ci[:, hp, :], C("not_first"), lw[:, hp, :], 0.0,
                                                                   ALU.mult, ALU.add).then_inc(V_.h, V_.one(f"scan{hp}{d}"))
                dve.wait_ge(me.h, me.m)
                if d == 0:
                    dve.tensor_tensor(ce, ci, lw, ALU.subtract).then_inc(V_.h, V_.one("excl0"))
                    dve.tensor_copy(kd[:, 0, 0:1], ci[:, 0, 0:1]).then_inc(V_.h, V_.one("incl0"))
                else:
                    tot = chunks_of(ci)[:, :, CH - 1:CH].broadcast_to((P, 2 * NCH, CH))
                    dve.tensor_tensor(chunks_of(ce), tot, chunks_of(ci), ALU.subtract).then_inc(V_.h, V_.one("excl1"))
                    dve.wait_ge(me.h, me.m)
                    dve.tensor_tensor(ci, ce, lw, ALU.add).then_inc(V_.h, V_.one("incl1"))
                dve.wait_ge(A_.h, A_.at(f"ex{d}"))
                dve.wait_ge(me.h, me.m)
                for hp in range(2):
                    dve.scalar_tensor_tensor(zr[:, 2 * d + hp, :, 0, :], by_chunk(ex[:, hp, :]), -1.0,
                                                                  by_chunk(kk[:, hp, :]), ALU.mult, ALU.mult).then_inc(V_.h, V_.one(f"z{hp}{d}"))
                dve.wait_ge(A_.h, A_.at(f"ep{d}"))
                for hp in range(2):
                    dve.tensor_tensor(zr[:, 2 * d + hp, :, 1, :], by_chunk(ce[:, hp, :]),
                                                           by_chunk(r[:, hp, :]), ALU.mult).then_inc(V_.h, V_.one(f"r{hp}{d}"))
                dve.wait_ge(A_.h, A_.at(f"a1{d}"))
                dve.tensor_tensor(lw, kk, av, ALU.mult).then_inc(V_.h, V_.one(f"b1{d}"))
                dve.wait_ge(me.h, me.m)
                dve.wait_ge(A_.h, A_.at(f"en{d}"))
                dve.tensor_tensor(bt[:, 2 * d:2 * d + 2, :], lw, ex, ALU.mult).then_inc(V_.h, V_.one(f"b{d}"))
                for hp in range(2):
                    dve.tensor_scalar(kd[:, hp, :], av[:, hp, :], Q1(l, "k_a", hp),
                                                            scal[:, 42 + hp:43 + hp], ALU.mult, ALU.add).then_inc(V_.h, V_.one(f"ka{hp}{d}"))
                dve.wait_ge(me.h, me.m)
                dve.tensor_tensor(kd, kd, k, ALU.mult).then_inc(V_.h, V_.one(f"kd{d}"))
                dve.wait_ge(me.h, me.m)
                dve.tensor_tensor(kt[:, 2 * d:2 * d + 2, :], kd, ex, ALU.mult).then_inc(V_.h, V_.one(f"k{d}"))
                for hp in range(2):
                    dve.scalar_tensor_tensor(av[:, hp, :], r[:, hp, :], Q1(l, "r_k", hp),
                                                                   kd[:, hp, :], ALU.mult, ALU.mult).then_inc(V_.h, V_.one(f"rk{hp}{d}"))
                dve.wait_ge(P_.h, P_.at(f"bonus{d}"))
                dve.tensor_tensor(av, v3(banks[:, 0:1024], 2), v, ALU.mult).then_inc(V_.h, V_.one(f"bv{d}"))
                dve.wait_ge(me.h, me.m)
                dve.wait_ge(A_.h, A_.at(f"pc{d}"))
                if d == 0:
                    dve.tensor_tensor(bon, av, gg[:, 0:2, :], ALU.mult).then_inc(V_.h, V_.one("bg0"))
                else:
                    dve.tensor_tensor(av, av, gg[:, 2:4, :], ALU.mult).then_inc(V_.h, V_.one("bg1"))
                    dve.wait_ge(me.h, me.m)
                    dve.tensor_tensor(bon, bon, av, ALU.add).then_inc(V_.h, V_.one("badd1"))
        end_phase()

        gb = Arena(tmp_at)
        lo = v3(us[:, 6:10, :].rearrange("p a b -> p (a b)"), 4)
        take = lambda: gb.take(512, 8)
        DT, DD, LL, MB, AK, MK, BS, KS, VS, D2, D2T, D4, D4T, E1, E2, DI, N1, GG_, TI = (take() for _ in range(19))
        X = gb.take(512, 2)
        lo8 = [v3(lo[:, i, :], 8) for i in range(4)]
        NTb, N2, INT_ = lo8[0], lo8[1], lo8[2]
        RH, UU = v3(lo[:, 3, 0:256], 4), v3(lo[:, 3, 256:512], 4)
        D8, E3, E4 = D2T, E1, E2
        b8 = lambda i: v3(bank(i), 8)
        b4 = lambda i: v3(bank(i)[:, 0:256], 4)
        eye = C("eye64").rearrange("p (o t) -> p o t", o=1).broadcast_to((P, 8, CH))
        Y = us
        pn, vn, an = [], ["x0"], []
        for g in range(NCH // 2):
            pn += [f"{x}_{g}" for x in ("gram", "p1", "p2", "p3", "p4", "p5", "p6", "p7", "p8")]
            vn += [f"{x}_{g}" for x in ("dt0", "mb0", "dt1", "mb1", "ak0", "mk0", "ak1", "mk1", "d", "l", "e1", "d2", "d4", "e2",
                                        "e3", "e4", "nt", "int", "n2", "g")]
            an += [f"{x}_{g}" for x in ("bs", "ks", "vs", "d2t", "d4t", "d8", "di", "n", "ti")]
            for j in range(2):
                pn += [f"{x}_{g}{j}" for x in ("rhs", "u", "dx", "y")]
                vn += [f"{x}_{g}{j}" for x in ("u", "xa", "xb")]
                an += [f"{x}_{g}{j}" for x in ("rhs", "y0", "y1")]
        P_, V_, A_ = Steps(S("rc_pe"), pn), Steps(S("rc_dve"), vn), Steps(S("rc_act"), an)
        hs = [slice(0, 64), slice(64, 128)]

        @block.tensor
        def _(pe):
            def products(out, left, right):
                for i in range(8):
                    for h in hs:
                        mm = pe.matmul(out[h, i, :], left[h, i, :], right[h, i, :], start=True, stop=True)
                return mm

            for g in range(NCH // 2):
                if g:
                    pe.wait_ge(A_.h, A_.at(f"y1_{g - 1}1"))
                    pe.wait_ge(V_.h, V_.at(f"xb_{g - 1}1"))
                for j in range(2):
                    for q in range(4):
                        c = CHUNKS[q // 2][2 * g + j]
                        cs = slice(c * CH, (c + 1) * CH)
                        i = 4 * j + q
                        for h in hs:
                            z_r = zr[h, q, c, :, :].rearrange("p w t -> p (w t)")
                            pe.matmul(bank(j)[h, q * 128:(q + 1) * 128], bt[h, q, cs], z_r, start=True, stop=True)
                            pe.matmul(bank(2 + j)[h, q * 128:(q + 1) * 128], kt[h, q, cs], z_r, start=True, stop=True)
                            pe.matmul(b8(4)[h, i, :], zr[h, q, c, 0, :], bt[h, q, cs], start=True, stop=True)
                            pe.matmul(b8(5)[h, i, :], bt[h, q, cs], eye[h, 0, :], start=True, stop=True)
                            pe.matmul(b8(6)[h, i, :], kt[h, q, cs], eye[h, 0, :], start=True, stop=True)
                            mm = pe.matmul(b8(7)[h, i, :], us[h, 4 + q % 2, cs], eye[h, 0, :], start=True, stop=True)
                mm.then_inc(P_.h, P_.one(f"gram_{g}"))
                pe.wait_ge(V_.h, V_.at(f"e1_{g}"))
                products(b8(0), DT, DD)
                products(b8(1), DD, DT).then_inc(P_.h, P_.one(f"p1_{g}"))
                pe.wait_ge(V_.h, V_.at(f"d2_{g}"))
                pe.wait_ge(A_.h, A_.at(f"d2t_{g}"))
                products(b8(2), D2T, D2)
                products(b8(3), D2, D2T)
                products(b8(4), D2, E1).then_inc(P_.h, P_.one(f"p2_{g}"))
                pe.wait_ge(V_.h, V_.at(f"e2_{g}"))
                pe.wait_ge(A_.h, A_.at(f"d4t_{g}"))
                products(b8(0), D4T, D4)
                products(b8(1), D4, E2).then_inc(P_.h, P_.one(f"p3_{g}"))
                pe.wait_ge(V_.h, V_.at(f"e3_{g}"))
                pe.wait_ge(A_.h, A_.at(f"d8_{g}"))
                products(b8(2), D8, E3).then_inc(P_.h, P_.one(f"p4_{g}"))
                pe.wait_ge(V_.h, V_.at(f"e4_{g}"))
                products(b8(3), E4, eye)
                products(b8(0), LL, E4)
                products(b8(1), E4, LL).then_inc(P_.h, P_.one(f"p5_{g}"))
                pe.wait_ge(V_.h, V_.at(f"int_{g}"))
                pe.wait_ge(A_.h, A_.at(f"n_{g}"))
                products(b8(2), NTb, N1).then_inc(P_.h, P_.one(f"p6_{g}"))
                pe.wait_ge(V_.h, V_.at(f"n2_{g}"))
                products(b8(3), N2, INT_).then_inc(P_.h, P_.one(f"p7_{g}"))
                pe.wait_ge(V_.h, V_.at(f"g_{g}"))
                products(b8(4), DI, GG_).then_inc(P_.h, P_.one(f"p8_{g}"))
                for j in range(2):
                    old = v3(X[:, j, :], 4)
                    if j or g:
                        pe.wait_ge(V_.h, V_.at(f"xb_{g if j else g - 1}{1 - j}"))
                    else:
                        pe.wait_ge(V_.h, V_.at("x0"))
                    at_c = [CHUNKS[q // 2][2 * g + j] for q in range(4)]
                    for q in range(4):
                        i = 4 * j + q
                        for h in hs:
                            pe.matmul(b4(5)[h, q, :], zr[h, q, at_c[q], 0, :], old[h, q, :], start=True, stop=False)
                            mm = pe.matmul(b4(5)[h, q, :], AK[h, i, :], VS[h, i, :], start=False, stop=True)
                    mm.then_inc(P_.h, P_.one(f"rhs_{g}{j}"))
                    pe.wait_ge(A_.h, A_.at(f"ti_{g}"))
                    pe.wait_ge(A_.h, A_.at(f"rhs_{g}{j}"))
                    for q in range(4):
                        for h in hs:
                            mm = pe.matmul(b4(6)[h, q, :], TI[h, 4 * j + q, :], RH[h, q, :], start=True, stop=True)
                    mm.then_inc(P_.h, P_.one(f"u_{g}{j}"))
                    pe.wait_ge(V_.h, V_.at(f"u_{g}{j}"))
                    for q in range(4):
                        i = 4 * j + q
                        for h in hs:
                            pe.matmul(b4(7)[h, q, :], BS[h, i, :], UU[h, q, :], start=True, stop=False)
                            mm = pe.matmul(b4(7)[h, q, :], KS[h, i, :], VS[h, i, :], start=False, stop=True)
                    mm.then_inc(P_.h, P_.one(f"dx_{g}{j}"))
                    for q in range(4):
                        i = 4 * j + q
                        for h in hs:
                            pe.matmul(b4(j)[h, q, :], old[h, q, :], zr[h, q, at_c[q], 1, :], start=True, stop=False)
                            pe.matmul(b4(j)[h, q, :], UU[h, q, :], MB[h, i, :], start=False, stop=False)
                            mm = pe.matmul(b4(j)[h, q, :], VS[h, i, :], MK[h, i, :], start=False, stop=True)
                    mm.then_inc(P_.h, P_.one(f"y_{g}{j}"))

        @block.scalar
        def _(act):
            for g in range(NCH // 2):
                act.wait_ge(P_.h, P_.at(f"gram_{g}"))
                for name, b, o in (("bs", 5, BS), ("ks", 6, KS), ("vs", 7, VS)):
                    act.activation(o, b8(b), ACT.Copy).then_inc(A_.h, A_.one(f"{name}_{g}"))
                for name, after, b, o in (("d2t", "p1", 1, D2T), ("d4t", "p2", 3, D4T), ("d8", "p3", 0, D8),
                                          ("di", "p5", 3, DI), ("n", "p5", 1, N1), ("ti", "p8", 4, TI)):
                    act.wait_ge(P_.h, P_.at(f"{after}_{g}"))
                    act.activation(o, b8(b), ACT.Copy).then_inc(A_.h, A_.one(f"{name}_{g}"))
                for j in range(2):
                    act.wait_ge(P_.h, P_.at(f"rhs_{g}{j}"))
                    act.activation(RH, b4(5), ACT.Copy).then_inc(A_.h, A_.one(f"rhs_{g}{j}"))
                    act.wait_ge(P_.h, P_.at(f"y_{g}{j}"))
                    for d in range(2):
                        c = CHUNKS[d][2 * g + j]
                        act.activation(Y[:, 2 * d:2 * d + 2, c * CH:(c + 1) * CH],
                                                               b4(j)[:, 2 * d:2 * d + 2, :], ACT.Copy).then_inc(A_.h, A_.one(f"y{d}_{g}{j}"))

        @block.vector
        def _(dve):
            dve.memset(X[:, :, :], 0.0).then_inc(V_.h, V_.one("x0"))
            mzr = C("mask_zr").rearrange("p (q w t) -> p q w t", q=4, w=2)
            mdt = v3(C("mask_dt"), 4)
            zr_of = lambda b: bank(b).rearrange("p (q w t) -> p q w t", q=4, w=2)
            mult = lambda o, a, b: dve.tensor_tensor(o, a, b, ALU.mult)
            add = lambda o, a, b: dve.tensor_tensor(o, a, b, ALU.add)
            for g in range(NCH // 2):
                dve.wait_ge(P_.h, P_.at(f"gram_{g}"))
                for j in range(2):
                    s = slice(4 * j, 4 * j + 4)
                    mult(DT[:, s, :], zr_of(j)[:, :, 0, :], mdt).then_inc(V_.h, V_.one(f"dt{j}_{g}"))
                    mult(MB[:, s, :], zr_of(j)[:, :, 1, :], mzr[:, :, 1, :]).then_inc(V_.h, V_.one(f"mb{j}_{g}"))
                for j in range(2):
                    s = slice(4 * j, 4 * j + 4)
                    mult(AK[:, s, :], zr_of(2 + j)[:, :, 0, :], mzr[:, :, 0, :]).then_inc(V_.h, V_.one(f"ak{j}_{g}"))
                    mult(MK[:, s, :], zr_of(2 + j)[:, :, 1, :], mzr[:, :, 1, :]).then_inc(V_.h, V_.one(f"mk{j}_{g}"))
                both = lambda a: a.rearrange("p (j q) t -> p j (q t)", j=2)
                for name, o in (("d", DD), ("l", LL)):
                    m = C(f"mask_{name}").rearrange("p (j n) -> p j n", j=1).broadcast_to((P, 2, 4 * CH))
                    mult(both(o), both(b8(4)), m).then_inc(V_.h, V_.one(f"{name}_{g}"))
                dve.wait_ge(V_.s.h, V_.s.m)
                add(E1, DT, eye).then_inc(V_.h, V_.one(f"e1_{g}"))
                dve.wait_ge(P_.h, P_.at(f"p1_{g}"))
                dve.tensor_copy(D2, b8(0)).then_inc(V_.h, V_.one(f"d2_{g}"))
                dve.wait_ge(P_.h, P_.at(f"p2_{g}"))
                dve.tensor_copy(D4, b8(2)).then_inc(V_.h, V_.one(f"d4_{g}"))
                add(E2, b8(4), E1).then_inc(V_.h, V_.one(f"e2_{g}"))
                dve.wait_ge(P_.h, P_.at(f"p3_{g}"))
                dve.wait_ge(V_.s.h, V_.s.m)
                add(E3, b8(1), E2).then_inc(V_.h, V_.one(f"e3_{g}"))
                dve.wait_ge(P_.h, P_.at(f"p4_{g}"))
                dve.wait_ge(V_.s.h, V_.s.m)
                add(E4, b8(2), E3).then_inc(V_.h, V_.one(f"e4_{g}"))
                dve.wait_ge(P_.h, P_.at(f"p5_{g}"))
                dve.tensor_copy(NTb, b8(0)).then_inc(V_.h, V_.one(f"nt_{g}"))
                add(INT_, b8(0), eye).then_inc(V_.h, V_.one(f"int_{g}"))
                dve.wait_ge(P_.h, P_.at(f"p6_{g}"))
                dve.tensor_copy(N2, b8(2)).then_inc(V_.h, V_.one(f"n2_{g}"))
                dve.wait_ge(P_.h, P_.at(f"p7_{g}"))
                dve.wait_ge(V_.s.h, V_.s.m)
                add(GG_, b8(3), INT_).then_inc(V_.h, V_.one(f"g_{g}"))
                for j in range(2):
                    old, new = v3(X[:, j, :], 4), v3(X[:, 1 - j, :], 4)
                    dve.wait_ge(P_.h, P_.at(f"u_{g}{j}"))
                    dve.tensor_copy(UU, b4(6)).then_inc(V_.h, V_.one(f"u_{g}{j}"))
                    dve.wait_ge(P_.h, P_.at(f"dx_{g}{j}"))
                    dve.wait_ge(V_.s.h, V_.s.m)
                    add(new, b4(7), old).then_inc(V_.h, V_.one(f"xa_{g}{j}"))
                    dve.wait_ge(V_.s.h, V_.s.m)
                    for d in range(2):
                        c = CHUNKS[d][2 * g + j]
                        o = new[:, 2 * d:2 * d + 2, :]
                        ins = mult(o, o, pc[:, 2 * d:2 * d + 2, c:c + 1].broadcast_to((P, 2, CH)))
                        if d:
                            ins.then_inc(V_.h, V_.one(f"xb_{g}{j}"))
        end_phase()

        fb = Arena(tmp_at)
        dv, sq, sd = fb.take(4 * T, 4), fb.take(4 * T, 4), fb.take(4 * T, 4)
        names = [f"q{q}" for q in range(4)]
        P_, A_ = Steps(S("gn_pe"), ["m" + n for n in names] + ["v" + n for n in names]), \
            Steps(S("gn_act"), ["s" + n for n in names] + ["r" + n for n in names])
        V_ = Steps(S("gn_dve"), ["d" + n for n in names] + [x + n for n in names for x in "ingb"] + ["sum0", "sum1", "o0", "o1"])

        @block.tensor
        def _(pe):
            for q in range(4):
                pe.matmul(bank(q), C("head_sum"), Y[:, q, :], start=True, stop=True).then_inc(P_.h, P_.one(f"mq{q}"))
            for q in range(4):
                pe.wait_ge(A_.h, A_.at(f"sq{q}"))
                pe.matmul(bank(4 + q), C("head_sum"), sq[:, q, :], start=True, stop=True).then_inc(P_.h, P_.one(f"vq{q}"))

        @block.scalar
        def _(act):
            for q in range(4):
                act.wait_ge(V_.h, V_.at(f"dq{q}"))
                act.activation(sq[:, q, :], dv[:, q, :], ACT.Square).then_inc(A_.h, A_.one(f"sq{q}"))
            for q in range(4):
                act.wait_ge(P_.h, P_.at(f"vq{q}"))
                act.activation(sd[:, q, :], bank(4 + q), ACT.Sqrt, bias=eps(EPS_GN), scale=1.0 / DH).then_inc(A_.h, A_.one(f"rq{q}"))

        @block.vector
        def _(dve):
            for q in range(4):
                dve.wait_ge(P_.h, P_.at(f"mq{q}"))
                dve.scalar_tensor_tensor(dv[:, q, :], bank(q), -1.0 / DH, Y[:, q, :], ALU.mult, ALU.add).then_inc(V_.h, V_.one(f"dq{q}"))
            for q in range(4):
                dve.wait_ge(A_.h, A_.at(f"rq{q}"))
                dve.reciprocal(sd[:, q, :], sd[:, q, :]).then_inc(V_.h, V_.one(f"iq{q}"))
                dve.wait_ge(V_.s.h, V_.s.m)
                dve.tensor_tensor(dv[:, q, :], dv[:, q, :], sd[:, q, :], ALU.mult).then_inc(V_.h, V_.one(f"nq{q}"))
                dve.wait_ge(V_.s.h, V_.s.m)
                dve.tensor_scalar(dv[:, q, :], dv[:, q, :], Q1(l, "gn_g", q % 2), Q1(l, "gn_b", q % 2),
                                                    ALU.mult, ALU.add).then_inc(V_.h, V_.one(f"gq{q}"))
                dve.wait_ge(V_.s.h, V_.s.m)
                dve.tensor_tensor(dv[:, q, :], dv[:, q, :], gg[:, q, :], ALU.mult).then_inc(V_.h, V_.one(f"bq{q}"))
            dve.wait_ge(V_.s.h, V_.s.m)
            for hp in range(2):
                dve.tensor_tensor(dv[:, hp, :], dv[:, hp, :], dv[:, 2 + hp, :], ALU.add).then_inc(V_.h, V_.one(f"sum{hp}"))
            dve.wait_ge(V_.s.h, V_.s.m)
            for hp in range(2):
                dve.tensor_tensor(mixT[:, 4 + hp, :], dv[:, hp, :], bon[:, hp, :], ALU.add).then_inc(V_.h, V_.one(f"o{hp}"))
        end_phase()

    def conformer(l, glu, lo_seq, at):
        a = Arena(at)
        ns = 2 - lo_seq
        n = ns * CTX
        acc = [a.take(n, ns) for _ in range(2)]
        sq, sd = a.take(2 * n, 2), a.take(n)
        flat = lambda x: x.rearrange("p s t -> p (s t)")
        tap, fin = S("cv_tap"), S("cv_step")
        V_ = Steps(fin, ["d0", "d1", "inv", "n0", "n1", "g0", "g1"])
        A_ = Steps(S("cv_act"), ["sq0", "sq1", "root", "o0", "o1"])
        P_ = Steps(S("cv_pe"), ["mean", "var"])

        @block.vector
        def _(dve):
            for t in range(CV_TAPS):
                for i in range(2):
                    src = glu[:, i, lo_seq:2, t:t + CTX]
                    if t >= 1:
                        dve.wait_ge(tap.h, tap.at(2 * (t - 1) + i + 1))
                    wt = Q1(l, "cv_w", 2 * t + i)
                    if t == 0:
                        dve.tensor_scalar(acc[i], src, wt, Q1(l, "cv_b", i), ALU.mult, ALU.add).then_inc(tap.h, tap.one())
                    else:
                        dve.scalar_tensor_tensor(acc[i], src, wt, acc[i], ALU.mult, ALU.add).then_inc(tap.h, tap.one())
            dve.wait_ge(P_.h, P_.at("mean"))
            for i in range(2):
                dve.tensor_tensor(flat(acc[i]), flat(acc[i]), bank(0)[:, 0:n], ALU.subtract).then_inc(V_.h, V_.one(f"d{i}"))
            dve.wait_ge(A_.h, A_.at("root"))
            dve.reciprocal(sd, sd).then_inc(V_.h, V_.one("inv"))
            dve.wait_ge(fin.h, fin.m)
            for i in range(2):
                dve.tensor_tensor(flat(acc[i]), flat(acc[i]), sd, ALU.mult).then_inc(V_.h, V_.one(f"n{i}"))
            dve.wait_ge(fin.h, fin.m)
            for i in range(2):
                dve.tensor_scalar(flat(acc[i]), flat(acc[i]), Q1(l, "cv_g", i), Q1(l, "cv_beta", i),
                                                   ALU.mult, ALU.add).then_inc(V_.h, V_.one(f"g{i}"))

        @block.tensor
        def _(pe):
            pe.wait_ge(tap.h, tap.at(2 * CV_TAPS))
            for i in range(2):
                mm = pe.matmul(bank(0)[:, 0:n], C("mean_cv"), flat(acc[i]), start=i == 0, stop=i == 1)
            mm.then_inc(P_.h, P_.one("mean"))
            pe.wait_ge(A_.h, A_.at("sq1"))
            for i in range(2):
                mm = pe.matmul(bank(1)[:, 0:n], C("mean_cv"), sq[:, i, :], start=i == 0, stop=i == 1)
            mm.then_inc(P_.h, P_.one("var"))

        @block.scalar
        def _(act):
            for i in range(2):
                act.wait_ge(V_.h, V_.at(f"d{i}"))
                act.activation(sq[:, i, :], flat(acc[i]), ACT.Square).then_inc(A_.h, A_.one(f"sq{i}"))
            act.wait_ge(P_.h, P_.at("var"))
            act.activation(sd, bank(1)[:, 0:n], ACT.Sqrt, bias=eps(EPS_LN)).then_inc(A_.h, A_.one("root"))
            for i in range(2):
                act.wait_ge(V_.h, V_.at(f"g{i}"))
                act.activation(mixT[:, 6 + i, lo_seq * CTX:T], flat(acc[i]), ACT.Silu).then_inc(A_.h, A_.one(f"o{i}"))
        end_phase()

    def route(gates, at):
        a = Arena(at)
        rt = a.take(KT * N_EXP, KT)
        W = lambda: a.take(2 * N_EXP, 2)
        lg, v1, o1, v2, o2, l2 = W(), W(), W(), W(), W(), W()
        st = [a.take(2, 2) for _ in range(8)]
        gt = a.take(LAT)
        rin = S("router_loaded")

        @block.scalar
        def _(sp):
            sp.dma_start(rt, router_in[:, :].rearrange("p (k e) -> p k e", e=N_EXP)).then_inc(rin.h, 16)
        V_ = Steps(S("route_dve"), ["lg"] + [f"{x}{i}" for i in range(2) for x in ("m", "v", "w", "x", "o")][:5] + ["l2"] +
                   [f"{x}1" for x in ("m", "v", "w", "x", "o")] + ["dif", "one", "inv", "g2", "s0", "s1", "s2", "s3", "gt"])
        A_ = Steps(S("route_act"), ["e", "copy"])
        P_ = Steps(S("route_pe"), ["lg", "t", "b0", "b1"])
        iota = con[:, CON["iota"][0]:CON["iota"][1]]

        @block.tensor
        def _(pe):
            pe.wait_ge(rin.h, 16)
            for tt in range(2):
                for k in range(KT):
                    mm = pe.matmul(bank(0)[:, tt * 8:tt * 8 + 8], hT[:, k, CTX + tt * P:CTX + (tt + 1) * P], rt[:, k, :],
                                   start=k == 0, stop=k == KT - 1)
            mm.then_inc(P_.h, P_.one("lg"))
            pe.wait_ge(V_.h, V_.at("s3"))
            for tt in range(2):
                mm = pe.transpose(bank(1)[0:8, tt * P:(tt + 1) * P], v2[:, tt, :], C("ident"))
            mm.then_inc(P_.h, P_.one("t"))
            pe.wait_ge(V_.h, V_.at("gt"))
            for e in range(N_EXP):
                b = 2 + (e % 4)
                if e == 4:
                    pe.wait_ge(A_.h, A_.at("copy"))
                mm = pe.matmul(bank(b)[:, 0:LAT], con[0:8, CON["sel"][0] + e * P:CON["sel"][0] + (e + 1) * P], gt[0:8, :],
                               start=True, stop=True)
                if e % 4 == 3:
                    mm.then_inc(P_.h, P_.one(f"b{e // 4}"))

        @block.scalar
        def _(act):
            act.wait_ge(V_.h, V_.at("dif"))
            act.activation(st[3][:, :], st[2][:, :], ACT.Exp).then_inc(A_.h, A_.one("e"))
            for half in range(2):
                act.wait_ge(P_.h, P_.at(f"b{half}"))
                ins = act.activation(gates[:, 4 * half:4 * half + 4, :], v3(banks[:, 2 * 512:6 * 512], 4)[:, :, 0:LAT], ACT.Copy)
                if half == 0:
                    ins.then_inc(A_.h, A_.one("copy"))

        @block.vector
        def _(dve):
            me = V_.s
            wide = lambda s: s.broadcast_to((P, 2, N_EXP))
            it = iota.rearrange("p (o e) -> p o e", o=1).broadcast_to((P, 2, N_EXP))
            dve.wait_ge(P_.h, P_.at("lg"))
            dve.tensor_copy(lg, v3(bank(0)[:, 0:16], 2)).then_inc(V_.h, V_.one("lg"))

            def pick(i, src, v, o):
                dve.wait_ge(me.h, me.m)
                dve.tensor_reduce(st[i], src, AX.X, ALU.max).then_inc(V_.h, V_.one(f"m{i}"))
                dve.wait_ge(me.h, me.m)
                dve.tensor_tensor(v, src, wide(st[i]), ALU.is_equal).then_inc(V_.h, V_.one(f"v{i}"))
                dve.wait_ge(me.h, me.m)
                dve.scalar_tensor_tensor(v, v, -100.0, it, ALU.mult, ALU.add).then_inc(V_.h, V_.one(f"w{i}"))
                dve.wait_ge(me.h, me.m)
                dve.tensor_reduce(st[4 + i], v, AX.X, ALU.min).then_inc(V_.h, V_.one(f"x{i}"))
                dve.wait_ge(me.h, me.m)
                dve.tensor_tensor(o, v, wide(st[4 + i]), ALU.is_equal).then_inc(V_.h, V_.one(f"o{i}"))
            pick(0, lg, v1, o1)
            dve.wait_ge(me.h, me.m)
            dve.scalar_tensor_tensor(l2, o1, NEG, lg, ALU.mult, ALU.add).then_inc(V_.h, V_.one("l2"))
            pick(1, l2, v2, o2)
            dve.tensor_tensor(st[2], st[1], st[0], ALU.subtract).then_inc(V_.h, V_.one("dif"))
            dve.wait_ge(A_.h, A_.at("e"))
            dve.tensor_scalar(st[6], st[3], 1.0, None, ALU.add).then_inc(V_.h, V_.one("one"))
            dve.wait_ge(me.h, me.m)
            dve.reciprocal(st[6], st[6]).then_inc(V_.h, V_.one("inv"))
            dve.wait_ge(me.h, me.m)
            dve.tensor_tensor(st[7], st[3], st[6], ALU.mult).then_inc(V_.h, V_.one("g2"))
            dve.wait_ge(me.h, me.m)
            dve.tensor_tensor(v1, o1, wide(st[6]), ALU.mult).then_inc(V_.h, V_.one("s0"))
            dve.tensor_tensor(l2, o2, wide(st[7]), ALU.mult).then_inc(V_.h, V_.one("s1"))
            dve.wait_ge(me.h, me.m)
            dve.tensor_tensor(v2, v1, l2, ALU.add).then_inc(V_.h, V_.one("s2"))
            dve.wait_ge(me.h, me.m)
            dve.tensor_copy(o1, v2).then_inc(V_.h, V_.one("s3"))
            dve.wait_ge(P_.h, P_.at("t"))
            dve.tensor_copy(gt[0:8, :], bank(1)[0:8, 0:LAT]).then_inc(V_.h, V_.one("gt"))
        end_phase()

    def mixer_inputs(l):
        ctx_out = l < DEPTH - 1
        first = 0 if ctx_out else CTX
        a = Arena()
        us = a.take(10 * T, 10)
        glu = a.take(2 * 2 * (CTX + 2 * CV_PAD)).rearrange("p (i s t) -> p i s t", i=2, s=2)
        q, k, v = a.take(4 * T, 4), a.take(4 * T, 4), a.take(4 * T, 4)
        bias = a.take(2 * NA_H * LAT, 2 * NA_H)
        at = a.at
        gate = a.take(2 * T, 2)
        rw_tiles = [dict(part=6 + t // 2, j=t % 2, cols=(0, T), src=hT, owner="dve") for t in range(10)]
        tiles = [dict(part=t // 2, j=t % 2, cols=(first, T), src=hT, owner="act") for t in range(4)]
        tiles += [dict(part=2 + t // 2, j=t % 2, cols=(0, T), src=hT, owner="act") for t in range(4)]
        tiles += [dict(part=4 + p, tok=t, cols=(0, T), src=hT, owner="act") for p in range(2) for t in range(4)]
        tiles += rw_tiles
        tiles += [dict(part=11, j=t, cols=(first, T), src=hT, owner="act") for t in range(2)]
        tiles += [dict(part=12, j=t, cols=(first, T), src=hT, owner="dve") for t in range(2)]
        tile_done, free = project(tiles)
        own_part, sig, b_in, b_ok = S("shift_own"), S("conv_gate"), S("bias_loaded"), S("bias_masked")

        @block.scalar
        def _(act):
            act.dma_start(bias, bias_in[l, :, :].rearrange("p (q k) -> p q k", k=LAT)).then_inc(b_in.h, 16)
            for t in range(len(tiles)):
                bk = bank(t % 8)
                act.wait_ge(*tile_done(t))
                if t < 4:
                    act.activation(q[:, t, first:T], bk[:, 0:T - first], ACT.Copy, scale=DH ** -0.5).then_inc(free["act"].h, free["act"].one())
                elif t < 8:
                    act.activation(k[:, t - 4, :], bk, ACT.Copy).then_inc(free["act"].h, free["act"].one())
                elif t < 16:
                    p, tok = divmod(t - 8, 4)
                    act.activation(v[:, tok, p * UNIT:(p + 1) * UNIT], bk[:, 0:UNIT], ACT.Copy).then_inc(free["act"].h, free["act"].one())
                elif t < 26:
                    act.activation(us[:, t - 16, :], bk, ACT.Copy, scale=scal[:, 32 + t - 16:33 + t - 16]).then_inc(own_part.h, own_part.one())
                elif t < 28:
                    act.activation(gate[:, t - 26, first:T], bk[:, 0:T - first], ACT.Sigmoid).then_inc(free["act"].h, free["act"].one())

        @block.vector
        def _(dve):
            own_pad = S("conv_pad")
            for s in range(2):
                dve.memset(glu[:, :, s, 0:CV_PAD], 0.0).then_inc(own_pad.h, own_pad.one())
                dve.memset(glu[:, :, s, CV_PAD + CTX:], 0.0).then_inc(own_pad.h, own_pad.one())
            dve.wait_ge(b_in.h, 16 * (l + 1))
            for h in range(2):
                bh = bias[:, h * NA_H:(h + 1) * NA_H, :].rearrange("p h (r c) -> p (h r) c", c=64)
                for i, (name, op) in enumerate((("win", ALU.mult), ("out_win", ALU.add))):
                    dve.wait_ge(b_ok.h, b_ok.at(2 * h + i))
                    m = C(name).rearrange("p (o k) -> p o k", o=1).broadcast_to((P, NA_H * 4, 64))
                    dve.tensor_tensor(bh, bh, m, op).then_inc(b_ok.h, b_ok.one())
            side = S("shift_side")
            for t in range(16, 26):
                i = t - 16
                dve.wait_ge(own_part.h, own_part.at(i + 1))
                u3, p3 = (x.rearrange("p (s t) -> p s t", s=2) for x in (us[:, i, :], bank(t % 8)))
                dve.scalar_tensor_tensor(u3[:, :, 1:CTX], p3[:, :, 0:CTX - 1], Q1(l, "mu_prev", i), u3[:, :, 1:CTX],
                                                  ALU.mult, ALU.add).then_inc(side.h, side.one())
                dve.wait_ge(side.h, side.at(i + 1))
                dve.scalar_tensor_tensor(u3[:, :, 0:CTX - 1], p3[:, :, 1:CTX], Q1(l, "mu_next", i),
                                                         u3[:, :, 0:CTX - 1], ALU.mult, ALU.add).then_inc(free["dve"].h, free["dve"].one())
            for t in range(28, 30):
                i = t - 28
                dve.wait_ge(*tile_done(t))
                dve.wait_ge(free["act"].h, free["act"].at(18))
                ns = (T - first) // CTX
                dve.tensor_tensor(glu[:, i, 2 - ns:2, CV_PAD:CV_PAD + CTX],
                                                  bank(t % 8)[:, 0:T - first].rearrange("p (s t) -> p s t", s=ns),
                                                  gate[:, i, first:T].rearrange("p (s t) -> p s t", s=ns), ALU.mult).then_inc(free["dve"].h, free["dve"].one())
        end_phase()
        units = []
        for h in range(NA_H):
            for t in range(2):
                units.append((h // 2, h % 2, CTX + t * P, [(CTX, T), (0, CTX)], [2, 3, 0, 1], bias[:, t * NA_H + h, :], CTX))
        k_same, v_cols = (lambda tile: tile), (lambda tile, half: tile * P + half * DH)
        attention(units, q, k, v, 1.0, LAT, k_same, v_cols, at)
        if ctx_out:
            units = [(h // 2, h % 2, t * P, [(0, CTX)], [0, 1], None, 0) for h in range(NA_H) for t in range(2)]
            attention(units, q, k, v, 1.0, CTX, k_same, v_cols, at)
        conformer(l, glu, 0 if ctx_out else 1, at)
        recurrence(l, us, 10 * T)

    def second_mixers(l):
        a = Arena()
        qk = a.take(5 * LAT, 5)
        v = a.take(2 * P, 2)
        sv, su, cb, cc = (a.take(2 * LAT, 2) for _ in range(4))
        cx = a.take(2 * (LAT + 2), 2)
        qn, sq, sd = a.take(5 * LAT, 5), a.take(7 * LAT, 7), a.take(6 * LAT, 6)
        vnt, sgw, sgb, cv = a.take(2 * 2 * P, 2), a.take(4 * P, 4), a.take(P), a.take(2 * LAT, 2)
        at = a.at
        lat = (CTX, T)
        tiles = [dict(part=t // 2, j=t % 2, cols=lat, src=hT, owner="act") for t in range(4)]
        tiles += [dict(part=2, j=0, cols=lat, src=hT, owner="act")]
        tiles += [dict(part=2, tok=2 + t, wide=P, cols=lat, src=hT, owner="act") for t in range(2)]
        tiles += [dict(part=3 + t // 2, j=t % 2, cols=lat, src=hT, owner="act") for t in range(8)]
        tiles += [dict(part=7, j=t, cols=lat, src=hT, owner="dve") for t in range(2)]
        tile_done, free = project(tiles)
        s_in = S("gating_loaded")

        @block.scalar
        def _(act):
            act.dma_start(sgw, sgw_in[l, :, :].rearrange("p (h n) -> p h n", h=4)).then_inc(s_in.h, 16)
            act.dma_start(sgb[0:4, :], sgb_in[l, :, :]).then_inc(s_in.h, 16)
            for t in range(15):
                act.wait_ge(*tile_done(t))
                bk = bank(t % 8)
                if t < 5:
                    o = qk[:, t, :]
                elif t < 7:
                    o = v[:, t - 5, :]
                else:
                    o = (sv, su, cb, cc)[(t - 7) // 2][:, (t - 7) % 2, :]
                n = P if 5 <= t < 7 else LAT
                act.activation(o, bk[:, 0:n], ACT.Copy).then_inc(free["act"].h, free["act"].one())

        @block.vector
        def _(dve):
            pad = S("conv_pad")
            dve.memset(cx[:, :, 0:1], 0.0).then_inc(pad.h, pad.one())
            dve.memset(cx[:, :, LAT + 1:LAT + 2], 0.0).then_inc(pad.h, pad.one())
            for i in range(2):
                dve.wait_ge(*tile_done(15 + i))
                dve.wait_ge(free["act"].h, free["act"].at(15))
                dve.tensor_tensor(cx[:, i, 1:LAT + 1], bank((15 + i) % 8)[:, 0:LAT], cc[:, i, :], ALU.mult).then_inc(free["dve"].h, free["dve"].one())
        end_phase()

        sA, sP, sV = S("m2_act"), S("m2_pe"), S("m2_dve")
        A_ = Steps(sA, [f"sq{t}" for t in range(7)] + [f"rt{t}" for t in range(6)] + ["tn0", "tn1"])
        P_ = Steps(sP, [f"ms{t}" for t in range(6)] + [f"sw{t}" for t in range(5)] + ["vt", "mixed"])
        V_ = Steps(sV, ["c00", "c01", "c10", "c11", "c20", "c21", "cm0", "cm1"] + [f"i{t}" for t in range(6)] +
                   [f"n{t}" for t in range(7)] + [f"{x}{t}" for t in range(5) for x in ("sin", "cos", "rot")] + ["g0", "g1"])
        bk = lambda t: bank(t)[:, 0:LAT]

        @block.scalar
        def _(act):
            for t in range(7):
                act.activation(sq[:, t, :], qk[:, t, :] if t < 5 else sv[:, t - 5, :], ACT.Square).then_inc(A_.h, A_.one(f"sq{t}"))
            for t in range(6):
                act.wait_ge(P_.h, P_.at(f"ms{t}"))
                act.activation(sd[:, t, :], bk(t), ACT.Sqrt, bias=eps(EPS_RMS),
                                                 scale=1.0 / DH if t < 5 else 1.0).then_inc(A_.h, A_.one(f"rt{t}"))
            act.wait_ge(P_.h, P_.at("vt"))
            for c in range(2):
                act.activation(vnt[:, c, :], bank(6)[:, c * 256:(c + 1) * 256], ACT.Copy).then_inc(A_.h, A_.one(f"tn{c}"))

        @block.tensor
        def _(pe):
            for t in range(5):
                pe.wait_ge(A_.h, A_.at(f"sq{t}"))
                pe.matmul(bk(t), C("head_sum"), sq[:, t, :], start=True, stop=True).then_inc(P_.h, P_.one(f"ms{t}"))
            pe.wait_ge(A_.h, A_.at("sq6"))
            for i in range(2):
                mm = pe.matmul(bk(5), C("mean_cv"), sq[:, 5 + i, :], start=i == 0, stop=i == 1)
            mm.then_inc(P_.h, P_.one("ms5"))
            for t in range(5):
                pe.wait_ge(V_.h, V_.at(f"n{t}"))
                pe.matmul(bk(t), C("swap"), qn[:, t, :],
                                            start=True, stop=True).then_inc(P_.h, P_.one(f"sw{t}"))
            pe.wait_ge(V_.h, V_.at("n6"))
            for c in range(2):
                for i in range(2):
                    mm = pe.transpose(bank(6)[:, c * 256 + i * P:c * 256 + (i + 1) * P], sq[:, 5 + i, c * P:(c + 1) * P],
                                      C("ident"))
            mm.then_inc(P_.h, P_.one("vt"))
            pe.wait_ge(A_.h, A_.at("tn1"))
            pe.wait_ge(s_in.h, 32 * (l + 1))
            for h in range(4):
                hs = slice((h % 2) * DH, (h % 2) * DH + DH)
                for c in range(2):
                    o = bank(7)[hs, (h // 2) * LAT + c * P:(h // 2) * LAT + (c + 1) * P]
                    pe.matmul(o, vnt[:, c, h * DH:(h + 1) * DH], sgw[:, h, :], start=True, stop=False)
                    lo = CON["sel"][0] + h * P
                    mm = pe.matmul(o, con[0:4, lo:lo + DH], sgb[0:4, :], start=False, stop=True)
            mm.then_inc(P_.h, P_.one("mixed"))

        @block.vector
        def _(dve):
            for tap in range(3):
                dve.wait_ge(sV.h, sV.m)
                for i in range(2):
                    w, x = Q2(l, "conv_w", 2 * tap + i), cx[:, i, tap:tap + LAT]
                    ins = dve.tensor_scalar(cv[:, i, :], x, w, None, ALU.mult) if tap == 0 else \
                        dve.scalar_tensor_tensor(cv[:, i, :], x, w, cv[:, i, :], ALU.mult, ALU.add)
                    ins.then_inc(V_.h, V_.one(f"c{tap}{i}"))
            dve.wait_ge(sV.h, sV.m)
            for i in range(2):
                dve.tensor_tensor(mixT[:, 6 + i, CTX:T], cv[:, i, :], cb[:, i, :], ALU.mult).then_inc(V_.h, V_.one(f"cm{i}"))
            for t in range(6):
                dve.wait_ge(A_.h, A_.at(f"rt{t}"))
                dve.reciprocal(sd[:, t, :], sd[:, t, :]).then_inc(V_.h, V_.one(f"i{t}"))
            dve.wait_ge(sV.h, sV.m)
            for t in range(5):
                dve.scalar_tensor_tensor(qn[:, t, :], qk[:, t, :], Q2(l, "q_g" if t < 4 else "k_g", 0),
                                                          sd[:, t, :], ALU.mult, ALU.mult).then_inc(V_.h, V_.one(f"n{t}"))
            dve.wait_ge(P_.h, P_.at("ms5"))
            for i in range(2):
                dve.scalar_tensor_tensor(sq[:, 5 + i, :], sv[:, i, :], Q2(l, "sg_g", i), sd[:, 5, :],
                                                              ALU.mult, ALU.mult).then_inc(V_.h, V_.one(f"n{5 + i}"))
            for t in range(5):
                dve.wait_ge(P_.h, P_.at(f"sw{t}"))
                dve.tensor_tensor(qk[:, t, :], bk(t), C("sin"),
                                                     ALU.mult).then_inc(V_.h, V_.one(f"sin{t}"))
                dve.tensor_tensor(qn[:, t, :], qn[:, t, :], C("cos"), ALU.mult).then_inc(V_.h, V_.one(f"cos{t}"))
                dve.wait_ge(sV.h, sV.m)
                dve.tensor_tensor(qk[:, t, :], qk[:, t, :], qn[:, t, :], ALU.add).then_inc(V_.h, V_.one(f"rot{t}"))
            dve.wait_ge(P_.h, P_.at("mixed"))
            for i in range(2):
                dve.tensor_tensor(mixT[:, 4 + i, CTX:T], bank(7)[:, i * LAT:(i + 1) * LAT], su[:, i, :],
                                                   ALU.mult).then_inc(V_.h, V_.one(f"g{i}"))
        end_phase()
        units = [(j, g, t * P, [(0, LAT)], [0, 1], None, CTX) for j in range(4) for g in range(2) for t in range(2)]
        attention(units, qk, qk, v, DH ** -0.5, LAT, lambda tile: 4, lambda tile, half: half * DH, at)

    ready = S("inputs_loaded")

    @block.scalar
    def _(act):
        act.dma_start(ct[:, :], ct_in[:, :]).then_inc(ready.h, 16)
        act.dma_start(con[:, :], con_in[:, :]).then_inc(ready.h, 16)
        act.dma_start(x_buf[:, :], xt_in[:, :]).then_inc(ready.h, 16)
        for l in range(DEPTH):
            act.dma_start(par1[l][:, :], par1_in[l, :, :]).then_inc(ready.h, 16)
            act.dma_start(par2[l][:, :], par2_in[l, :, :]).then_inc(ready.h, 16)
        act.wait_ge(ready.h, 16 * 7)
        act.activation(ct[:, :], ct[:, :], ACT.Silu).then_inc(S("condition").h, S("condition").one())
    end_phase()

    def gated(l_gate, s):
        def put(dve, m, acc):
            cols = xT[:, m, s * CTX:(s + 1) * CTX]
            if l_gate:
                ins = dve.scalar_tensor_tensor(cols, acc, modc(40 + m, s), cols, ALU.mult, ALU.add)
            else:
                ins = dve.tensor_tensor(cols, acc, cols, ALU.add)
            ins.then_inc(S("residual").h, S("residual").one())
        return put

    for l in range(DEPTH):
        ctx_out = l < DEPTH - 1
        cols = (0, T) if ctx_out else (CTX, T)
        modulation(l)
        norm(xT, hT, (0, T), gain1, modc, "1")
        mixer_inputs(l)
        out_project(mixT, cols, lambda t, s: modc(16 + t, s))
        norm(xT, hT, cols, gain2, lambda t, s: modc(24 + t, s), "2")
        if l % 2 == 0:
            feed_forward("silu", 1, FF_UNITS, hT, CTX, gated(True, 1))
            if ctx_out:
                stream["skew"] += 3 * FF_UNITS
                feed_forward("silu", 1, FF_UNITS, hT, 0, gated(True, 0))
        else:
            gates = Arena().take(N_EXP * LAT, N_EXP)
            route(gates, N_EXP * LAT)
            feed_forward("expert", N_EXP, FFE_UNITS, hT, CTX, gated(True, 1), gates=gates, at=N_EXP * LAT)
    lat = (CTX, T)
    norm(xT, xT, lat, lambda k, s: Q1(0, "final_g", k), None, "final")
    for l in range(DEPTH):
        norm(xT, hT, lat, lambda k, s, l=l: Q2(l, "norm1_g", k), None, "1")
        second_mixers(l)
        out_project(mixT, lat, None)
        norm(xT, hT, lat, lambda k, s, l=l: Q2(l, "norm2_g", k), None, "2")
        feed_forward("conv", 1, FF_UNITS, hT, CTX, gated(False, 1),
                     taps=lambda tap, t, l=l: Q2(l, "ffn_w", 44 * tap + t))

    @block.scalar
    def _(act):
        stored = S("output_stored")
        act.dma_start(out[:, :].rearrange("p (k t) -> p k t", k=KT), xT[:, :, CTX:T]).then_inc(stored.h, 16)
        act.wait_ge(stored.h, 16)
    assert stream["put"] == stream["got"]
    ctx.close()
    return stream["got"] - stream["skew"]


def cols_of(w):
    n = w.shape[1] // UNIT
    return w.reshape(KT, P, n, UNIT).transpose(2, 1, 0, 3).reshape(n, P, PART)


def rows_of(w):
    n = w.shape[0] // UNIT
    return w.reshape(n, 2, P, D).transpose(0, 2, 1, 3).reshape(n, P, PART)


def ff_parts(gate, up, down):
    n = len(gate)
    out = [gate[0], up[0]]
    for u in range(1, n):
        out += [gate[u], up[u], down[u - 1]]
    return out + [down[n - 1]]


def columns(v):
    return np.asarray(v).reshape(-1, P).T


def kernel(**i):
    import concourse.bacc as bacc
    from concourse.bass_utils import run_bass_kernel_spmd as run

    i = {k: np.asarray(v) for k, v in i.items()}
    parts = []
    for l in range(DEPTH):
        parts += list(cols_of(i["mod_w"][l]))
        w = i["w_in"][l]
        o_cv = 3 * NA_W + RW_IN
        parts += list(cols_of(w[:, :o_cv])) + list(cols_of(w[:, o_cv + 256:])) + list(cols_of(w[:, o_cv:o_cv + 256]))
        parts += list(cols_of(i["w_out"][l]))
        if l % 2 == 0:
            j = l // 2
            parts += ff_parts(cols_of(i["ffn_w_gate"][j]), cols_of(i["ffn_w_up"][j]), rows_of(i["ffn_w_down"][j]))
        else:
            j = l // 2
            parts += ff_parts([p for e in range(N_EXP) for p in cols_of(i["moe_w_gate"][j, e])],
                              [p for e in range(N_EXP) for p in cols_of(i["moe_w_up"][j, e])],
                              [p for e in range(N_EXP) for p in rows_of(i["moe_w_down"][j, e])])
    for l in range(DEPTH):
        w = i["w_in_2"][l]
        heads = [h * DH + f for t in range(4) for h in (t, t + 4) for f in range(DH)]
        q, kv, su, sv, rest = w[:, :512][:, heads], w[:, 512:768], w[:, 768:1024], w[:, 1024:1280], w[:, 1280:]
        parts += list(cols_of(np.concatenate([q, kv, sv, su, rest], 1)))
        wo = i["w_out_2"][l]
        parts += list(cols_of(np.concatenate([wo[:512][heads], wo[512:]], 0)))
        up = i["ffn_w_up_2"][l]
        parts += ff_parts(cols_of(up[:, :D_FF]), cols_of(up[:, D_FF:]), rows_of(i["ffn_w_down_2"][l]))
    n_parts = len(parts)
    xt = np.concatenate([i["ctx"][0], i["x"][0]], 0).T.reshape(KT, P, T).transpose(1, 0, 2).reshape(P, KT * T)
    ct = np.stack([i["c_ctx"], i["c"][0]], 1).reshape(KT, P, 2).transpose(1, 0, 2).reshape(P, KT * 2)
    par1, par2, lora, gate2, bias = [], [], [], [], []
    qr, qc = np.arange(LAT) // 64, np.arange(LAT) % 64
    r_at = qr[None, :] - qr[:, None] + 7
    c_at = qc[None, :] - qc[:, None] + 15
    near = (c_at >= 0) & (c_at <= 30)
    for l in range(DEPTH):
        vec = dict(norm1_g="norm1_g", norm2_g="norm2_g", mod_b="mod_b", mu_prev="rw_mu_prev", mu_next="rw_mu_next",
                   w0="rw_w0", a0="rw_a0", k_k="rw_k_k", k_a="rw_k_a", r_k="rw_r_k", gn_g="rw_gn_g", gn_b="rw_gn_b",
                   cv_b="cv_dw_b", cv_g="cv_ln_g", cv_beta="cv_ln_b", cv_w="cv_dw_w")
        par1.append(np.concatenate([columns(i["final_g"] if n == "final_g" else i[vec[n]][l]) for n in P1], 1))
        q_g, k_g = (np.concatenate([i[n][l]] * 2) for n in ("q_norm_g_2", "k_norm_g_2"))
        par2.append(np.concatenate([columns(v) for v in (i["norm1_g_2"][l], i["norm2_g_2"][l], q_g, k_g, i["sg_norm_g_2"][l],
                                                         i["conv_w_2"][l], i["ffn_conv_w_2"][l])], 1))
        lora.append(np.concatenate([i["rw_w2"][l], i["rw_a2"][l]], 1).transpose(1, 0, 2).reshape(P, 512))
        gate2.append(i["rw_g2"][l].transpose(1, 0, 2).reshape(P, 512))
        b = i["na_rpb"][l][:, r_at, np.clip(c_at, 0, 30)]
        b = np.where(near, b, np.float32(0))
        bias.append(b.reshape(NA_H, 2, P, LAT).transpose(2, 1, 0, 3).reshape(P, -1))
    router = i["moe_router"][0].reshape(KT, P, N_EXP).transpose(1, 0, 2).reshape(P, KT * N_EXP)
    sgw = i["sg_w_2"].transpose(0, 3, 1, 2).reshape(DEPTH, P, 4 * P)
    arrays = {
        "parts": np.stack(parts), "xt": xt, "ct": ct, "con": constants(), "par1": np.stack(par1), "par2": np.stack(par2),
        "lora": np.stack(lora), "gate2": np.stack(gate2), "router": router, "bias": np.stack(bias), "sgw": sgw,
        "sgb": i["sg_b_2"],
    }
    nc = bacc.Bacc("TRN2", target_bir_lowering=False, num_devices=1)
    args = []
    for name, a in arrays.items():
        arrays[name] = np.ascontiguousarray(a)
        args.append(nc.dram_tensor(name, a.shape, F32, kind="ExternalInput").ap())
    args.append(nc.dram_tensor("out", (P, KT * LAT), F32, kind="ExternalOutput").ap())
    assert build(nc, *args) == n_parts
    got = run(nc, [arrays], core_ids=[0]).results[0]["out"]
    return got.reshape(P, KT, LAT).transpose(2, 1, 0).reshape(1, LAT, D)
```

```python
from contextlib import ExitStack

import numpy as np

import concourse.bass as bass
from concourse import mybir

F32 = mybir.dt.float32
ACT = mybir.ActivationFunctionType
ALU = mybir.AluOpType
AX = mybir.AxisListType

P = 128
D = 1024
KT = D // P
CTX, LAT = 256, 256
T = CTX + LAT
DH = 64
DEPTH = 2
NA_H, NA_W = 8, 512
RW_W, RW_IN = 256, 1280
CV_TAPS, CV_PAD = 31, 15
D_FF, D_FFE, N_EXP = 2816, 3584, 8
UNIT = 256
PART = KT * UNIT
RING = 6
CH = 64
NCH = T // CH
NEG = -1.0e30
FF_UNITS, FFE_UNITS = D_FF // UNIT, D_FFE // UNIT
MOD_PARTS = 6 * D // UNIT
SG_CHUNK = 128

CHUNKS = [list(range(NCH)), [3, 2, 1, 0, 7, 6, 5, 4]]

P1 = {}
_at = 0
for _name, _n in [("norm1_g", 8), ("norm2_g", 8), ("mod_b", 48), ("mu_prev", 10), ("mu_next", 10),
                  ("w0", 4), ("a0", 4), ("k_k", 2), ("k_a", 2), ("r_k", 2), ("gn_g", 2), ("gn_b", 2),
                  ("cv_b", 2), ("cv_g", 2), ("cv_beta", 2), ("cv_w", 2 * CV_TAPS), ("final_g", 8)]:
    P1[_name] = (_at, _at + _n)
    _at += _n
P1_COLS = _at
P2 = {}
_at = 0
for _name, _n in [("norm1_g", 8), ("norm2_g", 8), ("q_g", 1), ("k_g", 1), ("sg_g", 2), ("conv_w", 6),
                  ("ffn_w", 3 * 44)]:
    P2[_name] = (_at, _at + _n)
    _at += _n
P2_COLS = _at

CON = {}
_at = 0
for _name, _n in [("mean_d", 128), ("head_sum", 128), ("ident", 128), ("eye64", 64), ("mask_zr", 512),
                  ("mask_d", 256), ("mask_l", 256), ("mask_dt", 256), ("not_first", 512), ("swap", 128),
                  ("cos", 256), ("sin", 256), ("win", 64), ("out_win", 64), ("sel", 512),
                  ("eps", 8), ("iota", 8), ("mean_cv", 128), ("ones", 128),
                  ("before", 128), ("slot", 128)]:
    CON[_name] = (_at, _at + _n)
    _at += _n
CON_COLS = _at
EPS_RMS, EPS_LN, EPS_GN, EPS_KK = 0, 1, 2, 3


def constants():
    c = np.zeros((P, CON_COLS), np.float32)

    def put(name, a):
        lo, hi = CON[name]
        c[:a.shape[0], lo:hi] = a
    p = np.arange(P)
    put("mean_d", np.full((P, P), 1.0 / D))
    put("head_sum", (p[:, None] // DH == p[None, :] // DH) * 1.0)
    put("ident", np.eye(P))
    put("eye64", (p[:, None] % CH == np.arange(CH)[None, :]) * 1.0)
    row = (p % CH)[:, None]
    col = np.arange(CH)[None, :]
    fwd_st, bwd_st = (row < col) * 1.0, (row > col) * 1.0
    fwd_in, bwd_in = (row <= col) * 1.0, (row >= col) * 1.0
    same = (row // 16 == col // 16) * 1.0
    two = lambda f, b: [f, f, b, b]
    put("mask_zr", np.concatenate([np.concatenate(x, 1) for x in
                                   [(fwd_st, fwd_in)] * 2 + [(bwd_st, bwd_in)] * 2], 1))
    put("mask_dt", np.concatenate(two(fwd_st * same, bwd_st * same), 1))
    put("mask_d", np.concatenate(two(bwd_st * same, fwd_st * same), 1))
    put("mask_l", np.concatenate(two(bwd_st * (1 - same), fwd_st * (1 - same)), 1))
    put("not_first", np.tile((np.arange(T) % CH != 0) * 1.0, (P, 1)))
    f = p % DH
    axis, half, freq = f // 32, (f % 32) // 16, f % 16
    inv = (1.0 / (10000.0 ** (np.arange(16, dtype=np.float32) * np.float32(2.0) / np.float32(32)))).astype(np.float32)
    tok = np.arange(LAT)
    pos = np.where(axis[:, None] == 0, tok[None, :] // 64, tok[None, :] % 64).astype(np.float32)
    ang = pos * inv[freq][:, None]
    put("cos", np.cos(ang).astype(np.float32))
    put("sin", (np.sin(ang) * np.where(half == 0, -1.0, 1.0)[:, None]).astype(np.float32))
    partner = np.where(half == 0, p + 16, p - 16)
    put("swap", (p[:, None] == partner[None, :]) * 1.0)
    qc, kc = (p % 64)[:, None], np.arange(64)[None, :]
    ws = np.clip(qc - 8, 0, 48)
    inside = (kc >= ws) & (kc < ws + 16)
    put("win", inside * 1.0)
    put("out_win", np.where(inside, 0.0, NEG))
    put("sel", np.concatenate([(p[0:8, None] == e) * np.ones((1, P)) for e in range(4)], 1))
    lo, _ = CON["eps"]
    for at, v in ((EPS_RMS, 1e-6), (EPS_LN, 1e-5), (EPS_GN, 64e-5), (EPS_KK, 1e-12)):
        c[:, lo + at] = v
    put("ones", np.ones((P, P)))
    put("before", (p[:, None] < p[None, :]) * 1.0)
    put("slot", np.tile(np.arange(P) * 1.0, (P, 1)))
    put("mean_cv", np.full((P, P), 1.0 / 256))
    put("iota", np.tile(np.arange(8.0), (P, 1)))
    return c


class Steps:

    def __init__(self, signal, names):
        self.s, self.names, self.i = signal, names, 0

        self.h = signal.h

    def one(self, name):
        assert self.names[self.i] == name, (self.names[self.i], name)
        self.i += 1
        return self.s.one()

    def at(self, name):
        return self.s.at(self.names.index(name) + 1)


class Signal:

    def __init__(self, handle):
        self.h, self.n, self.m = handle, 0, 0

    def one(self, times=1):
        self.m += times
        return 1

    def at(self, k):
        return max(self.n + k, 0) if isinstance(k, int) else k + self.n


def build(nc, parts, xt_in, ct_in, con_in, par1_in, par2_in, lora_in, gate2_in, router_in, bias_in,
          sgw_in, sgb_in, out):
    ctx = ExitStack()
    sb = lambda name, cols: ctx.enter_context(nc.sbuf_tensor(name, [P, cols], F32))
    sems = {}

    def S(name):
        if name not in sems:
            sems[name] = Signal(ctx.enter_context(nc.semaphore(name)))
        return sems[name]

    x_buf = sb("x_buf", KT * T)
    h_buf = sb("h_buf", KT * T)
    mix_buf = sb("mix_buf", KT * T)
    ring = sb("ring", RING * PART)
    con = sb("constants", CON_COLS)
    par1 = [sb(f"par1_{l}", P1_COLS) for l in range(DEPTH)]
    par2 = [sb(f"par2_{l}", P2_COLS) for l in range(DEPTH)]
    modv = [sb(f"modv_{l}", 48 * 2) for l in range(DEPTH)]
    scal = [sb(f"scal_{l}", 44) for l in range(DEPTH)]
    mod_rows = sb("mod_rows", 2 * UNIT)
    passes = ctx.enter_context(nc.sbuf_tensor("passes", [P, 1], mybir.dt.int32))
    ct = sb("condition_buf", KT * 2)
    arena = sb("arena", 22560)
    banks = ctx.enter_context(nc.psum_tensor("banks", [P, 8 * 512], F32))

    v3 = lambda a, n: a.rearrange("p (a b) -> p a b", a=n)
    xT, hT, mixT = (v3(b[:, :], KT) for b in (x_buf, h_buf, mix_buf))
    bank = lambda i: banks[:, i * 512:(i + 1) * 512]
    C = lambda name: con[:, CON[name][0]:CON[name][1]]
    Q1 = lambda l, name, i: par1[l][:, P1[name][0] + i:P1[name][0] + i + 1]
    Q2 = lambda l, name, i: par2[l][:, P2[name][0] + i:P2[name][0] + i + 1]
    eps = lambda i: con[:, CON["eps"][0] + i:CON["eps"][0] + i + 1]
    mod3 = [v3(m[:, :], 48) for m in modv]
    slots = v3(ring[:, :], RING)

    class Arena:

        def __init__(self, at=0, buf=None, size=22560):
            self.at, self.buf, self.size = at, buf or arena, size

        def take(self, cols, n=None):
            a = self.buf[:, self.at:self.at + cols]
            self.at += cols
            assert self.at <= self.size, self.at
            return v3(a, n) if n else a

    block = ctx.enter_context(nc.Block())
    loaded = [S(f"part_loaded_{i}") for i in range(RING)]
    used = S("parts_used")
    stream = {"put": 0, "got": 0, "skew": 0}

    phase = {"n": 0}

    def end_phase():
        phase["n"] += 1
        met = S("phase_met")
        goal = 4 * phase["n"]

        def meet(eng):
            eng.drain().then_inc(met.h, met.one())
            eng.wait_ge(met.h, goal)

        @block.tensor
        def _(pe):
            meet(pe)

        @block.scalar
        def _(act):
            meet(act)

        @block.vector
        def _(dve):
            meet(dve)

        @block.gpsimd
        def _(pool):
            meet(pool)
        for s in sems.values():
            if s not in loaded and s is not used:
                s.n = s.m

    def load_parts(sp, count):
        for _ in range(count):
            n = stream["put"]
            if n >= RING:
                sp.wait_ge(used.h, n - RING + 1)
            sp.dma_start(slots[:, n % RING, :], parts[n - stream["skew"], :, :]).then_inc(loaded[n % RING].h, 16)
            stream["put"] += 1

    def load_looped(sp, trips):
        n0 = stream["put"]
        with sp.Fori(0, trips) as i:
            for j in range(RING):
                n = n0 + j
                sp.wait_ge(used.h, i * RING + (n - RING + 1))
                sp.dma_start(slots[:, n % RING, :], parts[bass.ds(i * RING + (n - stream["skew"]), 1), :, :]
                             .rearrange("a p n -> p (a n)")).then_inc(loaded[n % RING].h, 16)
        stream["put"] += trips * RING

    def take_part(pe, n, i=None):
        goal = 16 * (n // RING + 1)
        pe.wait_ge(loaded[n % RING].h, goal if i is None else i * 16 + goal)
        return slots[:, n % RING, :]

    def norm(src, dst, cols, gain, shift, name):
        lo, hi = cols
        n = hi - lo
        streams = [s for s in range(2) if lo <= s * CTX < hi]
        a = Arena()
        sq, sd, rs = a.take(KT * n, KT), a.take(n), a.take(n)
        sq_done, ms_done, sd_done, rs_done, t_done, h_done = (
            S(f"norm_{x}") for x in ("squared", "mean", "root", "inverse", "scaled", "shifted"))

        @block.scalar
        def _(act):
            for k in range(KT):
                act.activation(sq[:, k, :], src[:, k, lo:hi], ACT.Square).then_inc(sq_done.h, sq_done.one())
            act.wait_ge(ms_done.h, ms_done.at(1))
            act.activation(sd, bank(0)[:, 0:n], ACT.Sqrt, bias=eps(EPS_RMS)).then_inc(sd_done.h, sd_done.one())
            if shift:
                for k in range(KT):
                    for j, s in enumerate(streams):
                        act.wait_ge(t_done.h, t_done.at(k * len(streams) + j + 1))
                        y = dst[:, k, s * CTX:(s + 1) * CTX]
                        act.activation(y, y, ACT.Identity, bias=shift(k, s)).then_inc(h_done.h, h_done.one())

        @block.tensor
        def _(pe):
            for k in range(KT):
                pe.wait_ge(sq_done.h, sq_done.at(k + 1))
                mm = pe.matmul(bank(0)[:, 0:n], C("mean_d"), sq[:, k, :], start=k == 0, stop=k == KT - 1)
            mm.then_inc(ms_done.h, ms_done.one())

        @block.vector
        def _(dve):
            dve.wait_ge(sd_done.h, sd_done.at(1))
            dve.reciprocal(rs, sd).then_inc(rs_done.h, rs_done.one())
            dve.wait_ge(rs_done.h, rs_done.at(1))
            for k in range(KT):
                for s in streams:
                    c = slice(s * CTX, (s + 1) * CTX)
                    r = slice(s * CTX - lo, (s + 1) * CTX - lo)
                    dve.scalar_tensor_tensor(dst[:, k, c], src[:, k, c], gain(k, s), rs[:, r],
                                                        ALU.mult, ALU.mult).then_inc(t_done.h, t_done.one())
        end_phase()

    class Modulation:

        def __init__(self, runs):
            self.runs = runs
            self.tiles = [(l, t) for l, lo, hi in runs for t in range(lo, hi)]
            self.n, self.first = len(self.tiles) // 2, stream["got"]
            self.copied, self.turned, self.next = S("mod_row_copied"), S("mod_turned"), 0
            self.rows = v3(mod_rows[:, :], 2)
            stream["got"] += self.n

        def turn(self, pe, m):
            for j in range(2):
                at = 256 + 2 * (2 * m + j)
                mm = pe.transpose(bank(7)[:, at:at + 2], self.rows[0:2, m % 2, j * P:(j + 1) * P],
                                  con[0:2, CON["ident"][0]:CON["ident"][0] + 2])
            return mm

        def half(self, pe):
            m, second = divmod(self.next, 2)
            self.next += 1
            if m >= self.n:
                return
            if not second and m:
                pe.wait_ge(self.copied.h, self.copied.at(m))
                self.turn(pe, m - 1)
            w = v3(take_part(pe, self.first + m), KT)
            c3 = v3(ct[:, :], KT)
            for k in range(4 * second, 4 * second + 4):
                mm = pe.matmul(bank(7)[0:2, 0:UNIT], c3[:, k, :], w[:, k, :], start=k == 0, stop=k == KT - 1)
            if second:
                mm.then_inc(used.h, used.one())

        def last(self, pe):
            pe.wait_ge(self.copied.h, self.copied.at(self.n))
            self.turn(pe, self.n - 1).then_inc(self.turned.h, self.turned.one())

        def copy(self, act, m):
            act.wait_ge(used.h, self.first + m + 1)
            act.activation(self.rows[0:2, m % 2, :], bank(7)[0:2, 0:UNIT], ACT.Copy)\
                .then_inc(self.copied.h, self.copied.one())

        def store(self, dve):
            biased, gained = S("mod_biased"), S("mod_gains")
            dve.wait_ge(self.turned.h, self.turned.at(1))
            at = 0
            for l, lo, hi in self.runs:
                acc = v3(bank(7)[:, 256 + 2 * at:256 + 2 * (at + hi - lo)], hi - lo)
                at += hi - lo
                b = par1[l][:, P1["mod_b"][0] + lo:P1["mod_b"][0] + hi]
                for s in range(2):
                    dve.tensor_tensor(mod3[l][:, lo:hi, s], acc[:, :, s], b, ALU.add).then_inc(biased.h, biased.one())
                dve.wait_ge(biased.h, biased.m)
                for i, name in enumerate(("norm1_g", "norm2_g")):
                    t = 24 * i + 8
                    if not lo <= t < hi:
                        continue
                    g = par1[l][:, P1[name][0]:P1[name][1]]
                    for s in range(2):
                        o = v3(scal[l][:, i * 16:(i + 1) * 16], 8)[:, :, s]
                        dve.scalar_tensor_tensor(o, mod3[l][:, t:t + 8, s], 1.0, g, ALU.add, ALU.mult)\
                            .then_inc(gained.h, gained.one())

    def modulation(runs):
        mod = Modulation(runs)

        @block.sync
        def _(sp):
            load_parts(sp, mod.n)

        @block.tensor
        def _(pe):
            for _ in range(2 * mod.n):
                mod.half(pe)
            mod.last(pe)

        @block.scalar
        def _(act):
            for m in range(mod.n):
                mod.copy(act, m)

        @block.vector
        def _(dve):
            tok, fin = S("shift_weight"), S("shift_rest")
            for l in range(DEPTH):
                c0 = scal[l][:, 32:42]
                mp = par1[l][:, P1["mu_prev"][0]:P1["mu_prev"][1]]
                mn = par1[l][:, P1["mu_next"][0]:P1["mu_next"][1]]
                ka = par1[l][:, P1["k_a"][0]:P1["k_a"][1]]
                dve.tensor_tensor(c0, mp, mn, ALU.add).then_inc(tok.h, tok.one())
                dve.wait_ge(tok.h, tok.m)
                dve.tensor_scalar(c0, c0, -1.0, 1.0, ALU.mult, ALU.add).then_inc(fin.h, fin.one())
                dve.tensor_scalar(scal[l][:, 42:44], ka, -1.0, 1.0, ALU.mult, ALU.add).then_inc(fin.h, fin.one())
            mod.store(dve)
        end_phase()

    gain1 = lambda l: lambda k, s: scal[l][:, 2 * k + s:2 * k + s + 1]
    gain2 = lambda l: lambda k, s: scal[l][:, 16 + 2 * k + s:16 + 2 * k + s + 1]
    modc = lambda l, t, s: mod3[l][:, t, s:s + 1]

    def project(tiles):
        ready, free = S("tile_ready"), {"act": S("tile_free_act"), "dve": S("tile_free_dve")}
        first = stream["got"]
        n_parts = tiles[-1]["part"] + 1
        closes = [t + 1 == len(tiles) or tiles[t + 1]["part"] != tiles[t]["part"] for t in range(len(tiles))]

        @block.sync
        def _(sp):
            load_parts(sp, n_parts)

        @block.tensor
        def _(pe):
            freed = {"act": 0, "dve": 0}
            part = -1
            for t, tile in enumerate(tiles):
                if tile["part"] != part:
                    part = tile["part"]
                    w = v3(take_part(pe, first + part), KT)
                if t >= 8:
                    o = tiles[t - 8]["owner"]
                    freed[o] += 1
                    pe.wait_ge(free[o].h, free[o].at(freed[o]))
                for k in range(KT):
                    if "tok" in tile:
                        tk, wd = tile["tok"], tile.get("wide", UNIT)
                        mm = pe.matmul(bank(t % 8)[:, 0:wd], tile["src"][:, k, tk * P:(tk + 1) * P],
                                       w[:, k, UNIT - wd:UNIT], start=k == 0, stop=k == KT - 1)
                    else:
                        lo, hi = tile["cols"]
                        mm = pe.matmul(bank(t % 8)[:, 0:hi - lo], w[:, k, tile["j"] * P:(tile["j"] + 1) * P],
                                       tile["src"][:, k, lo:hi], start=k == 0, stop=k == KT - 1)
                mm.then_inc((used if closes[t] else ready).h, (used if closes[t] else ready).one())
        stream["got"] += n_parts

        def tile_done(t):
            if closes[t]:
                return used.h, first + tiles[t]["part"] + 1
            return ready.h, ready.at(sum(not c for c in closes[:t + 1]))
        return tile_done, free

    def attention(units, q, k, v, scale, qwide, k_tile, v_col, at):
        per = qwide // P
        a = Arena(at)
        nk_max = max(len(u[4]) for u in units) * P
        pr = a.take(2 * nk_max, 2)
        ptr = [v3(x, nk_max // P) for x in (a.take(nk_max // P * qwide), a.take(nk_max // P * qwide))]
        st = a.take(2 * 4, 2)
        s_ok, m_ok, e_ok, n_ok, t_ok, c_ok, o_ok, w_ok, mm_ok, ri_ok = (S(f"attn_{x}") for x in (
            "scores", "max", "exp", "probs", "probs_turned", "turned_copied", "out", "out_copied",
            "rowmax", "inverse"))
        N = len(units)

        @block.tensor
        def _(pe):
            def scores(i):
                tile, half, qc, kcols, vt, bias, _ = units[i]
                hs = slice(half * DH, half * DH + DH)
                if i >= 2:
                    pe.wait_ge(e_ok.h, e_ok.at(i - 1))
                at = 0
                for lo, hi in kcols:
                    b = bias if at == 0 else None
                    mm = pe.matmul(bank(i % 2)[:, at:at + hi - lo], q[hs, tile, qc:qc + P], k[hs, k_tile(tile), lo:hi],
                                   start=True, stop=b is None)
                    if b is not None:
                        mm = pe.matmul(bank(i % 2)[:, at:at + hi - lo], C("ident"), b, start=False, stop=True)
                    at += hi - lo
                mm.then_inc(s_ok.h, s_ok.one())

            def turn(i):
                pe.wait_ge(n_ok.h, n_ok.at(i + 1))
                if i >= 2:
                    pe.wait_ge(c_ok.h, c_ok.at(i - 1))
                for t in range(len(units[i][4])):
                    mm = pe.transpose(bank(2 + i % 2)[:, t * P:(t + 1) * P], pr[:, i % 2, t * P:(t + 1) * P], C("ident"))
                mm.then_inc(t_ok.h, t_ok.one())

            def values(g):
                tile, half, _, _, vt, _, _ = units[g * per]
                hs = slice(half * DH, half * DH + DH)
                pe.wait_ge(c_ok.h, c_ok.at((g + 1) * per))
                if g >= 2:
                    pe.wait_ge(w_ok.h, w_ok.at(g - 1))
                for t, tv in enumerate(vt):
                    vc = v_col(tile, half)
                    mm = pe.matmul(bank(4 + g % 2)[hs, 0:qwide], v[:, tv, vc:vc + DH], ptr[g % 2][:, t, :],
                                   start=t == 0, stop=t == len(vt) - 1)
                mm.then_inc(o_ok.h, o_ok.one())

            for i in range(N + 2):
                if i < N:
                    scores(i)
                if 1 <= i <= N:
                    turn(i - 1)
                if i >= 2 and (i - 2) % per == per - 1:
                    values((i - 2) // per)

        @block.vector
        def _(dve):
            def top(i):
                nk = len(units[i][4]) * P
                dve.wait_ge(s_ok.h, s_ok.at(i + 1))
                if i >= 2:
                    dve.wait_ge(e_ok.h, e_ok.at(i - 1))
                dve.tensor_reduce(st[:, i % 2, 0:1], bank(i % 2)[:, 0:nk], AX.X, ALU.max).then_inc(mm_ok.h, mm_ok.one())
                dve.wait_ge(mm_ok.h, mm_ok.at(i + 1))
                dve.tensor_scalar(st[:, i % 2, 1:2], st[:, i % 2, 0:1], -scale, None, ALU.mult).then_inc(m_ok.h, m_ok.one())

            def normalise(i):
                nk = len(units[i][4]) * P
                dve.wait_ge(e_ok.h, e_ok.at(i + 1))
                dve.reciprocal(st[:, i % 2, 3:4], st[:, i % 2, 2:3]).then_inc(ri_ok.h, ri_ok.one())
                dve.wait_ge(ri_ok.h, ri_ok.at(i + 1))
                dve.tensor_scalar(pr[:, i % 2, 0:nk], pr[:, i % 2, 0:nk], st[:, i % 2, 3:4], None, ALU.mult).then_inc(n_ok.h, n_ok.one())

            def copy_out(g):
                tile, half, _, _, _, _, oc = units[g * per]
                hs = slice(half * DH, half * DH + DH)
                dve.wait_ge(o_ok.h, o_ok.at(g + 1))
                dve.tensor_copy(mixT[hs, tile, oc:oc + qwide], bank(4 + g % 2)[hs, 0:qwide]).then_inc(w_ok.h, w_ok.one())

            for i in range(N + 4):
                if i < N:
                    top(i)
                if 1 <= i <= N:
                    normalise(i - 1)
                if i >= 3 and (i - 3) % per == per - 1 and (i - 3) // per < N // per:
                    copy_out((i - 3) // per)

        @block.scalar
        def _(act):
            def exp(i):
                nk = len(units[i][4]) * P
                act.wait_ge(m_ok.h, m_ok.at(i + 1))
                if i >= 2:
                    act.wait_ge(t_ok.h, t_ok.at(i - 1))
                    act.wait_ge(ri_ok.h, ri_ok.at(i - 1))
                act.activation(pr[:, i % 2, 0:nk], bank(i % 2)[:, 0:nk], ACT.Exp, bias=st[:, i % 2, 1:2],
                                        scale=scale, accum_out=st[:, i % 2, 2:3]).then_inc(e_ok.h, e_ok.one())

            def copy_turned(i):
                nt = len(units[i][4])
                g, j = i // per, i % per
                act.wait_ge(t_ok.h, t_ok.at(i + 1))
                if g >= 2:
                    act.wait_ge(o_ok.h, o_ok.at(g - 1))
                act.activation(ptr[g % 2][:, 0:nt, j * P:(j + 1) * P], v3(bank(2 + i % 2)[:, 0:nt * P], nt),
                                        ACT.Copy).then_inc(c_ok.h, c_ok.one())

            for i in range(N + 1):
                if i < N:
                    exp(i)
                if i >= 1:
                    copy_turned(i - 1)
        end_phase()

    def out_project(src, cols, gate, n_parts=4):
        tiles = [dict(part=p, j=j, cols=cols, src=src, owner="dve") for p in range(n_parts) for j in range(2)]
        tile_done, free = project(tiles)
        lo, hi = cols

        @block.vector
        def _(dve):
            for t in range(len(tiles)):
                dve.wait_ge(*tile_done(t))
                for s in range(2):
                    a, b = s * CTX, (s + 1) * CTX
                    if not lo <= a < hi:
                        continue
                    ps = bank(t % 8)[:, a - lo:b - lo]
                    if gate:
                        ins = dve.scalar_tensor_tensor(xT[:, t, a:b], ps, gate(t, s), xT[:, t, a:b], ALU.mult, ALU.add)
                    else:
                        ins = dve.tensor_tensor(xT[:, t, a:b], ps, xT[:, t, a:b], ALU.add)
                ins.then_inc(free["dve"].h, free["dve"].one())
        end_phase()

    def feed_forward(kind, groups, n_units, src, c0, residual, taps=None, at=0):
        a = Arena(at)
        sg, hid = a.take(2 * 512, 2), a.take(2 * 512, 2)
        cen = a.take(2 * 1024, 2) if kind == "conv" else None
        si, ac, ce, tq = (S(f"ff_{x}") for x in ("silu", "hidden", "centre_tap", "side_taps"))
        N = groups * n_units
        B = stream["got"]
        y = lambda m: bank(4 + m // 2)[:, (m % 2) * 256:(m % 2 + 1) * 256]
        gate_bank, up_bank = (lambda u: bank(u % 2)), (lambda u: bank(2 + u % 2))
        looped = kind != "conv"

        gate_of = lambda U: B + 3 * U if U else B + 1
        up_of = lambda U: B + 3 * U + 1 if U else B + 2

        def over_units(eng, body, lead):
            for g in range(groups):
                if not looped:
                    for u in range(n_units):
                        body(g * n_units + u, 0, 1)
                    continue
                start = 0 if lead else 1
                if not lead:
                    body(g * n_units, 0, 1)
                trips = (n_units - 1) // 2
                with eng.Fori(0, trips) as i:
                    for j in range(2):
                        body(g * n_units + start + j, i, trips)
                for u in range(start + 2 * trips, n_units):
                    body(g * n_units + u, 0, 1)

        @block.sync
        def _(sp):
            load_parts(sp, 2)
            for g in range(groups):
                if looped:
                    trips = (n_units - 1) // 2
                    load_looped(sp, trips)
                    load_parts(sp, 3 * (n_units - 2 * trips) - (2 if g == groups - 1 else 0))
                else:
                    load_parts(sp, 3 * n_units - 2)

        @block.tensor
        def _(pe):
            def products(U, n, i, times):
                for which, bk in enumerate((gate_bank(U), up_bank(U))):
                    w = v3(take_part(pe, n + which, i), KT)
                    if which == 0:
                        pe.wait_ge(ac.h, ac.at(i * 2 + (U + 1)))
                    for j in range(2):
                        for k in range(KT):
                            mm = pe.matmul(bk[:, j * 256:(j + 1) * 256], w[:, k, j * P:(j + 1) * P],
                                           src[:, k, c0:c0 + 256], start=k == 0, stop=k == KT - 1)
                    mm.then_inc(used.h, used.one(times))

            def down(U, n, i, times):
                w = v3(take_part(pe, n, i), 2)
                pe.wait_ge(ac.h, ac.at(i * 2 + (U + 3)))
                for j in range(2):
                    for m in range(KT):
                        mm = pe.matmul(y(m), w[:, j, m * P:(m + 1) * P], hid[:, U % 2, j * 256:(j + 1) * 256],
                                       start=False, stop=False, skip_group_check=True)
                mm.then_inc(used.h, used.one(times))

            pe.wait_ge(ac.h, ac.at(1))
            for b in range(4):
                pe.matmul(bank(4 + b), C("ident"), hid[:, 0, :], start=True, stop=False, skip_group_check=True)
            products(0, B, 0, 1)

            def body(U, i, times):
                n = B + 2 + 3 * U
                if U < N - 1:
                    products(U + 1, n, i, times)
                    down(U, n + 2, i, times)
                else:
                    down(U, n, i, times)
            over_units(pe, body, 1)

        @block.scalar
        def _(act):
            def body(U, i, times):
                since = lambda v: i * 6 + v if times > 1 else v
                if kind == "conv":
                    act.wait_ge(used.h, since(gate_of(U)))
                    act.wait_ge(ac.h, ac.at(U + 1))
                    for h in range(2):
                        if h:
                            act.wait_ge(used.h, since(up_of(U)))
                        for j in range(2):
                            bk = (gate_bank(U), up_bank(U))[h]
                            act.activation(cen[:, U % 2, (2 * h + j) * 256:(2 * h + j + 1) * 256],
                                                  bk[:, j * 256:(j + 1) * 256], ACT.Copy,
                                                  scale=taps(1, 22 * h + 2 * U + j)).then_inc(ce.h, ce.one())
                    act.wait_ge(tq.h, tq.at(8 * U + 4))
                    act.activation(sg[:, U % 2, :], cen[:, U % 2, 0:512], ACT.Silu).then_inc(si.h, si.one())
                    return
                act.wait_ge(used.h, since(gate_of(U)))
                act.wait_ge(ac.h, ac.at(i * 2 + (U + 1)))
                act.activation(sg[:, U % 2, :], gate_bank(U), ACT.Silu).then_inc(si.h, si.one(times))
            over_units(act, body, 0)

        @block.vector
        def _(dve):
            for j in range(2):
                dve.memset(hid[:, j, :], 0.0).then_inc(ac.h, ac.one())

            def body(U, i, times):
                since = lambda v: i * 6 + v if times > 1 else v
                if kind == "conv":
                    dve.wait_ge(used.h, since(up_of(U)))
                    for h in range(2):
                        dve.wait_ge(ce.h, ce.at(4 * U + 2 * h + 2))
                        bk = (gate_bank(U), up_bank(U))[h]
                        for side in range(2):
                            if side:
                                dve.wait_ge(tq.h, tq.at(8 * U + 4 * h + 2))
                            for j in range(2):
                                c = cen[:, U % 2, (2 * h + j) * 256:(2 * h + j + 1) * 256]
                                p = bk[:, j * 256:(j + 1) * 256]
                                o, q = (c[:, 1:256], p[:, 0:255]) if side == 0 else (c[:, 0:255], p[:, 1:256])
                                dve.scalar_tensor_tensor(o, q, taps(2 * side, 22 * h + 2 * U + j), o,
                                                                ALU.mult, ALU.add).then_inc(tq.h, tq.one())
                    dve.wait_ge(si.h, si.at(U + 1))
                    dve.wait_ge(tq.h, tq.at(8 * U + 8))
                    dve.tensor_tensor(hid[:, U % 2, :], cen[:, U % 2, 512:1024], sg[:, U % 2, :], ALU.mult).then_inc(ac.h, ac.one())
                    return
                dve.wait_ge(used.h, since(up_of(U)))
                dve.wait_ge(si.h, si.at(i * 2 + (U + 1)))
                dve.tensor_tensor(hid[:, U % 2, :], up_bank(U), sg[:, U % 2, :], ALU.mult).then_inc(ac.h, ac.one(times))
            over_units(dve, body, 0)
            dve.wait_ge(used.h, B + 3 * N)
            for m in range(KT):
                residual(dve, m, y(m))
        stream["got"] += 3 * N
        end_phase()

    def recurrence(l, us, at):
        big, hb = Arena(at), Arena(0, h_buf, KT * T)
        zr = big.take(4 * T * 2).rearrange("p (q c w t) -> p q c w t", q=4, c=NCH, w=2)
        bt, kt = hb.take(4 * T, 4), hb.take(4 * T, 4)
        gg, bon, pc = big.take(4 * T, 4), big.take(2 * T, 2), big.take(4 * NCH, 4)
        tmp_at = big.at
        lora, g2w, tw, sgd = big.take(512, 2), big.take(512, 2), big.take(T), big.take(T)
        lw, av, kk, ci, ce, ex, kd = (big.take(2 * T, 2) for _ in range(7))
        r, k, v = us[:, 0:2, :], us[:, 2:4, :], us[:, 4:6, :]
        by_chunk = lambda a: a.rearrange("p (c t) -> p c t", t=CH)
        chunks_of = lambda a: a.rearrange("p h (c t) -> p (h c) t", t=CH)
        lo_in = S("lora_loaded")

        @block.scalar
        def _(sp):
            sp.dma_start(lora, lora_in[l, :, :].rearrange("p (d n) -> p d n", d=2)).then_inc(lo_in.h, 16)
            sp.dma_start(g2w, gate2_in[l, :, :].rearrange("p (d n) -> p d n", d=2)).then_inc(lo_in.h, 16)

        an = ["sq0", "sq1", "root0", "root1"]
        vn = ["kk0", "kk1", "inv0", "inv1", "kkn0", "kkn1"]
        pn = ["kksum"]
        for d in range(2):
            an += [f"{x}{d}" for x in ("tanh", "sgd", "sw0", "sw1", "a0", "a1", "g", "ex", "ep", "en", "pc")]
            pn += [f"{x}{d}" for x in ("w", "g", "bonus")]
            vn += [f"{x}{d}" for x in ("lw", "scan0", "scan1", "excl", "incl", "z0", "z1", "r0", "r1", "b1", "b",
                                       "ka0", "ka1", "kd", "k", "rk0", "rk1", "bv", "bg")]
            vn += ["badd1"] * d
        A_, V_, P_ = Steps(S("rw_act"), an), Steps(S("rw_dve"), vn), Steps(S("rw_pe"), pn)

        @block.tensor
        def _(pe):
            pe.wait_ge(A_.h, A_.at("sq1"))
            for hp in range(2):
                mm = pe.matmul(bank(hp), C("head_sum"), ex[:, hp, :], start=True, stop=True)
            mm.then_inc(P_.h, P_.one("kksum"))
            pe.wait_ge(lo_in.h, 32 * (l + 1))
            for d in range(2):
                pe.wait_ge(A_.h, A_.at(f"tanh{d}"))
                for hp in range(2):
                    c = slice(hp * P, (hp + 1) * P)
                    pe.matmul(bank(2 + hp), lora[0:64, d, c], tw[0:64, :], start=True, stop=True)
                    mm = pe.matmul(bank(4 + hp), lora[64:128, d, c], us[64:128, 6 + 2 * d, :], start=True, stop=True)
                mm.then_inc(P_.h, P_.one(f"w{d}"))
                pe.wait_ge(A_.h, A_.at(f"sgd{d}"))
                for hp in range(2):
                    mm = pe.matmul(bank(6 + hp), g2w[:, d, hp * P:(hp + 1) * P], sgd, start=True, stop=True)
                mm.then_inc(P_.h, P_.one(f"g{d}"))
                pe.wait_ge(V_.h, V_.at(f"rk1{d}"))
                for hp in range(2):
                    mm = pe.matmul(bank(hp), C("head_sum"), av[:, hp, :], start=True, stop=True)
                mm.then_inc(P_.h, P_.one(f"bonus{d}"))

        @block.scalar
        def _(act):
            for hp in range(2):
                act.wait_ge(V_.h, V_.at(f"kk{hp}"))
                act.activation(ex[:, hp, :], kk[:, hp, :], ACT.Square).then_inc(A_.h, A_.one(f"sq{hp}"))
            act.wait_ge(P_.h, P_.at("kksum"))
            for hp in range(2):
                act.activation(ce[:, hp, :], bank(hp), ACT.Sqrt, bias=eps(EPS_KK)).then_inc(A_.h, A_.one(f"root{hp}"))
            for d in range(2):
                if d:
                    act.wait_ge(P_.h, P_.at("g0"))
                    act.wait_ge(V_.h, V_.at("bg0"))
                act.activation(tw[0:64, :], us[0:64, 6 + 2 * d, :], ACT.Tanh).then_inc(A_.h, A_.one(f"tanh{d}"))
                act.activation(sgd, us[:, 7 + 2 * d, :], ACT.Sigmoid).then_inc(A_.h, A_.one(f"sgd{d}"))
                act.wait_ge(P_.h, P_.at(f"w{d}"))
                for hp in range(2):
                    act.activation(lw[:, hp, :], bank(2 + hp), ACT.Sigmoid,
                                                         bias=Q1(l, "w0", 2 * d + hp)).then_inc(A_.h, A_.one(f"sw{hp}{d}"))
                for hp in range(2):
                    act.activation(av[:, hp, :], bank(4 + hp), ACT.Sigmoid,
                                                        bias=Q1(l, "a0", 2 * d + hp)).then_inc(A_.h, A_.one(f"a{hp}{d}"))
                act.wait_ge(P_.h, P_.at(f"g{d}"))
                act.activation(gg[:, 2 * d:2 * d + 2, :], v3(banks[:, 6 * 512:8 * 512], 2), ACT.Copy).then_inc(A_.h, A_.one(f"g{d}"))
                act.wait_ge(V_.h, V_.at(f"incl{d}"))
                act.activation(ex, ce, ACT.Exp).then_inc(A_.h, A_.one(f"ex{d}"))
                act.wait_ge(A_.h, A_.at(f"ex{d}"))
                act.activation(ce, ci, ACT.Exp).then_inc(A_.h, A_.one(f"ep{d}"))
                act.wait_ge(V_.h, V_.at(f"z1{d}"))
                act.activation(ex, ci, ACT.Exp, scale=-1.0).then_inc(A_.h, A_.one(f"en{d}"))
                edge = CH - 1 if d == 0 else 0
                act.activation(pc[:, 2 * d:2 * d + 2, :],
                                                 ci.rearrange("p h (c t) -> p h c t", t=CH)[:, :, :, edge], ACT.Exp).then_inc(A_.h, A_.one(f"pc{d}"))

        @block.vector
        def _(dve):
            me = V_.s
            for hp in range(2):
                dve.tensor_scalar(kk[:, hp, :], k[:, hp, :], Q1(l, "k_k", hp), None, ALU.mult).then_inc(V_.h, V_.one(f"kk{hp}"))
            for hp in range(2):
                dve.wait_ge(A_.h, A_.at(f"root{hp}"))
                dve.reciprocal(ce[:, hp, :], ce[:, hp, :]).then_inc(V_.h, V_.one(f"inv{hp}"))
            dve.wait_ge(me.h, me.m)
            for hp in range(2):
                dve.tensor_tensor(kk[:, hp, :], kk[:, hp, :], ce[:, hp, :], ALU.mult).then_inc(V_.h, V_.one(f"kkn{hp}"))
            for d in range(2):
                dve.wait_ge(A_.h, A_.at(f"sw1{d}"))
                dve.tensor_scalar(lw, lw, -float(np.exp(-0.5)), None, ALU.mult).then_inc(V_.h, V_.one(f"lw{d}"))
                dve.wait_ge(me.h, me.m)
                for hp in range(2):
                    dve.tensor_tensor_scan(ci[:, hp, :], C("not_first"), lw[:, hp, :], 0.0,
                                                                   ALU.mult, ALU.add).then_inc(V_.h, V_.one(f"scan{hp}{d}"))
                dve.wait_ge(me.h, me.m)
                if d == 0:
                    dve.tensor_tensor(ce, ci, lw, ALU.subtract).then_inc(V_.h, V_.one("excl0"))
                    dve.tensor_copy(kd[:, 0, 0:1], ci[:, 0, 0:1]).then_inc(V_.h, V_.one("incl0"))
                else:
                    tot = chunks_of(ci)[:, :, CH - 1:CH].broadcast_to((P, 2 * NCH, CH))
                    dve.tensor_tensor(chunks_of(ce), tot, chunks_of(ci), ALU.subtract).then_inc(V_.h, V_.one("excl1"))
                    dve.wait_ge(me.h, me.m)
                    dve.tensor_tensor(ci, ce, lw, ALU.add).then_inc(V_.h, V_.one("incl1"))
                dve.wait_ge(A_.h, A_.at(f"ex{d}"))
                dve.wait_ge(me.h, me.m)
                for hp in range(2):
                    dve.scalar_tensor_tensor(zr[:, 2 * d + hp, :, 0, :], by_chunk(ex[:, hp, :]), -1.0,
                                                                  by_chunk(kk[:, hp, :]), ALU.mult, ALU.mult).then_inc(V_.h, V_.one(f"z{hp}{d}"))
                dve.wait_ge(A_.h, A_.at(f"ep{d}"))
                for hp in range(2):
                    dve.tensor_tensor(zr[:, 2 * d + hp, :, 1, :], by_chunk(ce[:, hp, :]),
                                                           by_chunk(r[:, hp, :]), ALU.mult).then_inc(V_.h, V_.one(f"r{hp}{d}"))
                dve.wait_ge(A_.h, A_.at(f"a1{d}"))
                dve.tensor_tensor(lw, kk, av, ALU.mult).then_inc(V_.h, V_.one(f"b1{d}"))
                dve.wait_ge(me.h, me.m)
                dve.wait_ge(A_.h, A_.at(f"en{d}"))
                dve.tensor_tensor(bt[:, 2 * d:2 * d + 2, :], lw, ex, ALU.mult).then_inc(V_.h, V_.one(f"b{d}"))
                for hp in range(2):
                    dve.tensor_scalar(kd[:, hp, :], av[:, hp, :], Q1(l, "k_a", hp),
                                                            scal[l][:, 42 + hp:43 + hp], ALU.mult, ALU.add).then_inc(V_.h, V_.one(f"ka{hp}{d}"))
                dve.wait_ge(me.h, me.m)
                dve.tensor_tensor(kd, kd, k, ALU.mult).then_inc(V_.h, V_.one(f"kd{d}"))
                dve.wait_ge(me.h, me.m)
                dve.tensor_tensor(kt[:, 2 * d:2 * d + 2, :], kd, ex, ALU.mult).then_inc(V_.h, V_.one(f"k{d}"))
                for hp in range(2):
                    dve.scalar_tensor_tensor(av[:, hp, :], r[:, hp, :], Q1(l, "r_k", hp),
                                                                   kd[:, hp, :], ALU.mult, ALU.mult).then_inc(V_.h, V_.one(f"rk{hp}{d}"))
                dve.wait_ge(P_.h, P_.at(f"bonus{d}"))
                dve.tensor_tensor(av, v3(banks[:, 0:1024], 2), v, ALU.mult).then_inc(V_.h, V_.one(f"bv{d}"))
                dve.wait_ge(me.h, me.m)
                dve.wait_ge(A_.h, A_.at(f"pc{d}"))
                if d == 0:
                    dve.tensor_tensor(bon, av, gg[:, 0:2, :], ALU.mult).then_inc(V_.h, V_.one("bg0"))
                else:
                    dve.tensor_tensor(av, av, gg[:, 2:4, :], ALU.mult).then_inc(V_.h, V_.one("bg1"))
                    dve.wait_ge(me.h, me.m)
                    dve.tensor_tensor(bon, bon, av, ALU.add).then_inc(V_.h, V_.one("badd1"))
        end_phase()

        gb = Arena(tmp_at)
        lo = v3(us[:, 6:10, :].rearrange("p a b -> p (a b)"), 4)
        take = lambda: gb.take(512, 8)
        DT, DD, LL, MB, AK, MK, BS, KS, VS, D2, D2T, D4, D4T, E1, E2, DI, N1, GG_, TI = (take() for _ in range(19))
        X = gb.take(512, 2)
        lo8 = [v3(lo[:, i, :], 8) for i in range(4)]
        NTb, N2, INT_ = lo8[0], lo8[1], lo8[2]
        RH, UU = v3(lo[:, 3, 0:256], 4), v3(lo[:, 3, 256:512], 4)
        D8, E3, E4 = D2T, E1, E2
        b8 = lambda i: v3(bank(i), 8)
        b4 = lambda i: v3(bank(i)[:, 0:256], 4)
        eye = C("eye64").rearrange("p (o t) -> p o t", o=1).broadcast_to((P, 8, CH))
        Y = us
        pn, vn, an = [], ["x0"], []
        for g in range(NCH // 2):
            pn += [f"{x}_{g}" for x in ("gram", "p1", "p2", "p3", "p4", "p5", "p6", "p7", "p8")]
            vn += [f"{x}_{g}" for x in ("dt0", "mb0", "dt1", "mb1", "ak0", "mk0", "ak1", "mk1", "d", "l", "e1", "d2", "d4", "e2",
                                        "e3", "e4", "nt", "int", "n2", "g")]
            an += [f"{x}_{g}" for x in ("bs", "ks", "d2t", "d4t", "vs", "d8", "di", "n", "ti")]
            for j in range(2):
                pn += [f"{x}_{g}{j}" for x in ("rhs", "u", "dx", "y")]
                vn += [f"{x}_{g}{j}" for x in ("u", "xa", "xb")]
                an += [f"{x}_{g}{j}" for x in ("rhs", "y0", "y1")]
        P_, V_, A_ = Steps(S("rc_pe"), pn), Steps(S("rc_dve"), vn), Steps(S("rc_act"), an)
        hs = [slice(0, 64), slice(64, 128)]
        mod = Modulation([(0, 16, 48), (1, 0, 48)]) if l == 0 else None
        fill = dict(gram=2, p1=2, p2=2, p3=2, p4=2, p5=1, p6=1, p7=1, p8=1, rhs0=1, u0=1, y0=1, rhs1=1, u1=1, y1=1)
        whole = {}
        h_at = 0
        for g in range(NCH // 2):
            for name, n in fill.items():
                whole[g, name] = [h // 2 for h in range(h_at, h_at + n) if h % 2]
                h_at += n

        def fill_pe(pe, name):
            if mod:
                for _ in range(fill[name]):
                    mod.half(pe)

        def fill_act(act, g, name):
            if mod:
                for m in whole[g, name]:
                    mod.copy(act, m)

        if mod:
            assert h_at == 2 * mod.n

            @block.sync
            def _(sp):
                load_parts(sp, mod.n)

        @block.tensor
        def _(pe):
            def products(out, left, right):
                for i in range(8):
                    for h in hs:
                        mm = pe.matmul(out[h, i, :], left[h, i, :], right[h, i, :], start=True, stop=True)
                return mm

            for g in range(NCH // 2):
                if g:
                    pe.wait_ge(A_.h, A_.at(f"y1_{g - 1}1"))
                    pe.wait_ge(V_.h, V_.at(f"xb_{g - 1}1"))
                for j in range(2):
                    for q in range(4):
                        c = CHUNKS[q // 2][2 * g + j]
                        cs = slice(c * CH, (c + 1) * CH)
                        i = 4 * j + q
                        for h in hs:
                            z_r = zr[h, q, c, :, :].rearrange("p w t -> p (w t)")
                            pe.matmul(bank(j)[h, q * 128:(q + 1) * 128], bt[h, q, cs], z_r, start=True, stop=True)
                            pe.matmul(bank(2 + j)[h, q * 128:(q + 1) * 128], kt[h, q, cs], z_r, start=True, stop=True)
                            pe.matmul(b8(4)[h, i, :], zr[h, q, c, 0, :], bt[h, q, cs], start=True, stop=True)
                            pe.matmul(b8(5)[h, i, :], bt[h, q, cs], eye[h, 0, :], start=True, stop=True)
                            mm = pe.matmul(b8(6)[h, i, :], kt[h, q, cs], eye[h, 0, :], start=True, stop=True)
                mm.then_inc(P_.h, P_.one(f"gram_{g}"))
                fill_pe(pe, "gram")
                pe.wait_ge(V_.h, V_.at(f"e1_{g}"))
                products(b8(0), DT, DD)
                products(b8(1), DD, DT).then_inc(P_.h, P_.one(f"p1_{g}"))
                fill_pe(pe, "p1")
                pe.wait_ge(V_.h, V_.at(f"d2_{g}"))
                pe.wait_ge(A_.h, A_.at(f"d2t_{g}"))
                products(b8(2), D2T, D2)
                products(b8(3), D2, D2T)
                for i in range(8):
                    c = CHUNKS[i % 4 // 2][2 * g + i // 4]
                    for h in hs:
                        pe.matmul(b8(5)[h, i, :], us[h, 4 + i % 2, c * CH:(c + 1) * CH], eye[h, 0, :], start=True, stop=True)
                products(b8(4), D2, E1).then_inc(P_.h, P_.one(f"p2_{g}"))
                fill_pe(pe, "p2")
                pe.wait_ge(V_.h, V_.at(f"e2_{g}"))
                pe.wait_ge(A_.h, A_.at(f"d4t_{g}"))
                products(b8(0), D4T, D4)
                products(b8(1), D4, E2).then_inc(P_.h, P_.one(f"p3_{g}"))
                fill_pe(pe, "p3")
                pe.wait_ge(V_.h, V_.at(f"e3_{g}"))
                pe.wait_ge(A_.h, A_.at(f"d8_{g}"))
                products(b8(2), D8, E3).then_inc(P_.h, P_.one(f"p4_{g}"))
                fill_pe(pe, "p4")
                pe.wait_ge(V_.h, V_.at(f"e4_{g}"))
                products(b8(3), E4, eye)
                products(b8(0), LL, E4)
                products(b8(1), E4, LL).then_inc(P_.h, P_.one(f"p5_{g}"))
                fill_pe(pe, "p5")
                pe.wait_ge(V_.h, V_.at(f"int_{g}"))
                pe.wait_ge(A_.h, A_.at(f"n_{g}"))
                products(b8(2), NTb, N1).then_inc(P_.h, P_.one(f"p6_{g}"))
                fill_pe(pe, "p6")
                pe.wait_ge(V_.h, V_.at(f"n2_{g}"))
                products(b8(3), N2, INT_).then_inc(P_.h, P_.one(f"p7_{g}"))
                fill_pe(pe, "p7")
                pe.wait_ge(V_.h, V_.at(f"g_{g}"))
                products(b8(4), DI, GG_).then_inc(P_.h, P_.one(f"p8_{g}"))
                fill_pe(pe, "p8")
                for j in range(2):
                    old = v3(X[:, j, :], 4)
                    if j or g:
                        pe.wait_ge(V_.h, V_.at(f"xb_{g if j else g - 1}{1 - j}"))
                    else:
                        pe.wait_ge(V_.h, V_.at("x0"))
                    at_c = [CHUNKS[q // 2][2 * g + j] for q in range(4)]
                    for q in range(4):
                        i = 4 * j + q
                        for h in hs:
                            pe.matmul(b4(5)[h, q, :], zr[h, q, at_c[q], 0, :], old[h, q, :], start=True, stop=False)
                            mm = pe.matmul(b4(5)[h, q, :], AK[h, i, :], VS[h, i, :], start=False, stop=True)
                    mm.then_inc(P_.h, P_.one(f"rhs_{g}{j}"))
                    fill_pe(pe, f"rhs{j}")
                    pe.wait_ge(A_.h, A_.at(f"ti_{g}"))
                    pe.wait_ge(A_.h, A_.at(f"rhs_{g}{j}"))
                    for q in range(4):
                        for h in hs:
                            mm = pe.matmul(b4(6)[h, q, :], TI[h, 4 * j + q, :], RH[h, q, :], start=True, stop=True)
                    mm.then_inc(P_.h, P_.one(f"u_{g}{j}"))
                    fill_pe(pe, f"u{j}")
                    pe.wait_ge(V_.h, V_.at(f"u_{g}{j}"))
                    for q in range(4):
                        i = 4 * j + q
                        for h in hs:
                            pe.matmul(b4(4)[h, q, :], BS[h, i, :], UU[h, q, :], start=True, stop=False)
                            mm = pe.matmul(b4(4)[h, q, :], KS[h, i, :], VS[h, i, :], start=False, stop=True)
                    mm.then_inc(P_.h, P_.one(f"dx_{g}{j}"))
                    for q in range(4):
                        i = 4 * j + q
                        for h in hs:
                            pe.matmul(b4(j)[h, q, :], old[h, q, :], zr[h, q, at_c[q], 1, :], start=True, stop=False)
                            pe.matmul(b4(j)[h, q, :], UU[h, q, :], MB[h, i, :], start=False, stop=False)
                            mm = pe.matmul(b4(j)[h, q, :], VS[h, i, :], MK[h, i, :], start=False, stop=True)
                    mm.then_inc(P_.h, P_.one(f"y_{g}{j}"))
                    fill_pe(pe, f"y{j}")
            if mod:
                mod.last(pe)

        @block.scalar
        def _(act):
            for g in range(NCH // 2):
                act.wait_ge(P_.h, P_.at(f"gram_{g}"))
                for name, b, o in (("bs", 5, BS), ("ks", 6, KS)):
                    act.activation(o, b8(b), ACT.Copy).then_inc(A_.h, A_.one(f"{name}_{g}"))
                fill_act(act, g, "gram")
                stages = ["p1", "p2", "p3", "p4", "p5", "p6", "p7", "p8"]
                for name, after, b, o in (("d2t", "p1", 1, D2T), ("d4t", "p2", 3, D4T), ("vs", "p2", 5, VS), ("d8", "p3", 0, D8),
                                          ("di", "p5", 3, DI), ("n", "p5", 1, N1), ("ti", "p8", 4, TI)):
                    while stages[0] != after:
                        fill_act(act, g, stages.pop(0))
                    act.wait_ge(P_.h, P_.at(f"{after}_{g}"))
                    act.activation(o, b8(b), ACT.Copy).then_inc(A_.h, A_.one(f"{name}_{g}"))
                for name in stages:
                    fill_act(act, g, name)
                for j in range(2):
                    act.wait_ge(P_.h, P_.at(f"rhs_{g}{j}"))
                    act.activation(RH, b4(5), ACT.Copy).then_inc(A_.h, A_.one(f"rhs_{g}{j}"))
                    fill_act(act, g, f"rhs{j}")
                    fill_act(act, g, f"u{j}")
                    act.wait_ge(P_.h, P_.at(f"y_{g}{j}"))
                    for d in range(2):
                        c = CHUNKS[d][2 * g + j]
                        act.activation(Y[:, 2 * d:2 * d + 2, c * CH:(c + 1) * CH],
                                                               b4(j)[:, 2 * d:2 * d + 2, :], ACT.Copy).then_inc(A_.h, A_.one(f"y{d}_{g}{j}"))
                    fill_act(act, g, f"y{j}")

        @block.vector
        def _(dve):
            dve.memset(X[:, :, :], 0.0).then_inc(V_.h, V_.one("x0"))
            mzr = C("mask_zr").rearrange("p (q w t) -> p q w t", q=4, w=2)
            mdt = v3(C("mask_dt"), 4)
            zr_of = lambda b: bank(b).rearrange("p (q w t) -> p q w t", q=4, w=2)
            mult = lambda o, a, b: dve.tensor_tensor(o, a, b, ALU.mult)
            add = lambda o, a, b: dve.tensor_tensor(o, a, b, ALU.add)
            for g in range(NCH // 2):
                dve.wait_ge(P_.h, P_.at(f"gram_{g}"))
                for j in range(2):
                    s = slice(4 * j, 4 * j + 4)
                    mult(DT[:, s, :], zr_of(j)[:, :, 0, :], mdt).then_inc(V_.h, V_.one(f"dt{j}_{g}"))
                    mult(MB[:, s, :], zr_of(j)[:, :, 1, :], mzr[:, :, 1, :]).then_inc(V_.h, V_.one(f"mb{j}_{g}"))
                for j in range(2):
                    s = slice(4 * j, 4 * j + 4)
                    mult(AK[:, s, :], zr_of(2 + j)[:, :, 0, :], mzr[:, :, 0, :]).then_inc(V_.h, V_.one(f"ak{j}_{g}"))
                    mult(MK[:, s, :], zr_of(2 + j)[:, :, 1, :], mzr[:, :, 1, :]).then_inc(V_.h, V_.one(f"mk{j}_{g}"))
                both = lambda a: a.rearrange("p (j q) t -> p j (q t)", j=2)
                for name, o in (("d", DD), ("l", LL)):
                    m = C(f"mask_{name}").rearrange("p (j n) -> p j n", j=1).broadcast_to((P, 2, 4 * CH))
                    mult(both(o), both(b8(4)), m).then_inc(V_.h, V_.one(f"{name}_{g}"))
                dve.wait_ge(V_.s.h, V_.s.m)
                add(E1, DT, eye).then_inc(V_.h, V_.one(f"e1_{g}"))
                dve.wait_ge(P_.h, P_.at(f"p1_{g}"))
                dve.tensor_copy(D2, b8(0)).then_inc(V_.h, V_.one(f"d2_{g}"))
                dve.wait_ge(P_.h, P_.at(f"p2_{g}"))
                dve.tensor_copy(D4, b8(2)).then_inc(V_.h, V_.one(f"d4_{g}"))
                add(E2, b8(4), E1).then_inc(V_.h, V_.one(f"e2_{g}"))
                dve.wait_ge(P_.h, P_.at(f"p3_{g}"))
                dve.wait_ge(V_.s.h, V_.s.m)
                add(E3, b8(1), E2).then_inc(V_.h, V_.one(f"e3_{g}"))
                dve.wait_ge(P_.h, P_.at(f"p4_{g}"))
                dve.wait_ge(V_.s.h, V_.s.m)
                add(E4, b8(2), E3).then_inc(V_.h, V_.one(f"e4_{g}"))
                dve.wait_ge(P_.h, P_.at(f"p5_{g}"))
                dve.tensor_copy(NTb, b8(0)).then_inc(V_.h, V_.one(f"nt_{g}"))
                add(INT_, b8(0), eye).then_inc(V_.h, V_.one(f"int_{g}"))
                dve.wait_ge(P_.h, P_.at(f"p6_{g}"))
                dve.tensor_copy(N2, b8(2)).then_inc(V_.h, V_.one(f"n2_{g}"))
                dve.wait_ge(P_.h, P_.at(f"p7_{g}"))
                dve.wait_ge(V_.s.h, V_.s.m)
                add(GG_, b8(3), INT_).then_inc(V_.h, V_.one(f"g_{g}"))
                for j in range(2):
                    old, new = v3(X[:, j, :], 4), v3(X[:, 1 - j, :], 4)
                    dve.wait_ge(P_.h, P_.at(f"u_{g}{j}"))
                    dve.tensor_copy(UU, b4(6)).then_inc(V_.h, V_.one(f"u_{g}{j}"))
                    dve.wait_ge(P_.h, P_.at(f"dx_{g}{j}"))
                    dve.wait_ge(V_.s.h, V_.s.m)
                    add(new, b4(4), old).then_inc(V_.h, V_.one(f"xa_{g}{j}"))
                    dve.wait_ge(V_.s.h, V_.s.m)
                    for d in range(2):
                        c = CHUNKS[d][2 * g + j]
                        o = new[:, 2 * d:2 * d + 2, :]
                        ins = mult(o, o, pc[:, 2 * d:2 * d + 2, c:c + 1].broadcast_to((P, 2, CH)))
                        if d:
                            ins.then_inc(V_.h, V_.one(f"xb_{g}{j}"))
            if mod:
                mod.store(dve)
        end_phase()

        fb = Arena(tmp_at)
        dv, sq, sd = fb.take(4 * T, 4), fb.take(4 * T, 4), fb.take(4 * T, 4)
        names = [f"q{q}" for q in range(4)]
        P_, A_ = Steps(S("gn_pe"), ["m" + n for n in names] + ["v" + n for n in names]), \
            Steps(S("gn_act"), ["s" + n for n in names] + ["r" + n for n in names])
        V_ = Steps(S("gn_dve"), ["d" + n for n in names] + [x + n for n in names for x in "ingb"] + ["sum0", "sum1", "o0", "o1"])

        @block.tensor
        def _(pe):
            for q in range(4):
                pe.matmul(bank(q), C("head_sum"), Y[:, q, :], start=True, stop=True).then_inc(P_.h, P_.one(f"mq{q}"))
            for q in range(4):
                pe.wait_ge(A_.h, A_.at(f"sq{q}"))
                pe.matmul(bank(4 + q), C("head_sum"), sq[:, q, :], start=True, stop=True).then_inc(P_.h, P_.one(f"vq{q}"))

        @block.scalar
        def _(act):
            for q in range(4):
                act.wait_ge(V_.h, V_.at(f"dq{q}"))
                act.activation(sq[:, q, :], dv[:, q, :], ACT.Square).then_inc(A_.h, A_.one(f"sq{q}"))
            for q in range(4):
                act.wait_ge(P_.h, P_.at(f"vq{q}"))
                act.activation(sd[:, q, :], bank(4 + q), ACT.Sqrt, bias=eps(EPS_GN), scale=1.0 / DH).then_inc(A_.h, A_.one(f"rq{q}"))

        @block.vector
        def _(dve):
            for q in range(4):
                dve.wait_ge(P_.h, P_.at(f"mq{q}"))
                dve.scalar_tensor_tensor(dv[:, q, :], bank(q), -1.0 / DH, Y[:, q, :], ALU.mult, ALU.add).then_inc(V_.h, V_.one(f"dq{q}"))
            for q in range(4):
                dve.wait_ge(A_.h, A_.at(f"rq{q}"))
                dve.reciprocal(sd[:, q, :], sd[:, q, :]).then_inc(V_.h, V_.one(f"iq{q}"))
                dve.wait_ge(V_.s.h, V_.s.m)
                dve.tensor_tensor(dv[:, q, :], dv[:, q, :], sd[:, q, :], ALU.mult).then_inc(V_.h, V_.one(f"nq{q}"))
                dve.wait_ge(V_.s.h, V_.s.m)
                dve.tensor_scalar(dv[:, q, :], dv[:, q, :], Q1(l, "gn_g", q % 2), Q1(l, "gn_b", q % 2),
                                                    ALU.mult, ALU.add).then_inc(V_.h, V_.one(f"gq{q}"))
                dve.wait_ge(V_.s.h, V_.s.m)
                dve.tensor_tensor(dv[:, q, :], dv[:, q, :], gg[:, q, :], ALU.mult).then_inc(V_.h, V_.one(f"bq{q}"))
            dve.wait_ge(V_.s.h, V_.s.m)
            for hp in range(2):
                dve.tensor_tensor(dv[:, hp, :], dv[:, hp, :], dv[:, 2 + hp, :], ALU.add).then_inc(V_.h, V_.one(f"sum{hp}"))
            dve.wait_ge(V_.s.h, V_.s.m)
            for hp in range(2):
                dve.tensor_tensor(mixT[:, 4 + hp, :], dv[:, hp, :], bon[:, hp, :], ALU.add).then_inc(V_.h, V_.one(f"o{hp}"))
        end_phase()

    def conformer(l, glu, lo_seq, at):
        a = Arena(at)
        ns = 2 - lo_seq
        n = ns * CTX
        acc = [a.take(n, ns) for _ in range(2)]
        sq, sd = a.take(2 * n, 2), a.take(n)
        flat = lambda x: x.rearrange("p s t -> p (s t)")
        tap, fin = S("cv_tap"), S("cv_step")
        V_ = Steps(fin, ["d0", "d1", "inv", "n0", "n1", "g0", "g1"])
        A_ = Steps(S("cv_act"), ["sq0", "sq1", "root", "o0", "o1"])
        P_ = Steps(S("cv_pe"), ["mean", "var"])

        @block.vector
        def _(dve):
            for t in range(CV_TAPS):
                for i in range(2):
                    src = glu[:, i, lo_seq:2, t:t + CTX]
                    if t >= 1:
                        dve.wait_ge(tap.h, tap.at(2 * (t - 1) + i + 1))
                    wt = Q1(l, "cv_w", 2 * t + i)
                    if t == 0:
                        dve.tensor_scalar(acc[i], src, wt, Q1(l, "cv_b", i), ALU.mult, ALU.add).then_inc(tap.h, tap.one())
                    else:
                        dve.scalar_tensor_tensor(acc[i], src, wt, acc[i], ALU.mult, ALU.add).then_inc(tap.h, tap.one())
            dve.wait_ge(P_.h, P_.at("mean"))
            for i in range(2):
                dve.tensor_tensor(flat(acc[i]), flat(acc[i]), bank(0)[:, 0:n], ALU.subtract).then_inc(V_.h, V_.one(f"d{i}"))
            dve.wait_ge(A_.h, A_.at("root"))
            dve.reciprocal(sd, sd).then_inc(V_.h, V_.one("inv"))
            dve.wait_ge(fin.h, fin.m)
            for i in range(2):
                dve.tensor_tensor(flat(acc[i]), flat(acc[i]), sd, ALU.mult).then_inc(V_.h, V_.one(f"n{i}"))
            dve.wait_ge(fin.h, fin.m)
            for i in range(2):
                dve.tensor_scalar(flat(acc[i]), flat(acc[i]), Q1(l, "cv_g", i), Q1(l, "cv_beta", i),
                                                   ALU.mult, ALU.add).then_inc(V_.h, V_.one(f"g{i}"))

        @block.tensor
        def _(pe):
            pe.wait_ge(tap.h, tap.at(2 * CV_TAPS))
            for i in range(2):
                mm = pe.matmul(bank(0)[:, 0:n], C("mean_cv"), flat(acc[i]), start=i == 0, stop=i == 1)
            mm.then_inc(P_.h, P_.one("mean"))
            pe.wait_ge(A_.h, A_.at("sq1"))
            for i in range(2):
                mm = pe.matmul(bank(1)[:, 0:n], C("mean_cv"), sq[:, i, :], start=i == 0, stop=i == 1)
            mm.then_inc(P_.h, P_.one("var"))

        @block.scalar
        def _(act):
            for i in range(2):
                act.wait_ge(V_.h, V_.at(f"d{i}"))
                act.activation(sq[:, i, :], flat(acc[i]), ACT.Square).then_inc(A_.h, A_.one(f"sq{i}"))
            act.wait_ge(P_.h, P_.at("var"))
            act.activation(sd, bank(1)[:, 0:n], ACT.Sqrt, bias=eps(EPS_LN)).then_inc(A_.h, A_.one("root"))
            for i in range(2):
                act.wait_ge(V_.h, V_.at(f"g{i}"))
                act.activation(mixT[:, 6 + i, lo_seq * CTX:T], flat(acc[i]), ACT.Silu).then_inc(A_.h, A_.one(f"o{i}"))
        end_phase()

    def experts(l):
        a = Arena()
        key, gate = a.take(2 * N_EXP, 2), a.take(2 * N_EXP, 2)
        htok = a.take(2 * D, 2)
        at = a.at
        rt = a.take(KT * N_EXP, KT)
        W = lambda: a.take(2 * N_EXP, 2)
        lg, v1, o1, v2, o2, l2, sel = (W() for _ in range(7))
        st = [a.take(2, 2) for _ in range(8)]
        cnt = a.take(2)
        rin = S("router_loaded")

        @block.scalar
        def _(act):
            act.dma_start(rt, router_in[:, :].rearrange("p (k e) -> p k e", e=N_EXP)).then_inc(rin.h, 16)
        V_ = Steps(S("route_dve"), ["lg"] + [f"{x}0" for x in ("m", "v", "w", "x", "o")] + ["l2"] +
                   [f"{x}1" for x in ("m", "v", "w", "x", "o")] + ["dif", "sel", "one", "inv", "g2", "s0", "s1", "s2",
                                                                 "key0", "key1", "cnt0", "cnt1", "passes"])
        A_ = Steps(S("route_act"), ["t0", "e", "t1"])
        P_ = Steps(S("route_pe"), ["lg", "t0", "t1", "pos"])
        iota = con[:, CON["iota"][0]:CON["iota"][1]]

        @block.tensor
        def _(pe):
            pe.wait_ge(rin.h, 16)
            for tt in range(2):
                for k in range(KT):
                    mm = pe.matmul(bank(0)[:, tt * 8:tt * 8 + 8], hT[:, k, CTX + tt * P:CTX + (tt + 1) * P], rt[:, k, :],
                                   start=k == 0, stop=k == KT - 1)
            mm.then_inc(P_.h, P_.one("lg"))
            for tt in range(2):
                for k in range(KT):
                    b = 2 + 2 * tt + k // 4
                    mm = pe.transpose(bank(b)[:, (k % 4) * P:(k % 4 + 1) * P], hT[:, k, CTX + tt * P:CTX + (tt + 1) * P],
                                      C("ident"))
                mm.then_inc(P_.h, P_.one(f"t{tt}"))
            pe.wait_ge(V_.h, V_.at("sel"))
            pe.matmul(bank(1)[:, 0:8], C("before"), sel[:, 0, :], start=True, stop=True)
            pe.matmul(bank(1)[:, 8:16], C("ones"), sel[:, 0, :], start=True, stop=False)
            pe.matmul(bank(1)[:, 8:16], C("before"), sel[:, 1, :], start=False, stop=True)
            pe.matmul(bank(1)[:, 16:24], C("ones"), sel[:, 0, :], start=True, stop=False)
            pe.matmul(bank(1)[:, 16:24], C("ones"), sel[:, 1, :], start=False, stop=True).then_inc(P_.h, P_.one("pos"))

        @block.scalar
        def _(act):
            act.wait_ge(P_.h, P_.at("t0"))
            act.activation(htok[:, 0, :], banks[:, 2 * 512:4 * 512], ACT.Copy).then_inc(A_.h, A_.one("t0"))
            act.wait_ge(V_.h, V_.at("dif"))
            act.activation(st[3], st[2], ACT.Exp).then_inc(A_.h, A_.one("e"))
            act.wait_ge(P_.h, P_.at("t1"))
            act.activation(htok[:, 1, :], banks[:, 4 * 512:6 * 512], ACT.Copy).then_inc(A_.h, A_.one("t1"))

        @block.vector
        def _(dve):
            wide = lambda s: s.broadcast_to((P, 2, N_EXP))
            it = iota.rearrange("p (o e) -> p o e", o=1).broadcast_to((P, 2, N_EXP))
            dve.wait_ge(P_.h, P_.at("lg"))
            dve.tensor_copy(lg, v3(bank(0)[:, 0:16], 2)).then_inc(V_.h, V_.one("lg"))

            def pick(i, src, v, o):
                dve.wait_ge(V_.h, V_.s.m)
                dve.tensor_reduce(st[i], src, AX.X, ALU.max).then_inc(V_.h, V_.one(f"m{i}"))
                dve.wait_ge(V_.h, V_.s.m)
                dve.tensor_tensor(v, src, wide(st[i]), ALU.is_equal).then_inc(V_.h, V_.one(f"v{i}"))
                dve.wait_ge(V_.h, V_.s.m)
                dve.scalar_tensor_tensor(v, v, -100.0, it, ALU.mult, ALU.add).then_inc(V_.h, V_.one(f"w{i}"))
                dve.wait_ge(V_.h, V_.s.m)
                dve.tensor_reduce(st[4 + i], v, AX.X, ALU.min).then_inc(V_.h, V_.one(f"x{i}"))
                dve.wait_ge(V_.h, V_.s.m)
                dve.tensor_tensor(o, v, wide(st[4 + i]), ALU.is_equal).then_inc(V_.h, V_.one(f"o{i}"))
            pick(0, lg, v1, o1)
            dve.wait_ge(V_.h, V_.s.m)
            dve.scalar_tensor_tensor(l2, o1, NEG, lg, ALU.mult, ALU.add).then_inc(V_.h, V_.one("l2"))
            pick(1, l2, v2, o2)
            dve.wait_ge(V_.h, V_.s.m)
            dve.tensor_tensor(st[2], st[1], st[0], ALU.subtract).then_inc(V_.h, V_.one("dif"))
            dve.tensor_tensor(sel, o1, o2, ALU.add).then_inc(V_.h, V_.one("sel"))
            dve.wait_ge(A_.h, A_.at("e"))
            dve.tensor_scalar(st[6], st[3], 1.0, None, ALU.add).then_inc(V_.h, V_.one("one"))
            dve.wait_ge(V_.h, V_.s.m)
            dve.reciprocal(st[6], st[6]).then_inc(V_.h, V_.one("inv"))
            dve.wait_ge(V_.h, V_.s.m)
            dve.tensor_tensor(st[7], st[3], st[6], ALU.mult).then_inc(V_.h, V_.one("g2"))
            dve.wait_ge(V_.h, V_.s.m)
            dve.tensor_tensor(v1, o1, wide(st[6]), ALU.mult).then_inc(V_.h, V_.one("s0"))
            dve.tensor_tensor(v2, o2, wide(st[7]), ALU.mult).then_inc(V_.h, V_.one("s1"))
            dve.wait_ge(V_.h, V_.s.m)
            dve.tensor_tensor(gate, v1, v2, ALU.add).then_inc(V_.h, V_.one("s2"))
            dve.wait_ge(P_.h, P_.at("pos"))
            dve.scalar_tensor_tensor(key, v3(bank(1)[:, 0:16], 2), 1.0, sel, ALU.add, ALU.mult)\
                .then_inc(V_.h, V_.one("key0"))
            dve.wait_ge(V_.h, V_.s.m)
            dve.tensor_scalar(key, key, 1.0, None, ALU.subtract).then_inc(V_.h, V_.one("key1"))
            dve.tensor_reduce(cnt[:, 0:1], bank(1)[:, 16:24], AX.X, ALU.max).then_inc(V_.h, V_.one("cnt0"))
            dve.wait_ge(V_.h, V_.s.m)
            dve.tensor_scalar(cnt[:, 1:2], cnt[:, 0:1], P + 0.5, 1.0, ALU.is_gt, ALU.add).then_inc(V_.h, V_.one("cnt1"))
            dve.wait_ge(V_.h, V_.s.m)
            dve.tensor_copy(passes[:, :], cnt[:, 1:2]).then_inc(V_.h, V_.one("passes"))
        end_phase()

        a = Arena(at)
        sg, hid = a.take(2 * 256, 2), a.take(2 * 256, 2)
        xg = [v3(b, KT) for b in (a.take(KT * P), a.take(KT * P))]
        pick_, send = ([v3(b, 2) for b in (a.take(2 * P), a.take(2 * P))] for _ in range(2))
        sent = [a.take(LAT) for _ in range(2)]
        ysb = a.take(D)
        work = [S(f"x_loaded_{i}") for i in range(RING)]
        x_loaded = work[:]
        names = ("x_used", "x_silu", "x_hidden", "x_picked", "x_gathered", "x_copied", "x_turned", "x_turned_copied",
                 "x_summed", "x_scattered", "x_added")
        x_used, si, ac, picked, gathered, xcop, turned, tcop, summed, scat, added = (S(n) for n in names)
        work += [S(n) for n in names]
        met, go = S("pass_met"), S("pass_go")
        N, n_units = N_EXP * FFE_UNITS, FFE_UNITS
        base = stream["put"] - stream["skew"]
        trips = (n_units - 2) // 2
        gate_bank, up_bank = (lambda U: bank(U % 2)), (lambda U: bank(2 + U % 2))
        gate_of = lambda U: 3 * U if U else 1
        up_of = lambda U: 3 * U + 1 if U else 2
        down_of = lambda U: 3 * U + 5 if U < N - 1 else 3 * N
        assert trips * 2 + 2 == n_units and 3 * n_units % RING == 0

        def passes_of(eng):
            return eng.value_load(passes[0:1, 0:1], min_val=1, max_val=2)

        def leave(eng, p):
            eng.drain().then_inc(met.h, 1)
            eng.wait_ge(go.h, 1)

        @block.gpsimd
        def _(pool):
            with pool.Fori(0, passes_of(pool)) as p:
                pool.wait_ge(met.h, 4)
                for s in work + [met]:
                    pool.sem_clear(s.h)
                pool.drain().then_inc(go.h, 1)

        @block.sync
        def _(sp):
            sp.wait_ge(S("phase_met").h, 4 * phase["n"])
            sp.wait_ge(used.h, stream["put"])
            with sp.Fori(0, passes_of(sp)) as p:
                def load(n, i=None, wait_for=None):
                    if wait_for is not None:
                        sp.wait_ge(x_used.h, wait_for)
                    src = parts[base + n, :, :] if i is None else \
                        parts[bass.ds(i * RING + (base + n), 1), :, :].rearrange("a p n -> p (a n)")
                    sp.dma_start(slots[:, n % RING, :], src).then_inc(x_loaded[n % RING].h, 16)
                for n in range(2):
                    load(n)
                for e in range(N_EXP):
                    n0 = 2 + 3 * n_units * e
                    for n in range(n0, n0 + 3):
                        load(n, None, n - RING + 1 if n >= RING else None)
                    with sp.Fori(0, trips) as i:
                        for n in range(n0 + 3, n0 + 9):
                            load(n, i, i * RING + (n - RING + 1))
                    for n in range(n0 + 3 * (n_units - 1), n0 + 3 * n_units - (2 if e == N_EXP - 1 else 0)):
                        load(n, None, n - RING + 1)
                leave(sp, p)

        def over_units(eng, e, body, static_part):
            body(e * n_units, 0, 1)
            static_part(e)
            with eng.Fori(0, trips) as i:
                for j in range(2):
                    body(e * n_units + 1 + j, i, trips)
            body((e + 1) * n_units - 1, 0, 1)

        @block.tensor
        def _(pe):
            with pe.Fori(0, passes_of(pe)) as p:
                def take(n, i):
                    goal = 16 * (n // RING + 1)
                    pe.wait_ge(x_loaded[n % RING].h, i * 16 + goal)
                    return slots[:, n % RING, :]

                def products(U, n, i, times):
                    x = xg[(U // n_units) % 2]
                    for which, bk in enumerate((gate_bank(U), up_bank(U))):
                        w = v3(take(n + which, i), KT)
                        if which == 0:
                            pe.wait_ge(ac.h, i * 2 + (U + 1))
                        for j in range(2):
                            for k in range(KT):
                                mm = pe.matmul(bk[:, j * P:(j + 1) * P], w[:, k, j * P:(j + 1) * P], x[:, k, :],
                                               start=k == 0, stop=k == KT - 1)
                        mm.then_inc(x_used.h, 1)

                def down(U, n, i, times):
                    u = U % n_units
                    w = v3(take(n, i), 2)
                    pe.wait_ge(ac.h, i * 2 + (U + 3))
                    if u == 0 and U:
                        pe.wait_ge(summed.h, U // n_units)
                    for j in range(2):
                        for half in range(2):
                            mm = pe.matmul(bank(4 + half), hid[:, U % 2, j * P:(j + 1) * P], w[:, j, half * 512:(half + 1) * 512],
                                           start=times == 1 and u == 0 and j == 0, stop=times == 1 and u > 0 and j == 1,
                                           skip_group_check=True)
                    mm.then_inc(x_used.h, 1)

                def gather(e):
                    pe.wait_ge(picked.h, e + 1)
                    if e >= 2:
                        pe.wait_ge(added.h, 4 * (e - 1))
                    for k in range(KT):
                        for tt in range(2):
                            mm = pe.matmul(bank(6 + k // 4)[:, (k % 4) * P:(k % 4 + 1) * P], htok[:, tt, k * P:(k + 1) * P],
                                           pick_[e % 2][:, tt, :], start=tt == 0, stop=tt == 1)
                    mm.then_inc(gathered.h, 1)
                    pe.wait_ge(xcop.h, e + 1)
                    for tt in range(2):
                        mm = pe.transpose(bank(6)[:, tt * P:(tt + 1) * P], send[e % 2][:, tt, :], C("ident"))
                    mm.then_inc(turned.h, 1)

                def scatter(e):
                    pe.wait_ge(summed.h, e + 1)
                    pe.wait_ge(tcop.h, min(e + 2, N_EXP))
                    for f in range(4):
                        if f >= 2:
                            pe.wait_ge(added.h, 4 * e + f - 1)
                        for m in range(2 * f, 2 * f + 2):
                            mm = pe.matmul(bank(6 + f % 2)[:, (m % 2) * LAT:(m % 2 + 1) * LAT], ysb[:, m * P:(m + 1) * P],
                                           sent[e % 2], start=True, stop=True)
                        mm.then_inc(scat.h, 1)

                gather(0)
                products(0, 0, 0, 1)

                def body(U, i, times):
                    n = 2 + 3 * U
                    if U < N - 1:
                        products(U + 1, n, i, times)
                        down(U, n + 2, i, times)
                    else:
                        down(U, n, i, times)

                def own_part(e):
                    if e:
                        scatter(e - 1)
                    if e + 1 < N_EXP:
                        gather(e + 1)
                for e in range(N_EXP):
                    over_units(pe, e, body, own_part)
                scatter(N_EXP - 1)
                leave(pe, p)

        @block.scalar
        def _(act):
            with act.Fori(0, passes_of(act)) as p:
                def gathered_out(e):
                    act.wait_ge(gathered.h, e + 1)
                    act.activation(xg[e % 2].rearrange("p k s -> p (k s)"), banks[:, 6 * 512:8 * 512], ACT.Copy)\
                        .then_inc(xcop.h, 1)
                    act.wait_ge(turned.h, e + 1)
                    act.activation(sent[e % 2], bank(6)[:, 0:LAT], ACT.Copy).then_inc(tcop.h, 1)

                def sums_out(e):
                    act.wait_ge(x_used.h, down_of(n_units * (e + 1) - 1))
                    if e:
                        act.wait_ge(scat.h, 4 * e)
                    act.activation(ysb, banks[:, 4 * 512:6 * 512], ACT.Copy).then_inc(summed.h, 1)

                def body(U, i, times):
                    act.wait_ge(x_used.h, i * RING + gate_of(U))
                    act.wait_ge(ac.h, i * 2 + (U + 1))
                    act.activation(sg[:, U % 2, :], gate_bank(U)[:, 0:256], ACT.Silu).then_inc(si.h, 1)
                    if U and U % n_units == 0 and times == 1:
                        sums_out(U // n_units - 1)

                def own_part(e):
                    if e + 1 < N_EXP:
                        gathered_out(e + 1)
                gathered_out(0)
                for e in range(N_EXP):
                    over_units(act, e, body, own_part)
                sums_out(N_EXP - 1)
                leave(act, p)

        @block.vector
        def _(dve):
            keyed = S("key_moved")
            with dve.Fori(0, passes_of(dve)) as p:
                def choose(e):
                    for o, by_gate in ((pick_, False), (send, True)):
                        for tt in range(2):
                            kc, gc = key[:, tt, e:e + 1], gate[:, tt, e:e + 1]
                            if by_gate:
                                ins = dve.tensor_scalar(o[e % 2][:, tt, :], C("slot"), kc, gc, ALU.is_equal, ALU.mult)
                            else:
                                ins = dve.tensor_scalar(o[e % 2][:, tt, :], C("slot"), kc, None, ALU.is_equal)
                    ins.then_inc(picked.h, 1)

                def add(e):
                    for f in range(4):
                        dve.wait_ge(scat.h, 4 * e + f + 1)
                        for m in range(2 * f, 2 * f + 2):
                            xs = xT[:, m, CTX:T]
                            ins = dve.scalar_tensor_tensor(xs, bank(6 + f % 2)[:, (m % 2) * LAT:(m % 2 + 1) * LAT],
                                                           modc(l, 40 + m, 1), xs, ALU.mult, ALU.add)
                        ins.then_inc(added.h, 1)

                for j in range(2):
                    dve.memset(hid[:, j, :], 0.0).then_inc(ac.h, 1)
                choose(0)

                def body(U, i, times):
                    dve.wait_ge(x_used.h, i * RING + up_of(U))
                    dve.wait_ge(si.h, i * 2 + (U + 1))
                    dve.tensor_tensor(hid[:, U % 2, :], up_bank(U)[:, 0:256], sg[:, U % 2, :], ALU.mult).then_inc(ac.h, 1)

                def own_part(e):
                    if e + 1 < N_EXP:
                        choose(e + 1)
                    if e:
                        add(e - 1)
                for e in range(N_EXP):
                    over_units(dve, e, body, own_part)
                add(N_EXP - 1)
                dve.tensor_scalar(key, key, float(P), None, ALU.subtract).then_inc(picked.h, 1)
                leave(dve, p)
        stream["skew"] -= 3 * N
        end_phase()

        @block.sync
        def _(sp):
            sp.wait_ge(S("phase_met").h, 4 * phase["n"])

    def mixer_inputs(l):
        ctx_out = l < DEPTH - 1
        first = 0 if ctx_out else CTX
        a = Arena()
        us = a.take(10 * T, 10)
        glu = a.take(2 * 2 * (CTX + 2 * CV_PAD)).rearrange("p (i s t) -> p i s t", i=2, s=2)
        q, k, v = a.take(4 * T, 4), a.take(4 * T, 4), a.take(4 * T, 4)
        bias = a.take(2 * NA_H * LAT, 2 * NA_H)
        at = a.at
        gate = a.take(2 * T, 2)
        rw_tiles = [dict(part=6 + t // 2, j=t % 2, cols=(0, T), src=hT, owner="dve") for t in range(10)]
        tiles = [dict(part=t // 2, j=t % 2, cols=(first, T), src=hT, owner="act") for t in range(4)]
        tiles += [dict(part=2 + t // 2, j=t % 2, cols=(0, T), src=hT, owner="act") for t in range(4)]
        tiles += [dict(part=4 + p, tok=t, cols=(0, T), src=hT, owner="act") for p in range(2) for t in range(4)]
        tiles += rw_tiles
        tiles += [dict(part=11, j=t, cols=(first, T), src=hT, owner="act") for t in range(2)]
        tiles += [dict(part=12, j=t, cols=(first, T), src=hT, owner="dve") for t in range(2)]
        tile_done, free = project(tiles)
        own_part, sig, b_in, b_ok = S("shift_own"), S("conv_gate"), S("bias_loaded"), S("bias_masked")

        @block.scalar
        def _(act):
            act.dma_start(bias, bias_in[l, :, :].rearrange("p (q k) -> p q k", k=LAT)).then_inc(b_in.h, 16)
            for t in range(len(tiles)):
                bk = bank(t % 8)
                act.wait_ge(*tile_done(t))
                if t < 4:
                    act.activation(q[:, t, first:T], bk[:, 0:T - first], ACT.Copy, scale=DH ** -0.5).then_inc(free["act"].h, free["act"].one())
                elif t < 8:
                    act.activation(k[:, t - 4, :], bk, ACT.Copy).then_inc(free["act"].h, free["act"].one())
                elif t < 16:
                    p, tok = divmod(t - 8, 4)
                    act.activation(v[:, tok, p * UNIT:(p + 1) * UNIT], bk[:, 0:UNIT], ACT.Copy).then_inc(free["act"].h, free["act"].one())
                elif t < 26:
                    act.activation(us[:, t - 16, :], bk, ACT.Copy, scale=scal[l][:, 32 + t - 16:33 + t - 16]).then_inc(own_part.h, own_part.one())
                elif t < 28:
                    act.activation(gate[:, t - 26, first:T], bk[:, 0:T - first], ACT.Sigmoid).then_inc(free["act"].h, free["act"].one())

        @block.vector
        def _(dve):
            own_pad = S("conv_pad")
            for s in range(2):
                dve.memset(glu[:, :, s, 0:CV_PAD], 0.0).then_inc(own_pad.h, own_pad.one())
                dve.memset(glu[:, :, s, CV_PAD + CTX:], 0.0).then_inc(own_pad.h, own_pad.one())
            dve.wait_ge(b_in.h, 16 * (l + 1))
            for h in range(2):
                bh = bias[:, h * NA_H:(h + 1) * NA_H, :].rearrange("p h (r c) -> p (h r) c", c=64)
                for i, (name, op) in enumerate((("win", ALU.mult), ("out_win", ALU.add))):
                    dve.wait_ge(b_ok.h, b_ok.at(2 * h + i))
                    m = C(name).rearrange("p (o k) -> p o k", o=1).broadcast_to((P, NA_H * 4, 64))
                    dve.tensor_tensor(bh, bh, m, op).then_inc(b_ok.h, b_ok.one())
            side = S("shift_side")
            for t in range(16, 26):
                i = t - 16
                dve.wait_ge(own_part.h, own_part.at(i + 1))
                u3, p3 = (x.rearrange("p (s t) -> p s t", s=2) for x in (us[:, i, :], bank(t % 8)))
                dve.scalar_tensor_tensor(u3[:, :, 1:CTX], p3[:, :, 0:CTX - 1], Q1(l, "mu_prev", i), u3[:, :, 1:CTX],
                                                  ALU.mult, ALU.add).then_inc(side.h, side.one())
                dve.wait_ge(side.h, side.at(i + 1))
                dve.scalar_tensor_tensor(u3[:, :, 0:CTX - 1], p3[:, :, 1:CTX], Q1(l, "mu_next", i),
                                                         u3[:, :, 0:CTX - 1], ALU.mult, ALU.add).then_inc(free["dve"].h, free["dve"].one())
            for t in range(28, 30):
                i = t - 28
                dve.wait_ge(*tile_done(t))
                dve.wait_ge(free["act"].h, free["act"].at(18))
                ns = (T - first) // CTX
                dve.tensor_tensor(glu[:, i, 2 - ns:2, CV_PAD:CV_PAD + CTX],
                                                  bank(t % 8)[:, 0:T - first].rearrange("p (s t) -> p s t", s=ns),
                                                  gate[:, i, first:T].rearrange("p (s t) -> p s t", s=ns), ALU.mult).then_inc(free["dve"].h, free["dve"].one())
        end_phase()
        units = []
        for h in range(NA_H):
            for t in range(2):
                units.append((h // 2, h % 2, CTX + t * P, [(CTX, T), (0, CTX)], [2, 3, 0, 1], bias[:, t * NA_H + h, :], CTX))
        k_same, v_cols = (lambda tile: tile), (lambda tile, half: tile * P + half * DH)
        attention(units, q, k, v, 1.0, LAT, k_same, v_cols, at)
        if ctx_out:
            units = [(h // 2, h % 2, t * P, [(0, CTX)], [0, 1], None, 0) for h in range(NA_H) for t in range(2)]
            attention(units, q, k, v, 1.0, CTX, k_same, v_cols, at)
        conformer(l, glu, 0 if ctx_out else 1, at)
        recurrence(l, us, 10 * T)

    def second_mixers(l):
        a = Arena()
        qk = a.take(5 * LAT, 5)
        v = a.take(2 * P, 2)
        sv, su, cb, cc = (a.take(2 * LAT, 2) for _ in range(4))
        cx = a.take(2 * (LAT + 2), 2)
        qn, sq, sd = a.take(5 * LAT, 5), a.take(7 * LAT, 7), a.take(6 * LAT, 6)
        vnt, sgw, sgb, cv = a.take(2 * 2 * P, 2), a.take(4 * P, 4), a.take(P), a.take(2 * LAT, 2)
        at = a.at
        lat = (CTX, T)
        tiles = [dict(part=t // 2, j=t % 2, cols=lat, src=hT, owner="act") for t in range(4)]
        tiles += [dict(part=2, j=0, cols=lat, src=hT, owner="act")]
        tiles += [dict(part=2, tok=2 + t, wide=P, cols=lat, src=hT, owner="act") for t in range(2)]
        tiles += [dict(part=3 + t // 2, j=t % 2, cols=lat, src=hT, owner="act") for t in range(8)]
        tiles += [dict(part=7, j=t, cols=lat, src=hT, owner="dve") for t in range(2)]
        tile_done, free = project(tiles)
        s_in = S("gating_loaded")

        @block.scalar
        def _(act):
            act.dma_start(sgw, sgw_in[l, :, :].rearrange("p (h n) -> p h n", h=4)).then_inc(s_in.h, 16)
            act.dma_start(sgb[0:4, :], sgb_in[l, :, :]).then_inc(s_in.h, 16)
            for t in range(15):
                act.wait_ge(*tile_done(t))
                bk = bank(t % 8)
                if t < 5:
                    o = qk[:, t, :]
                elif t < 7:
                    o = v[:, t - 5, :]
                else:
                    o = (sv, su, cb, cc)[(t - 7) // 2][:, (t - 7) % 2, :]
                n = P if 5 <= t < 7 else LAT
                act.activation(o, bk[:, 0:n], ACT.Copy).then_inc(free["act"].h, free["act"].one())

        @block.vector
        def _(dve):
            pad = S("conv_pad")
            dve.memset(cx[:, :, 0:1], 0.0).then_inc(pad.h, pad.one())
            dve.memset(cx[:, :, LAT + 1:LAT + 2], 0.0).then_inc(pad.h, pad.one())
            for i in range(2):
                dve.wait_ge(*tile_done(15 + i))
                dve.wait_ge(free["act"].h, free["act"].at(15))
                dve.tensor_tensor(cx[:, i, 1:LAT + 1], bank((15 + i) % 8)[:, 0:LAT], cc[:, i, :], ALU.mult).then_inc(free["dve"].h, free["dve"].one())
        end_phase()

        sA, sP, sV = S("m2_act"), S("m2_pe"), S("m2_dve")
        A_ = Steps(sA, [f"sq{t}" for t in range(7)] + [f"rt{t}" for t in range(6)] + ["tn0", "tn1"])
        P_ = Steps(sP, [f"ms{t}" for t in range(6)] + [f"sw{t}" for t in range(5)] + ["vt", "mixed"])
        V_ = Steps(sV, ["c00", "c01", "c10", "c11", "c20", "c21", "cm0", "cm1"] + [f"i{t}" for t in range(6)] +
                   [f"n{t}" for t in range(7)] + [f"{x}{t}" for t in range(5) for x in ("sin", "cos", "rot")] + ["g0", "g1"])
        bk = lambda t: bank(t)[:, 0:LAT]

        @block.scalar
        def _(act):
            for t in range(7):
                act.activation(sq[:, t, :], qk[:, t, :] if t < 5 else sv[:, t - 5, :], ACT.Square).then_inc(A_.h, A_.one(f"sq{t}"))
            for t in range(6):
                act.wait_ge(P_.h, P_.at(f"ms{t}"))
                act.activation(sd[:, t, :], bk(t), ACT.Sqrt, bias=eps(EPS_RMS),
                                                 scale=1.0 / DH if t < 5 else 1.0).then_inc(A_.h, A_.one(f"rt{t}"))
            act.wait_ge(P_.h, P_.at("vt"))
            for c in range(2):
                act.activation(vnt[:, c, :], bank(6)[:, c * 256:(c + 1) * 256], ACT.Copy).then_inc(A_.h, A_.one(f"tn{c}"))

        @block.tensor
        def _(pe):
            for t in range(5):
                pe.wait_ge(A_.h, A_.at(f"sq{t}"))
                pe.matmul(bk(t), C("head_sum"), sq[:, t, :], start=True, stop=True).then_inc(P_.h, P_.one(f"ms{t}"))
            pe.wait_ge(A_.h, A_.at("sq6"))
            for i in range(2):
                mm = pe.matmul(bk(5), C("mean_cv"), sq[:, 5 + i, :], start=i == 0, stop=i == 1)
            mm.then_inc(P_.h, P_.one("ms5"))
            for t in range(5):
                pe.wait_ge(V_.h, V_.at(f"n{t}"))
                pe.matmul(bk(t), C("swap"), qn[:, t, :],
                                            start=True, stop=True).then_inc(P_.h, P_.one(f"sw{t}"))
            pe.wait_ge(V_.h, V_.at("n6"))
            for c in range(2):
                for i in range(2):
                    mm = pe.transpose(bank(6)[:, c * 256 + i * P:c * 256 + (i + 1) * P], sq[:, 5 + i, c * P:(c + 1) * P],
                                      C("ident"))
            mm.then_inc(P_.h, P_.one("vt"))
            pe.wait_ge(A_.h, A_.at("tn1"))
            pe.wait_ge(s_in.h, 32 * (l + 1))
            for h in range(4):
                hs = slice((h % 2) * DH, (h % 2) * DH + DH)
                for c in range(2):
                    o = bank(7)[hs, (h // 2) * LAT + c * P:(h // 2) * LAT + (c + 1) * P]
                    pe.matmul(o, vnt[:, c, h * DH:(h + 1) * DH], sgw[:, h, :], start=True, stop=False)
                    lo = CON["sel"][0] + h * P
                    mm = pe.matmul(o, con[0:4, lo:lo + DH], sgb[0:4, :], start=False, stop=True)
            mm.then_inc(P_.h, P_.one("mixed"))

        @block.vector
        def _(dve):
            for tap in range(3):
                dve.wait_ge(sV.h, sV.m)
                for i in range(2):
                    w, x = Q2(l, "conv_w", 2 * tap + i), cx[:, i, tap:tap + LAT]
                    ins = dve.tensor_scalar(cv[:, i, :], x, w, None, ALU.mult) if tap == 0 else \
                        dve.scalar_tensor_tensor(cv[:, i, :], x, w, cv[:, i, :], ALU.mult, ALU.add)
                    ins.then_inc(V_.h, V_.one(f"c{tap}{i}"))
            dve.wait_ge(sV.h, sV.m)
            for i in range(2):
                dve.tensor_tensor(mixT[:, 6 + i, CTX:T], cv[:, i, :], cb[:, i, :], ALU.mult).then_inc(V_.h, V_.one(f"cm{i}"))
            for t in range(6):
                dve.wait_ge(A_.h, A_.at(f"rt{t}"))
                dve.reciprocal(sd[:, t, :], sd[:, t, :]).then_inc(V_.h, V_.one(f"i{t}"))
            dve.wait_ge(sV.h, sV.m)
            for t in range(5):
                dve.scalar_tensor_tensor(qn[:, t, :], qk[:, t, :], Q2(l, "q_g" if t < 4 else "k_g", 0),
                                                          sd[:, t, :], ALU.mult, ALU.mult).then_inc(V_.h, V_.one(f"n{t}"))
            dve.wait_ge(P_.h, P_.at("ms5"))
            for i in range(2):
                dve.scalar_tensor_tensor(sq[:, 5 + i, :], sv[:, i, :], Q2(l, "sg_g", i), sd[:, 5, :],
                                                              ALU.mult, ALU.mult).then_inc(V_.h, V_.one(f"n{5 + i}"))
            for t in range(5):
                dve.wait_ge(P_.h, P_.at(f"sw{t}"))
                dve.tensor_tensor(qk[:, t, :], bk(t), C("sin"),
                                                     ALU.mult).then_inc(V_.h, V_.one(f"sin{t}"))
                dve.tensor_tensor(qn[:, t, :], qn[:, t, :], C("cos"), ALU.mult).then_inc(V_.h, V_.one(f"cos{t}"))
                dve.wait_ge(sV.h, sV.m)
                dve.tensor_tensor(qk[:, t, :], qk[:, t, :], qn[:, t, :], ALU.add).then_inc(V_.h, V_.one(f"rot{t}"))
            dve.wait_ge(P_.h, P_.at("mixed"))
            for i in range(2):
                dve.tensor_tensor(mixT[:, 4 + i, CTX:T], bank(7)[:, i * LAT:(i + 1) * LAT], su[:, i, :],
                                                   ALU.mult).then_inc(V_.h, V_.one(f"g{i}"))
        end_phase()
        units = [(j, g, t * P, [(0, LAT)], [0, 1], None, CTX) for j in range(4) for g in range(2) for t in range(2)]
        attention(units, qk, qk, v, DH ** -0.5, LAT, lambda tile: 4, lambda tile, half: half * DH, at)

    ready = S("inputs_loaded")

    @block.scalar
    def _(act):
        act.dma_start(ct[:, :], ct_in[:, :]).then_inc(ready.h, 16)
        act.dma_start(con[:, :], con_in[:, :]).then_inc(ready.h, 16)
        act.dma_start(x_buf[:, :], xt_in[:, :]).then_inc(ready.h, 16)
        for l in range(DEPTH):
            act.dma_start(par1[l][:, :], par1_in[l, :, :]).then_inc(ready.h, 16)
            act.dma_start(par2[l][:, :], par2_in[l, :, :]).then_inc(ready.h, 16)
        act.wait_ge(ready.h, 16 * 7)
        act.activation(ct[:, :], ct[:, :], ACT.Silu).then_inc(S("condition").h, S("condition").one())
    end_phase()

    def gated(l_gate, s):
        def put(dve, m, acc):
            cols = xT[:, m, s * CTX:(s + 1) * CTX]
            if l_gate:
                ins = dve.scalar_tensor_tensor(cols, acc, modc(l_gate - 1, 40 + m, s), cols, ALU.mult, ALU.add)
            else:
                ins = dve.tensor_tensor(cols, acc, cols, ALU.add)
            ins.then_inc(S("residual").h, S("residual").one())
        return put

    modulation([(0, 0, 16)])
    for l in range(DEPTH):
        ctx_out = l < DEPTH - 1
        cols = (0, T) if ctx_out else (CTX, T)
        norm(xT, hT, (0, T), gain1(l), lambda t, s: modc(l, t, s), "1")
        mixer_inputs(l)
        out_project(mixT, cols, lambda t, s: modc(l, 16 + t, s))
        norm(xT, hT, cols, gain2(l), lambda t, s: modc(l, 24 + t, s), "2")
        if l % 2 == 0:
            feed_forward("silu", 1, FF_UNITS, hT, CTX, gated(l + 1, 1))
            if ctx_out:
                stream["skew"] += 3 * FF_UNITS
                feed_forward("silu", 1, FF_UNITS, hT, 0, gated(l + 1, 0))
        else:
            experts(l)
    lat = (CTX, T)
    norm(xT, xT, lat, lambda k, s: Q1(0, "final_g", k), None, "final")
    for l in range(DEPTH):
        norm(xT, hT, lat, lambda k, s, l=l: Q2(l, "norm1_g", k), None, "1")
        second_mixers(l)
        out_project(mixT, lat, None)
        norm(xT, hT, lat, lambda k, s, l=l: Q2(l, "norm2_g", k), None, "2")
        feed_forward("conv", 1, FF_UNITS, hT, CTX, gated(False, 1),
                     taps=lambda tap, t, l=l: Q2(l, "ffn_w", 44 * tap + t))

    @block.scalar
    def _(act):
        stored = S("output_stored")
        act.dma_start(out[:, :].rearrange("p (k t) -> p k t", k=KT), xT[:, :, CTX:T]).then_inc(stored.h, 16)
        act.wait_ge(stored.h, 16)
    assert stream["put"] == stream["got"]
    ctx.close()
    return stream["got"] - stream["skew"]


def cols_of(w):
    n = w.shape[1] // UNIT
    return w.reshape(KT, P, n, UNIT).transpose(2, 1, 0, 3).reshape(n, P, PART)


def rows_of(w):
    n = w.shape[0] // UNIT
    return w.reshape(n, 2, P, D).transpose(0, 2, 1, 3).reshape(n, P, PART)


def ff_parts(gate, up, down):
    n = len(gate)
    out = [gate[0], up[0]]
    for u in range(1, n):
        out += [gate[u], up[u], down[u - 1]]
    return out + [down[n - 1]]


def columns(v):
    return np.asarray(v).reshape(-1, P).T


def kernel(**i):
    import concourse.bacc as bacc
    from concourse.bass_utils import run_bass_kernel_spmd as run

    i = {k: np.asarray(v) for k, v in i.items()}
    parts = []
    mod = [list(cols_of(w)) for w in i["mod_w"]]
    parts += mod[0][:8]
    for l in range(DEPTH):
        w = i["w_in"][l]
        o_cv = 3 * NA_W + RW_IN
        parts += list(cols_of(w[:, :o_cv])) + list(cols_of(w[:, o_cv + 256:])) + list(cols_of(w[:, o_cv:o_cv + 256]))
        if l == 0:
            parts += mod[0][8:] + mod[1]
        parts += list(cols_of(i["w_out"][l]))
        if l % 2 == 0:
            j = l // 2
            parts += ff_parts(cols_of(i["ffn_w_gate"][j]), cols_of(i["ffn_w_up"][j]), rows_of(i["ffn_w_down"][j]))
        else:
            j = l // 2
            parts += ff_parts([p for e in range(N_EXP) for p in cols_of(i["moe_w_gate"][j, e])],
                              [p for e in range(N_EXP) for p in cols_of(i["moe_w_up"][j, e])],
                              [p for e in range(N_EXP) for p in rows_of(i["moe_w_down"][j, e])])
    for l in range(DEPTH):
        w = i["w_in_2"][l]
        heads = [h * DH + f for t in range(4) for h in (t, t + 4) for f in range(DH)]
        q, kv, su, sv, rest = w[:, :512][:, heads], w[:, 512:768], w[:, 768:1024], w[:, 1024:1280], w[:, 1280:]
        parts += list(cols_of(np.concatenate([q, kv, sv, su, rest], 1)))
        wo = i["w_out_2"][l]
        parts += list(cols_of(np.concatenate([wo[:512][heads], wo[512:]], 0)))
        up = i["ffn_w_up_2"][l]
        parts += ff_parts(cols_of(up[:, :D_FF]), cols_of(up[:, D_FF:]), rows_of(i["ffn_w_down_2"][l]))
    n_parts = len(parts)
    xt = np.concatenate([i["ctx"][0], i["x"][0]], 0).T.reshape(KT, P, T).transpose(1, 0, 2).reshape(P, KT * T)
    ct = np.stack([i["c_ctx"], i["c"][0]], 1).reshape(KT, P, 2).transpose(1, 0, 2).reshape(P, KT * 2)
    par1, par2, lora, gate2, bias = [], [], [], [], []
    qr, qc = np.arange(LAT) // 64, np.arange(LAT) % 64
    r_at = qr[None, :] - qr[:, None] + 7
    c_at = qc[None, :] - qc[:, None] + 15
    near = (c_at >= 0) & (c_at <= 30)
    for l in range(DEPTH):
        vec = dict(norm1_g="norm1_g", norm2_g="norm2_g", mod_b="mod_b", mu_prev="rw_mu_prev", mu_next="rw_mu_next",
                   w0="rw_w0", a0="rw_a0", k_k="rw_k_k", k_a="rw_k_a", r_k="rw_r_k", gn_g="rw_gn_g", gn_b="rw_gn_b",
                   cv_b="cv_dw_b", cv_g="cv_ln_g", cv_beta="cv_ln_b", cv_w="cv_dw_w")
        par1.append(np.concatenate([columns(i["final_g"] if n == "final_g" else i[vec[n]][l]) for n in P1], 1))
        q_g, k_g = (np.concatenate([i[n][l]] * 2) for n in ("q_norm_g_2", "k_norm_g_2"))
        par2.append(np.concatenate([columns(v) for v in (i["norm1_g_2"][l], i["norm2_g_2"][l], q_g, k_g, i["sg_norm_g_2"][l],
                                                         i["conv_w_2"][l], i["ffn_conv_w_2"][l])], 1))
        lora.append(np.concatenate([i["rw_w2"][l], i["rw_a2"][l]], 1).transpose(1, 0, 2).reshape(P, 512))
        gate2.append(i["rw_g2"][l].transpose(1, 0, 2).reshape(P, 512))
        b = i["na_rpb"][l][:, r_at, np.clip(c_at, 0, 30)]
        b = np.where(near, b, np.float32(0))
        bias.append(b.reshape(NA_H, 2, P, LAT).transpose(2, 1, 0, 3).reshape(P, -1))
    router = i["moe_router"][0].reshape(KT, P, N_EXP).transpose(1, 0, 2).reshape(P, KT * N_EXP)
    sgw = i["sg_w_2"].transpose(0, 3, 1, 2).reshape(DEPTH, P, 4 * P)
    arrays = {
        "parts": np.stack(parts), "xt": xt, "ct": ct, "con": constants(), "par1": np.stack(par1), "par2": np.stack(par2),
        "lora": np.stack(lora), "gate2": np.stack(gate2), "router": router, "bias": np.stack(bias), "sgw": sgw,
        "sgb": i["sg_b_2"],
    }
    nc = bacc.Bacc("TRN2", target_bir_lowering=False, num_devices=1)
    args = []
    for name, a in arrays.items():
        arrays[name] = np.ascontiguousarray(a)
        args.append(nc.dram_tensor(name, a.shape, F32, kind="ExternalInput").ap())
    args.append(nc.dram_tensor("out", (P, KT * LAT), F32, kind="ExternalOutput").ap())
    assert build(nc, *args) == n_parts
    got = run(nc, [arrays], core_ids=[0]).results[0]["out"]
    return got.reshape(P, KT, LAT).transpose(2, 1, 0).reshape(1, LAT, D)
```

```python
from contextlib import ExitStack

import numpy as np

import concourse.bass as bass
from concourse import mybir

F32 = mybir.dt.float32
F32R = mybir.dt.float32r
ACT = mybir.ActivationFunctionType
ALU = mybir.AluOpType
AX = mybir.AxisListType

P = 128
D = 1024
KT = D // P
CTX, LAT = 256, 256
T = CTX + LAT
DH = 64
DEPTH = 2
NA_H, NA_W = 8, 512
RW_W, RW_IN = 256, 1280
CV_TAPS, CV_PAD = 31, 15
D_FF, D_FFE, N_EXP = 2816, 3584, 8
UNIT = 256
PART = KT * UNIT
HIGHS = 2
RING = 6
CH = 64
NCH = T // CH
NEG = -1.0e30
FF_UNITS, FFE_UNITS = D_FF // UNIT, D_FFE // UNIT
MOD_PARTS = 6 * D // UNIT
SG_CHUNK = 128

CHUNKS = [list(range(NCH)), [3, 2, 1, 0, 7, 6, 5, 4]]

P1 = {}
_at = 0
for _name, _n in [("norm1_g", 8), ("norm2_g", 8), ("mod_b", 48), ("mu_prev", 10), ("mu_next", 10),
                  ("w0", 4), ("a0", 4), ("k_k", 2), ("k_a", 2), ("r_k", 2), ("gn_g", 2), ("gn_b", 2),
                  ("cv_b", 2), ("cv_g", 2), ("cv_beta", 2), ("cv_w", 2 * CV_TAPS), ("final_g", 8)]:
    P1[_name] = (_at, _at + _n)
    _at += _n
P1_COLS = _at
P2 = {}
_at = 0
for _name, _n in [("norm1_g", 8), ("norm2_g", 8), ("q_g", 1), ("k_g", 1), ("sg_g", 2), ("conv_w", 6),
                  ("ffn_w", 3 * 44)]:
    P2[_name] = (_at, _at + _n)
    _at += _n
P2_COLS = _at

CON = {}
_at = 0
for _name, _n in [("mean_d", 128), ("head_sum", 128), ("ident", 128), ("eye64", 64), ("mask_zr", 512),
                  ("mask_d", 256), ("mask_l", 256), ("mask_dt", 256), ("not_first", 512), ("swap", 128),
                  ("cos", 256), ("sin", 256), ("win", 64), ("out_win", 64), ("sel", 512),
                  ("eps", 8), ("iota", 8), ("mean_cv", 128), ("ones", 128),
                  ("before", 128), ("slot", 128)]:
    CON[_name] = (_at, _at + _n)
    _at += _n
CON_COLS = _at
EPS_RMS, EPS_LN, EPS_GN, EPS_KK = 0, 1, 2, 3


def constants():
    c = np.zeros((P, CON_COLS), np.float32)

    def put(name, a):
        lo, hi = CON[name]
        c[:a.shape[0], lo:hi] = a
    p = np.arange(P)
    put("mean_d", np.full((P, P), 1.0 / D))
    put("head_sum", (p[:, None] // DH == p[None, :] // DH) * 1.0)
    put("ident", np.eye(P))
    put("eye64", (p[:, None] % CH == np.arange(CH)[None, :]) * 1.0)
    row = (p % CH)[:, None]
    col = np.arange(CH)[None, :]
    fwd_st, bwd_st = (row < col) * 1.0, (row > col) * 1.0
    fwd_in, bwd_in = (row <= col) * 1.0, (row >= col) * 1.0
    same = (row // 16 == col // 16) * 1.0
    two = lambda f, b: [f, f, b, b]
    put("mask_zr", np.concatenate([np.concatenate(x, 1) for x in
                                   [(fwd_st, fwd_in)] * 2 + [(bwd_st, bwd_in)] * 2], 1))
    put("mask_dt", np.concatenate(two(fwd_st * same, bwd_st * same), 1))
    put("mask_d", np.concatenate(two(bwd_st * same, fwd_st * same), 1))
    put("mask_l", np.concatenate(two(bwd_st * (1 - same), fwd_st * (1 - same)), 1))
    put("not_first", np.tile((np.arange(T) % CH != 0) * 1.0, (P, 1)))
    f = p % DH
    axis, half, freq = f // 32, (f % 32) // 16, f % 16
    inv = (1.0 / (10000.0 ** (np.arange(16, dtype=np.float32) * np.float32(2.0) / np.float32(32)))).astype(np.float32)
    tok = np.arange(LAT)
    pos = np.where(axis[:, None] == 0, tok[None, :] // 64, tok[None, :] % 64).astype(np.float32)
    ang = pos * inv[freq][:, None]
    put("cos", np.cos(ang).astype(np.float32))
    put("sin", (np.sin(ang) * np.where(half == 0, -1.0, 1.0)[:, None]).astype(np.float32))
    partner = np.where(half == 0, p + 16, p - 16)
    put("swap", (p[:, None] == partner[None, :]) * 1.0)
    qc, kc = (p % 64)[:, None], np.arange(64)[None, :]
    ws = np.clip(qc - 8, 0, 48)
    inside = (kc >= ws) & (kc < ws + 16)
    put("win", inside * 1.0)
    put("out_win", np.where(inside, 0.0, NEG))
    put("sel", np.concatenate([(p[0:8, None] == e) * np.ones((1, P)) for e in range(4)], 1))
    lo, _ = CON["eps"]
    for at, v in ((EPS_RMS, 1e-6), (EPS_LN, 1e-5), (EPS_GN, 64e-5), (EPS_KK, 1e-12)):
        c[:, lo + at] = v
    put("ones", np.ones((P, P)))
    put("before", (p[:, None] < p[None, :]) * 1.0)
    put("slot", np.tile(np.arange(P) * 1.0, (P, 1)))
    put("mean_cv", np.full((P, P), 1.0 / 256))
    put("iota", np.tile(np.arange(8.0), (P, 1)))
    return c


class Steps:

    def __init__(self, signal, names):
        self.s, self.names, self.i = signal, names, 0

        self.h = signal.h

    def one(self, name):
        assert self.names[self.i] == name, (self.names[self.i], name)
        self.i += 1
        return self.s.one()

    def at(self, name):
        return self.s.at(self.names.index(name) + 1)


class Signal:

    def __init__(self, handle):
        self.h, self.n, self.m = handle, 0, 0

    def one(self, times=1):
        self.m += times
        return 1

    def at(self, k):
        return max(self.n + k, 0) if isinstance(k, int) else k + self.n


def build(nc, parts, xt_in, ct_in, con_in, par1_in, par2_in, lora_in, gate2_in, router_in, bias_in,
          sgw_in, sgb_in, out):
    ctx = ExitStack()
    sb = lambda name, cols: ctx.enter_context(nc.sbuf_tensor(name, [P, cols], F32))
    sems = {}

    def S(name):
        if name not in sems:
            sems[name] = Signal(ctx.enter_context(nc.semaphore(name)))
        return sems[name]

    x_buf = sb("x_buf", KT * T)
    h_buf = sb("h_buf", KT * T)
    mix_buf = sb("mix_buf", KT * T)
    ring = sb("ring", RING * PART)
    con = sb("constants", CON_COLS)
    par1 = [sb(f"par1_{l}", P1_COLS) for l in range(DEPTH)]
    par2 = [sb(f"par2_{l}", P2_COLS) for l in range(DEPTH)]
    modv = [sb(f"modv_{l}", 48 * 2) for l in range(DEPTH)]
    scal = [sb(f"scal_{l}", 44) for l in range(DEPTH)]
    mod_rows = sb("mod_rows", 2 * UNIT)
    passes = ctx.enter_context(nc.sbuf_tensor("passes", [P, 1], mybir.dt.int32))
    ct = sb("condition_buf", KT * 2)
    arena = sb("arena", 22560)
    banks = ctx.enter_context(nc.psum_tensor("banks", [P, 8 * 512], F32))

    again = lambda t, name, cols: nc.alloc_sbuf_tensor_at(name, [P, cols], F32R, offset=nc.lookup_mloc(t).addr)
    h_split = again(h_buf, "h_split", KT * T)
    mix_split = again(mix_buf, "mix_split", KT * T)
    ring_split = again(ring, "ring_split", RING * PART)
    arena_split = again(arena, "arena_split", 22560)

    v3 = lambda a, n: a.rearrange("p (a b) -> p a b", a=n)
    xT, hT, mixT = (v3(b[:, :], KT) for b in (x_buf, h_buf, mix_buf))
    bank = lambda i: banks[:, i * 512:(i + 1) * 512]
    C = lambda name: con[:, CON[name][0]:CON[name][1]]
    Q1 = lambda l, name, i: par1[l][:, P1[name][0] + i:P1[name][0] + i + 1]
    Q2 = lambda l, name, i: par2[l][:, P2[name][0] + i:P2[name][0] + i + 1]
    eps = lambda i: con[:, CON["eps"][0] + i:CON["eps"][0] + i + 1]
    mod3 = [v3(m[:, :], 48) for m in modv]
    slots = v3(ring[:, :], RING)
    low_slots = v3(ring_split[:, :], RING)

    class Arena:

        def __init__(self, at=0, buf=None, size=22560):
            self.at, self.buf, self.size = at, buf or arena, size

        def take(self, cols, n=None):
            a = self.buf[:, self.at:self.at + cols]
            self.at += cols
            assert self.at <= self.size, self.at
            return v3(a, n) if n else a

        def take_split(self, cols, n=None):
            a = arena_split[:, self.at:self.at + cols]
            self.take(cols)
            return v3(a, n) if n else a

    block = ctx.enter_context(nc.Block())
    loaded = [S(f"part_loaded_{i}") for i in range(RING)]
    used = S("parts_used")
    stream = {"put": 0, "got": 0, "skew": 0}

    phase = {"n": 0}

    def end_phase():
        phase["n"] += 1
        met = S("phase_met")
        goal = 4 * phase["n"]

        def meet(eng):
            eng.drain().then_inc(met.h, met.one())
            eng.wait_ge(met.h, goal)

        @block.tensor
        def _(pe):
            meet(pe)

        @block.scalar
        def _(act):
            meet(act)

        @block.vector
        def _(dve):
            meet(dve)

        @block.gpsimd
        def _(pool):
            meet(pool)
        for s in sems.values():
            if s not in loaded and s is not used:
                s.n = s.m

    def load_parts(sp, count):
        for _ in range(count):
            n = stream["put"]
            if n >= RING:
                sp.wait_ge(used.h, n - RING + 1)
            sp.dma_start(slots[:, n % RING, :], parts[n - stream["skew"], :, :]).then_inc(loaded[n % RING].h, 16)
            stream["put"] += 1

    def load_looped(sp, trips):
        n0 = stream["put"]
        with sp.Fori(0, trips) as i:
            for j in range(RING):
                n = n0 + j
                sp.wait_ge(used.h, i * RING + (n - RING + 1))
                sp.dma_start(slots[:, n % RING, :], parts[bass.ds(i * RING + (n - stream["skew"]), 1), :, :]
                             .rearrange("a p n -> p (a n)")).then_inc(loaded[n % RING].h, 16)
        stream["put"] += trips * RING

    def take_part(pe, n, i=None):
        goal = 16 * (n // RING + 1)
        pe.wait_ge(loaded[n % RING].h, goal if i is None else i * 16 + goal)
        return slots[:, n % RING, :]

    w_high, w_low = S("weight_high"), S("weight_low")

    def split_high(act, high, n, m, i=None, times=1):
        goal, depth = 16 * (n // RING + 1), high.shape[1]
        act.wait_ge(loaded[n % RING].h, goal if i is None else i * 16 + goal)
        if i is not None:
            act.wait_ge(used.h, i * RING + (n - depth + 1))
        elif m >= depth:
            act.wait_ge(used.h, n - depth + 1)
        act.activation(high[:, m % depth, :], slots[:, n % RING, :], ACT.Copy).then_inc(w_high.h, w_high.one(times))

    def split_low(dve, high, n, m, i=None, times=1):
        dve.wait_ge(w_high.h, w_high.at(m + 1) if i is None else w_high.at(i * RING + (m + 1)))
        dve.tensor_tensor(low_slots[:, n % RING, :], slots[:, n % RING, :], high[:, m % high.shape[1], :].bitcast(F32),
                          ALU.subtract).then_inc(w_low.h, w_low.one(times))

    def take_split_part(pe, high, n, m, i=None):
        pe.wait_ge(w_low.h, w_low.at(m + 1) if i is None else w_low.at(i * RING + (m + 1)))
        return high[:, m % high.shape[1], :], low_slots[:, n % RING, :]

    halves_of = {"h": (hT, v3(mix_split[:, :], KT), v3(h_split[:, :], KT)),
                 "mix": (mixT, v3(h_split[:, :], KT), v3(mix_split[:, :], KT))}
    t_high, t_low = S("tokens_high"), S("tokens_low")

    def tokens_high(act, which, cols):
        plain, high, _ = halves_of[which]
        for k in range(KT):
            act.activation(high[:, k, cols[0]:cols[1]], plain[:, k, cols[0]:cols[1]], ACT.Copy).then_inc(t_high.h, t_high.one())

    def tokens_low(dve, which, cols):
        plain, high, low = halves_of[which]
        for k in range(KT):
            dve.wait_ge(t_high.h, t_high.at(k + 1))
            dve.tensor_tensor(low[:, k, cols[0]:cols[1]], plain[:, k, cols[0]:cols[1]],
                              high[:, k, cols[0]:cols[1]].bitcast(F32), ALU.subtract).then_inc(t_low.h, t_low.one())

    def norm(src, dst, cols, gain, shift, name):
        lo, hi = cols
        n = hi - lo
        streams = [s for s in range(2) if lo <= s * CTX < hi]
        a = Arena()
        sq, sd, rs = a.take(KT * n, KT), a.take(n), a.take(n)
        sq_done, ms_done, sd_done, rs_done, t_done, h_done = (
            S(f"norm_{x}") for x in ("squared", "mean", "root", "inverse", "scaled", "shifted"))

        @block.scalar
        def _(act):
            for k in range(KT):
                act.activation(sq[:, k, :], src[:, k, lo:hi], ACT.Square).then_inc(sq_done.h, sq_done.one())
            act.wait_ge(ms_done.h, ms_done.at(1))
            act.activation(sd, bank(0)[:, 0:n], ACT.Sqrt, bias=eps(EPS_RMS)).then_inc(sd_done.h, sd_done.one())
            if shift:
                for k in range(KT):
                    for j, s in enumerate(streams):
                        act.wait_ge(t_done.h, t_done.at(k * len(streams) + j + 1))
                        y = dst[:, k, s * CTX:(s + 1) * CTX]
                        act.activation(y, y, ACT.Identity, bias=shift(k, s)).then_inc(h_done.h, h_done.one())

        @block.tensor
        def _(pe):
            for k in range(KT):
                pe.wait_ge(sq_done.h, sq_done.at(k + 1))
                mm = pe.matmul(bank(0)[:, 0:n], C("mean_d"), sq[:, k, :], start=k == 0, stop=k == KT - 1)
            mm.then_inc(ms_done.h, ms_done.one())

        @block.vector
        def _(dve):
            dve.wait_ge(sd_done.h, sd_done.at(1))
            dve.reciprocal(rs, sd).then_inc(rs_done.h, rs_done.one())
            dve.wait_ge(rs_done.h, rs_done.at(1))
            for k in range(KT):
                for s in streams:
                    c = slice(s * CTX, (s + 1) * CTX)
                    r = slice(s * CTX - lo, (s + 1) * CTX - lo)
                    dve.scalar_tensor_tensor(dst[:, k, c], src[:, k, c], gain(k, s), rs[:, r],
                                                        ALU.mult, ALU.mult).then_inc(t_done.h, t_done.one())
        end_phase()

    class Modulation:

        def __init__(self, runs):
            self.runs = runs
            self.tiles = [(l, t) for l, lo, hi in runs for t in range(lo, hi)]
            self.n, self.first = len(self.tiles) // 2, stream["got"]
            self.copied, self.turned, self.next = S("mod_row_copied"), S("mod_turned"), 0
            self.rows = v3(mod_rows[:, :], 2)
            stream["got"] += self.n

        def turn(self, pe, m):
            for j in range(2):
                at = 256 + 2 * (2 * m + j)
                mm = pe.transpose(bank(7)[:, at:at + 2], self.rows[0:2, m % 2, j * P:(j + 1) * P],
                                  con[0:2, CON["ident"][0]:CON["ident"][0] + 2])
            return mm

        def half(self, pe):
            m, second = divmod(self.next, 2)
            self.next += 1
            if m >= self.n:
                return
            if not second and m:
                pe.wait_ge(self.copied.h, self.copied.at(m))
                self.turn(pe, m - 1)
            w = v3(take_part(pe, self.first + m), KT)
            c3 = v3(ct[:, :], KT)
            for k in range(4 * second, 4 * second + 4):
                mm = pe.matmul(bank(7)[0:2, 0:UNIT], c3[:, k, :], w[:, k, :], start=k == 0, stop=k == KT - 1)
            if second:
                mm.then_inc(used.h, used.one())

        def last(self, pe):
            pe.wait_ge(self.copied.h, self.copied.at(self.n))
            self.turn(pe, self.n - 1).then_inc(self.turned.h, self.turned.one())

        def copy(self, act, m):
            act.wait_ge(used.h, self.first + m + 1)
            act.activation(self.rows[0:2, m % 2, :], bank(7)[0:2, 0:UNIT], ACT.Copy)\
                .then_inc(self.copied.h, self.copied.one())

        def store(self, dve):
            biased, gained = S("mod_biased"), S("mod_gains")
            dve.wait_ge(self.turned.h, self.turned.at(1))
            at = 0
            for l, lo, hi in self.runs:
                acc = v3(bank(7)[:, 256 + 2 * at:256 + 2 * (at + hi - lo)], hi - lo)
                at += hi - lo
                b = par1[l][:, P1["mod_b"][0] + lo:P1["mod_b"][0] + hi]
                for s in range(2):
                    dve.tensor_tensor(mod3[l][:, lo:hi, s], acc[:, :, s], b, ALU.add).then_inc(biased.h, biased.one())
                dve.wait_ge(biased.h, biased.m)
                for i, name in enumerate(("norm1_g", "norm2_g")):
                    t = 24 * i + 8
                    if not lo <= t < hi:
                        continue
                    g = par1[l][:, P1[name][0]:P1[name][1]]
                    for s in range(2):
                        o = v3(scal[l][:, i * 16:(i + 1) * 16], 8)[:, :, s]
                        dve.scalar_tensor_tensor(o, mod3[l][:, t:t + 8, s], 1.0, g, ALU.add, ALU.mult)\
                            .then_inc(gained.h, gained.one())

    def modulation(runs, late):
        mod = Modulation(runs)

        @block.sync
        def _(sp):
            load_parts(sp, mod.n)

        @block.tensor
        def _(pe):
            for _ in range(2 * mod.n):
                mod.half(pe)
            mod.last(pe)

        @block.scalar
        def _(act):
            for m in range(mod.n):
                mod.copy(act, m)
            act.wait_ge(late.h, 16 * 3)

        @block.vector
        def _(dve):
            tok, fin = S("shift_weight"), S("shift_rest")
            for l in range(DEPTH):
                c0 = scal[l][:, 32:42]
                mp = par1[l][:, P1["mu_prev"][0]:P1["mu_prev"][1]]
                mn = par1[l][:, P1["mu_next"][0]:P1["mu_next"][1]]
                ka = par1[l][:, P1["k_a"][0]:P1["k_a"][1]]
                dve.tensor_tensor(c0, mp, mn, ALU.add).then_inc(tok.h, tok.one())
                dve.wait_ge(tok.h, tok.m)
                dve.tensor_scalar(c0, c0, -1.0, 1.0, ALU.mult, ALU.add).then_inc(fin.h, fin.one())
                dve.tensor_scalar(scal[l][:, 42:44], ka, -1.0, 1.0, ALU.mult, ALU.add).then_inc(fin.h, fin.one())
            mod.store(dve)
        end_phase()

    gain1 = lambda l: lambda k, s: scal[l][:, 2 * k + s:2 * k + s + 1]
    gain2 = lambda l: lambda k, s: scal[l][:, 16 + 2 * k + s:16 + 2 * k + s + 1]
    modc = lambda l, t, s: mod3[l][:, t, s:s + 1]

    def project(tiles, which, cols, high):
        ready, free = S("tile_ready"), {"act": S("tile_free_act"), "dve": S("tile_free_dve")}
        first = stream["got"]
        n_parts = tiles[-1]["part"] + 1
        closes = [t + 1 == len(tiles) or tiles[t + 1]["part"] != tiles[t]["part"] for t in range(len(tiles))]

        _, x_high, x_low = halves_of[which]
        depth = high.shape[1]

        @block.sync
        def _(sp):
            load_parts(sp, n_parts)

        @block.scalar
        def _(act):
            split_high(act, high, first, 0)
            tokens_high(act, which, cols)
            for m in range(1, depth):
                split_high(act, high, first + m, m)

        @block.vector
        def _(dve):
            split_low(dve, high, first, 0)
            tokens_low(dve, which, cols)
            for m in range(1, depth):
                split_low(dve, high, first + m, m)

        def next_high(act, t):
            m = tiles[t]["part"] + depth
            if closes[t] and m < n_parts:
                split_high(act, high, first + m, m)

        def next_low(dve, t):
            m = tiles[t]["part"] + depth
            if closes[t] and m < n_parts:
                split_low(dve, high, first + m, m)

        @block.tensor
        def _(pe):
            freed = {"act": 0, "dve": 0}
            part = -1
            for t, tile in enumerate(tiles):
                if tile["part"] != part:
                    part = tile["part"]
                    wh, wl = (v3(w, KT) for w in take_split_part(pe, high, first + part, part))
                if t >= 8:
                    o = tiles[t - 8]["owner"]
                    freed[o] += 1
                    pe.wait_ge(free[o].h, free[o].at(freed[o]))
                for k in range(KT):
                    if t == 0:
                        pe.wait_ge(t_low.h, t_low.at(k + 1))
                    if "tok" in tile:
                        c = slice(tile["tok"] * P, (tile["tok"] + 1) * P)
                        o = bank(t % 8)[:, 0:UNIT]
                        pairs = [(x[:, k, c], w[:, k, :]) for x, w in ((x_high, wh), (x_high, wl), (x_low, wh))]
                    else:
                        lo, hi = tile["cols"]
                        c = slice(tile["j"] * P, (tile["j"] + 1) * P)
                        o = bank(t % 8)[:, 0:hi - lo]
                        pairs = [(w[:, k, c], x[:, k, lo:hi]) for w, x in ((wh, x_high), (wh, x_low), (wl, x_high))]
                    for n, (left, right) in enumerate(pairs):
                        mm = pe.matmul(o, left, right, start=k == 0 and n == 0, stop=k == KT - 1 and n == 2)
                mm.then_inc((used if closes[t] else ready).h, (used if closes[t] else ready).one())
        stream["got"] += n_parts

        def tile_done(t):
            if closes[t]:
                return used.h, first + tiles[t]["part"] + 1
            return ready.h, ready.at(sum(not c for c in closes[:t + 1]))
        return tile_done, free, next_high, next_low

    class Taps:

        def __init__(self, l, glu, lo_seq, at):
            a = Arena(at)
            self.l, self.glu, self.lo_seq, self.next = l, glu, lo_seq, 0
            self.acc = [a.take((2 - lo_seq) * CTX, 2 - lo_seq) for _ in range(2)]
            self.at = a.at

        def some(self, dve, count):
            tap, acc = S("cv_tap"), self.acc
            for t in range(self.next, min(self.next + count, CV_TAPS)):
                for i in range(2):
                    src = self.glu[:, i, self.lo_seq:2, t:t + CTX]
                    if t >= 1:
                        dve.wait_ge(tap.h, tap.at(2 * (t - 1) + i + 1))
                    wt = Q1(self.l, "cv_w", 2 * t + i)
                    if t == 0:
                        dve.tensor_scalar(acc[i], src, wt, Q1(self.l, "cv_b", i), ALU.mult, ALU.add).then_inc(tap.h, tap.one())
                    else:
                        dve.scalar_tensor_tensor(acc[i], src, wt, acc[i], ALU.mult, ALU.add).then_inc(tap.h, tap.one())
            self.next = min(self.next + count, CV_TAPS)

    def conformer(l, taps, lo_seq):
        a, acc = Arena(taps.at), taps.acc
        n = (2 - lo_seq) * CTX
        assert taps.next == CV_TAPS
        sq, sd = a.take(2 * n, 2), a.take(n)
        flat = lambda x: x.rearrange("p s t -> p (s t)")
        fin = S("cv_step")
        V_ = Steps(fin, ["d0", "d1", "inv", "n0", "n1", "g0", "g1"])
        A_ = Steps(S("cv_act"), ["sq0", "sq1", "root", "o0", "o1"])
        P_ = Steps(S("cv_pe"), ["mean", "var"])

        @block.vector
        def _(dve):
            dve.wait_ge(P_.h, P_.at("mean"))
            for i in range(2):
                dve.tensor_tensor(flat(acc[i]), flat(acc[i]), bank(0)[:, 0:n], ALU.subtract).then_inc(V_.h, V_.one(f"d{i}"))
            dve.wait_ge(A_.h, A_.at("root"))
            dve.reciprocal(sd, sd).then_inc(V_.h, V_.one("inv"))
            dve.wait_ge(fin.h, fin.m)
            for i in range(2):
                dve.tensor_tensor(flat(acc[i]), flat(acc[i]), sd, ALU.mult).then_inc(V_.h, V_.one(f"n{i}"))
            dve.wait_ge(fin.h, fin.m)
            for i in range(2):
                dve.tensor_scalar(flat(acc[i]), flat(acc[i]), Q1(l, "cv_g", i), Q1(l, "cv_beta", i),
                                                   ALU.mult, ALU.add).then_inc(V_.h, V_.one(f"g{i}"))

        @block.tensor
        def _(pe):
            for i in range(2):
                mm = pe.matmul(bank(0)[:, 0:n], C("mean_cv"), flat(acc[i]), start=i == 0, stop=i == 1)
            mm.then_inc(P_.h, P_.one("mean"))
            pe.wait_ge(A_.h, A_.at("sq1"))
            for i in range(2):
                mm = pe.matmul(bank(1)[:, 0:n], C("mean_cv"), sq[:, i, :], start=i == 0, stop=i == 1)
            mm.then_inc(P_.h, P_.one("var"))

        @block.scalar
        def _(act):
            for i in range(2):
                act.wait_ge(V_.h, V_.at(f"d{i}"))
                act.activation(sq[:, i, :], flat(acc[i]), ACT.Square).then_inc(A_.h, A_.one(f"sq{i}"))
            act.wait_ge(P_.h, P_.at("var"))
            act.activation(sd, bank(1)[:, 0:n], ACT.Sqrt, bias=eps(EPS_LN)).then_inc(A_.h, A_.one("root"))
            for i in range(2):
                act.wait_ge(V_.h, V_.at(f"g{i}"))
                act.activation(mixT[:, 6 + i, lo_seq * CTX:T], flat(acc[i]), ACT.Silu).then_inc(A_.h, A_.one(f"o{i}"))
        end_phase()

    def attention(units, q, k, v, scale, qwide, k_tile, v_col, at, taps=None):
        per = qwide // P
        a = Arena(at)
        nk_max = max(len(u[4]) for u in units) * P
        pr = a.take(3 * nk_max, 3)
        ptr = [v3(x, nk_max // P) for x in (a.take(nk_max // P * qwide), a.take(nk_max // P * qwide))]
        st = a.take(3 * 4, 3)
        s_ok, m_ok, e_ok, n_ok, t_ok, c_ok, o_ok, w_ok, mm_ok, ri_ok = (S(f"attn_{x}") for x in (
            "scores", "max", "exp", "probs", "probs_turned", "turned_copied", "out", "out_copied",
            "rowmax", "inverse"))
        N = len(units)
        score_bank = lambda i: bank((0, 1, 6)[i % 3])

        @block.tensor
        def _(pe):
            def scores(i):
                tile, half, qc, kcols, vt, bias, _ = units[i]
                hs = slice(half * DH, half * DH + DH)
                if i >= 3:
                    pe.wait_ge(e_ok.h, e_ok.at(i - 2))
                at = 0
                for lo, hi in kcols:
                    b = bias if at == 0 else None
                    mm = pe.matmul(score_bank(i)[:, at:at + hi - lo], q[hs, tile, qc:qc + P], k[hs, k_tile(tile), lo:hi],
                                   start=True, stop=b is None)
                    if b is not None:
                        mm = pe.matmul(score_bank(i)[:, at:at + hi - lo], C("ident"), b, start=False, stop=True)
                    at += hi - lo
                mm.then_inc(s_ok.h, s_ok.one())

            def turn(i):
                pe.wait_ge(n_ok.h, n_ok.at(i + 1))
                if i >= 2:
                    pe.wait_ge(c_ok.h, c_ok.at(i - 1))
                for t in range(len(units[i][4])):
                    mm = pe.transpose(bank(2 + i % 2)[:, t * P:(t + 1) * P], pr[:, i % 3, t * P:(t + 1) * P], C("ident"))
                mm.then_inc(t_ok.h, t_ok.one())

            def values(g):
                tile, half, _, _, vt, _, _ = units[g * per]
                hs = slice(half * DH, half * DH + DH)
                pe.wait_ge(c_ok.h, c_ok.at((g + 1) * per))
                if g >= 2:
                    pe.wait_ge(w_ok.h, w_ok.at(g - 1))
                for t, tv in enumerate(vt):
                    vc = v_col(tile, half)
                    mm = pe.matmul(bank(4 + g % 2)[hs, 0:qwide], v[:, tv, vc:vc + DH], ptr[g % 2][:, t, :],
                                   start=t == 0, stop=t == len(vt) - 1)
                mm.then_inc(o_ok.h, o_ok.one())

            for i in range(N + 3):
                if i < N:
                    scores(i)
                if 2 <= i <= N + 1:
                    turn(i - 2)
                if i >= 3 and (i - 3) % per == per - 1:
                    values((i - 3) // per)

        @block.vector
        def _(dve):
            def top(i):
                nk = len(units[i][4]) * P
                dve.wait_ge(s_ok.h, s_ok.at(i + 1))
                if i >= 3:
                    dve.wait_ge(e_ok.h, e_ok.at(i - 2))
                dve.tensor_reduce(st[:, i % 3, 0:1], score_bank(i)[:, 0:nk], AX.X, ALU.max).then_inc(mm_ok.h, mm_ok.one())
                dve.wait_ge(mm_ok.h, mm_ok.at(i + 1))
                dve.tensor_scalar(st[:, i % 3, 1:2], st[:, i % 3, 0:1], -scale, None, ALU.mult).then_inc(m_ok.h, m_ok.one())

            def normalise(i):
                nk = len(units[i][4]) * P
                dve.wait_ge(e_ok.h, e_ok.at(i + 1))
                dve.reciprocal(st[:, i % 3, 3:4], st[:, i % 3, 2:3]).then_inc(ri_ok.h, ri_ok.one())
                dve.wait_ge(ri_ok.h, ri_ok.at(i + 1))
                dve.tensor_scalar(pr[:, i % 3, 0:nk], pr[:, i % 3, 0:nk], st[:, i % 3, 3:4], None, ALU.mult).then_inc(n_ok.h, n_ok.one())

            def copy_out(g):
                tile, half, _, _, _, _, oc = units[g * per]
                hs = slice(half * DH, half * DH + DH)
                dve.wait_ge(o_ok.h, o_ok.at(g + 1))
                dve.tensor_copy(mixT[hs, tile, oc:oc + qwide], bank(4 + g % 2)[hs, 0:qwide]).then_inc(w_ok.h, w_ok.one())

            for i in range(N + 5):
                if i < N:
                    top(i)
                if 1 <= i <= N:
                    normalise(i - 1)
                if i >= 4 and (i - 4) % per == per - 1 and (i - 4) // per < N // per:
                    copy_out((i - 4) // per)
                if taps:
                    taps.some(dve, 2)

        @block.scalar
        def _(act):
            def exp(i):
                nk = len(units[i][4]) * P
                act.wait_ge(m_ok.h, m_ok.at(i + 1))
                if i >= 3:
                    act.wait_ge(t_ok.h, t_ok.at(i - 2))
                    act.wait_ge(ri_ok.h, ri_ok.at(i - 2))
                act.activation(pr[:, i % 3, 0:nk], score_bank(i)[:, 0:nk], ACT.Exp, bias=st[:, i % 3, 1:2],
                                        scale=scale, accum_out=st[:, i % 3, 2:3]).then_inc(e_ok.h, e_ok.one())

            def copy_turned(i):
                nt = len(units[i][4])
                g, j = i // per, i % per
                act.wait_ge(t_ok.h, t_ok.at(i + 1))
                if g >= 2:
                    act.wait_ge(o_ok.h, o_ok.at(g - 1))
                act.activation(ptr[g % 2][:, 0:nt, j * P:(j + 1) * P], v3(bank(2 + i % 2)[:, 0:nt * P], nt),
                                        ACT.Copy).then_inc(c_ok.h, c_ok.one())

            for i in range(N + 2):
                if i < N:
                    exp(i)
                if i >= 2:
                    copy_turned(i - 2)
        end_phase()

    def out_project(cols, gate, n_parts=4):
        tiles = [dict(part=p, j=j, cols=cols, owner="dve") for p in range(n_parts) for j in range(2)]
        tile_done, free, next_high, next_low = project(tiles, "mix", cols, Arena().take_split(3 * PART, 3))
        lo, hi = cols

        @block.scalar
        def _(act):
            for t in range(len(tiles)):
                next_high(act, t)

        @block.vector
        def _(dve):
            for t in range(len(tiles)):
                dve.wait_ge(*tile_done(t))
                for s in range(2):
                    a, b = s * CTX, (s + 1) * CTX
                    if not lo <= a < hi:
                        continue
                    ps = bank(t % 8)[:, a - lo:b - lo]
                    if gate:
                        ins = dve.scalar_tensor_tensor(xT[:, t, a:b], ps, gate(t, s), xT[:, t, a:b], ALU.mult, ALU.add)
                    else:
                        ins = dve.tensor_tensor(xT[:, t, a:b], ps, xT[:, t, a:b], ALU.add)
                ins.then_inc(free["dve"].h, free["dve"].one())
                next_low(dve, t)
        end_phase()

    def feed_forward(kind, n_units, c0, residual, taps=None):
        a = Arena()
        sg, hid_at = a.take(2 * 512, 2), a.at
        hid = a.take(2 * 512, 2)
        hid_low, hid_high = Arena(hid_at).take_split(2 * 512, 2), a.take_split(2 * 512, 2)
        cen = a.take(2 * 1024, 2) if kind == "conv" else None
        high = a.take_split(3 * PART, 3)
        _, x_high, x_low = halves_of["h"]
        cols = (c0, c0 + 256)
        si, ac, ce, tq, hp, hh = (S(f"ff_{x}") for x in ("silu", "hidden", "centre_tap", "side_taps", "hidden_plain",
                                                         "hidden_high"))
        N = n_units
        B = stream["got"]
        y = lambda m: bank(4 + m // 2)[:, (m % 2) * 256:(m % 2 + 1) * 256]
        gate_bank, up_bank = (lambda u: bank(u % 2)), (lambda u: bank(2 + u % 2))
        looped = kind != "conv"
        trips = (n_units - 1) // 2 if looped else 0

        gate_of = lambda U: B + 3 * U if U else B + 1
        up_of = lambda U: B + 3 * U + 1 if U else B + 2

        def over_units(eng, body, start):
            rounds = trips - start if looped else 0
            for u in range(start):
                body(u, None, 1)
            if rounds:
                with eng.Fori(0, rounds) as i:
                    for j in range(2):
                        body(start + j, i, rounds)
            for u in range(start + 2 * rounds, n_units):
                body(u, None, 1)

        @block.sync
        def _(sp):
            load_parts(sp, 2)
            if trips:
                load_looped(sp, trips)
            load_parts(sp, 3 * (n_units - 2 * trips) - 2)

        def per(i, k, v):
            return v if i is None else i * k + v

        @block.tensor
        def _(pe):
            def products(U, m, i, times):
                for which, bk in enumerate((gate_bank(U), up_bank(U))):
                    wh, wl = (v3(w, KT) for w in take_split_part(pe, high, B + m + which, m + which, i))
                    if which == 0:
                        pe.wait_ge(ac.h, ac.at(per(i, 2, U + 1)))
                    for j in range(2):
                        for k in range(KT):
                            if m == 0 and which == 0 and j == 0:
                                pe.wait_ge(t_low.h, t_low.at(k + 1))
                            for n, (w, x) in enumerate(((wh, x_high), (wh, x_low), (wl, x_high))):
                                mm = pe.matmul(bk[:, j * 256:(j + 1) * 256], w[:, k, j * P:(j + 1) * P],
                                               x[:, k, c0:c0 + 256], start=k == 0 and n == 0, stop=k == KT - 1 and n == 2)
                    mm.then_inc(used.h, used.one(times))

            def down(U, m, i, times):
                wh, wl = (v3(w, 2) for w in take_split_part(pe, high, B + m, m, i))
                pe.wait_ge(ac.h, ac.at(per(i, 2, U + 3)))
                for j in range(2):
                    for t in range(KT):
                        for w, h in ((wh, hid_high), (wh, hid_low), (wl, hid_high)):
                            mm = pe.matmul(y(t), w[:, j, t * P:(t + 1) * P], h[:, U % 2, j * 256:(j + 1) * 256],
                                           start=False, stop=False, skip_group_check=True)
                mm.then_inc(used.h, used.one(times))

            pe.wait_ge(ac.h, ac.at(1))
            for b in range(4):
                pe.matmul(bank(4 + b), C("ident"), hid[:, 0, :], start=True, stop=False, skip_group_check=True)
            products(0, 0, None, 1)

            def body(U, i, times):
                m = 2 + 3 * U
                if U < N - 1:
                    products(U + 1, m, i, times)
                    down(U, m + 2, i, times)
                else:
                    down(U, m, i, times)
            over_units(pe, body, 0)

        @block.scalar
        def _(act):
            def split(m, i, times):
                if m < 3 * N:
                    split_high(act, high, B + m, m, i, times)

            def body(U, i, times):
                act.wait_ge(used.h, per(i, 6, gate_of(U)))
                act.wait_ge(ac.h, ac.at(per(i, 2, U + 1)))
                if kind == "conv":
                    for h in range(2):
                        if h:
                            if U:
                                split(3 * U + 2, i, times)
                            act.wait_ge(used.h, up_of(U))
                        for j in range(2):
                            bk = (gate_bank(U), up_bank(U))[h]
                            act.activation(cen[:, U % 2, (2 * h + j) * 256:(2 * h + j + 1) * 256],
                                                  bk[:, j * 256:(j + 1) * 256], ACT.Copy,
                                                  scale=taps(1, 22 * h + 2 * U + j)).then_inc(ce.h, ce.one())
                    split(3 * U + 3, i, times)
                    act.wait_ge(tq.h, tq.at(8 * U + 4))
                    act.activation(sg[:, U % 2, :], cen[:, U % 2, 0:512], ACT.Silu).then_inc(si.h, si.one())
                else:
                    act.activation(sg[:, U % 2, :], gate_bank(U), ACT.Silu).then_inc(si.h, si.one(times))
                    if U:
                        split(3 * U + 2, i, times)
                    split(3 * U + 3, i, times)
                act.wait_ge(hp.h, hp.at(per(i, 2, U + 1)))
                act.activation(hid_high[:, U % 2, :], hid[:, U % 2, :], ACT.Copy).then_inc(hh.h, hh.one(times))
                split(3 * U + 4, i, times)
            split(0, None, 1)
            tokens_high(act, "h", cols)
            split(1, None, 1)
            split(2, None, 1)
            over_units(act, body, 1)

        @block.vector
        def _(dve):
            def split(m, i, times):
                if m < 3 * N:
                    split_low(dve, high, B + m, m, i, times)

            for j in range(2):
                dve.memset(hid[:, j, :], 0.0).then_inc(ac.h, ac.one())
            split(0, None, 1)
            tokens_low(dve, "h", cols)
            split(1, None, 1)
            split(2, None, 1)

            def body(U, i, times):
                if U:
                    split(3 * U + 2, i, times)
                dve.wait_ge(used.h, per(i, 6, up_of(U)))
                if kind == "conv":
                    for h in range(2):
                        dve.wait_ge(ce.h, ce.at(4 * U + 2 * h + 2))
                        bk = (gate_bank(U), up_bank(U))[h]
                        for side in range(2):
                            if side:
                                dve.wait_ge(tq.h, tq.at(8 * U + 4 * h + 2))
                            for j in range(2):
                                c = cen[:, U % 2, (2 * h + j) * 256:(2 * h + j + 1) * 256]
                                p = bk[:, j * 256:(j + 1) * 256]
                                o, q = (c[:, 1:256], p[:, 0:255]) if side == 0 else (c[:, 0:255], p[:, 1:256])
                                dve.scalar_tensor_tensor(o, q, taps(2 * side, 22 * h + 2 * U + j), o,
                                                                ALU.mult, ALU.add).then_inc(tq.h, tq.one())
                    split(3 * U + 3, i, times)
                    dve.wait_ge(si.h, si.at(U + 1))
                    dve.wait_ge(tq.h, tq.at(8 * U + 8))
                    dve.tensor_tensor(hid[:, U % 2, :], cen[:, U % 2, 512:1024], sg[:, U % 2, :], ALU.mult)\
                        .then_inc(hp.h, hp.one())
                else:
                    dve.wait_ge(si.h, si.at(per(i, 2, U + 1)))
                    dve.tensor_tensor(hid[:, U % 2, :], up_bank(U), sg[:, U % 2, :], ALU.mult).then_inc(hp.h, hp.one(times))
                    split(3 * U + 3, i, times)
                dve.wait_ge(hh.h, hh.at(per(i, 2, U + 1)))
                dve.tensor_tensor(hid_low[:, U % 2, :], hid[:, U % 2, :], hid_high[:, U % 2, :].bitcast(F32),
                                  ALU.subtract).then_inc(ac.h, ac.one(times))
                split(3 * U + 4, i, times)
            over_units(dve, body, 1)
            dve.wait_ge(used.h, B + 3 * N)
            for m in range(KT):
                residual(dve, m, y(m))
        stream["got"] += 3 * N
        end_phase()

    def recurrence(l, us, at):
        big, hb = Arena(at), Arena(0, h_buf, KT * T)
        zr = big.take(4 * T * 2).rearrange("p (q c w t) -> p q c w t", q=4, c=NCH, w=2)
        bt, kt = hb.take(4 * T, 4), hb.take(4 * T, 4)
        gg, bon, pc = big.take(4 * T, 4), big.take(2 * T, 2), big.take(4 * NCH, 4)
        tmp_at = big.at
        lora, g2w, tw, sgd = big.take(512, 2), big.take(512, 2), big.take(T), big.take(T)
        lw, av, kk, ci, ce, ex, kd = (big.take(2 * T, 2) for _ in range(7))
        r, k, v = us[:, 0:2, :], us[:, 2:4, :], us[:, 4:6, :]
        by_chunk = lambda a: a.rearrange("p (c t) -> p c t", t=CH)
        chunks_of = lambda a: a.rearrange("p h (c t) -> p (h c) t", t=CH)
        lo_in = S("lora_loaded")

        @block.scalar
        def _(sp):
            sp.dma_start(lora, lora_in[l, :, :].rearrange("p (d n) -> p d n", d=2)).then_inc(lo_in.h, 16)
            sp.dma_start(g2w, gate2_in[l, :, :].rearrange("p (d n) -> p d n", d=2)).then_inc(lo_in.h, 16)

        an = ["sq0", "sq1", "root0", "root1"]
        vn = ["kk0", "kk1", "inv0", "inv1", "kkn0", "kkn1"]
        pn = ["kksum"]
        for d in range(2):
            an += [f"{x}{d}" for x in ("tanh", "sgd", "sw0", "sw1", "a0", "a1", "g", "ex", "ep", "en", "pc")]
            pn += [f"{x}{d}" for x in ("w", "g", "bonus")]
            vn += [f"{x}{d}" for x in ("lw", "scan0", "scan1", "excl", "incl", "z0", "z1", "r0", "r1", "b1", "b",
                                       "ka0", "ka1", "kd", "k", "rk0", "rk1", "bv", "bg")]
            vn += ["badd1"] * d
        A_, V_, P_ = Steps(S("rw_act"), an), Steps(S("rw_dve"), vn), Steps(S("rw_pe"), pn)

        @block.tensor
        def _(pe):
            pe.wait_ge(A_.h, A_.at("sq1"))
            for hp in range(2):
                mm = pe.matmul(bank(hp), C("head_sum"), ex[:, hp, :], start=True, stop=True)
            mm.then_inc(P_.h, P_.one("kksum"))
            pe.wait_ge(lo_in.h, 32 * (l + 1))
            for d in range(2):
                pe.wait_ge(A_.h, A_.at(f"tanh{d}"))
                for hp in range(2):
                    c = slice(hp * P, (hp + 1) * P)
                    pe.matmul(bank(2 + hp), lora[0:64, d, c], tw[0:64, :], start=True, stop=True)
                    mm = pe.matmul(bank(4 + hp), lora[64:128, d, c], us[64:128, 6 + 2 * d, :], start=True, stop=True)
                mm.then_inc(P_.h, P_.one(f"w{d}"))
                pe.wait_ge(A_.h, A_.at(f"sgd{d}"))
                for hp in range(2):
                    mm = pe.matmul(bank(6 + hp), g2w[:, d, hp * P:(hp + 1) * P], sgd, start=True, stop=True)
                mm.then_inc(P_.h, P_.one(f"g{d}"))
                pe.wait_ge(V_.h, V_.at(f"rk1{d}"))
                for hp in range(2):
                    mm = pe.matmul(bank(hp), C("head_sum"), av[:, hp, :], start=True, stop=True)
                mm.then_inc(P_.h, P_.one(f"bonus{d}"))

        @block.scalar
        def _(act):
            for hp in range(2):
                act.wait_ge(V_.h, V_.at(f"kk{hp}"))
                act.activation(ex[:, hp, :], kk[:, hp, :], ACT.Square).then_inc(A_.h, A_.one(f"sq{hp}"))
            act.wait_ge(P_.h, P_.at("kksum"))
            for hp in range(2):
                act.activation(ce[:, hp, :], bank(hp), ACT.Sqrt, bias=eps(EPS_KK)).then_inc(A_.h, A_.one(f"root{hp}"))
            for d in range(2):
                if d:
                    act.wait_ge(P_.h, P_.at("g0"))
                    act.wait_ge(V_.h, V_.at("bg0"))
                act.activation(tw[0:64, :], us[0:64, 6 + 2 * d, :], ACT.Tanh).then_inc(A_.h, A_.one(f"tanh{d}"))
                act.activation(sgd, us[:, 7 + 2 * d, :], ACT.Sigmoid).then_inc(A_.h, A_.one(f"sgd{d}"))
                act.wait_ge(P_.h, P_.at(f"w{d}"))
                for hp in range(2):
                    act.activation(lw[:, hp, :], bank(2 + hp), ACT.Sigmoid,
                                                         bias=Q1(l, "w0", 2 * d + hp)).then_inc(A_.h, A_.one(f"sw{hp}{d}"))
                for hp in range(2):
                    act.activation(av[:, hp, :], bank(4 + hp), ACT.Sigmoid,
                                                        bias=Q1(l, "a0", 2 * d + hp)).then_inc(A_.h, A_.one(f"a{hp}{d}"))
                act.wait_ge(P_.h, P_.at(f"g{d}"))
                act.activation(gg[:, 2 * d:2 * d + 2, :], v3(banks[:, 6 * 512:8 * 512], 2), ACT.Copy).then_inc(A_.h, A_.one(f"g{d}"))
                act.wait_ge(V_.h, V_.at(f"incl{d}"))
                act.activation(ex, ce, ACT.Exp).then_inc(A_.h, A_.one(f"ex{d}"))
                act.wait_ge(A_.h, A_.at(f"ex{d}"))
                act.activation(ce, ci, ACT.Exp).then_inc(A_.h, A_.one(f"ep{d}"))
                act.wait_ge(V_.h, V_.at(f"z1{d}"))
                act.activation(ex, ci, ACT.Exp, scale=-1.0).then_inc(A_.h, A_.one(f"en{d}"))
                edge = CH - 1 if d == 0 else 0
                act.activation(pc[:, 2 * d:2 * d + 2, :],
                                                 ci.rearrange("p h (c t) -> p h c t", t=CH)[:, :, :, edge], ACT.Exp).then_inc(A_.h, A_.one(f"pc{d}"))

        @block.vector
        def _(dve):
            me = V_.s
            for hp in range(2):
                dve.tensor_scalar(kk[:, hp, :], k[:, hp, :], Q1(l, "k_k", hp), None, ALU.mult).then_inc(V_.h, V_.one(f"kk{hp}"))
            for hp in range(2):
                dve.wait_ge(A_.h, A_.at(f"root{hp}"))
                dve.reciprocal(ce[:, hp, :], ce[:, hp, :]).then_inc(V_.h, V_.one(f"inv{hp}"))
            dve.wait_ge(me.h, me.m)
            for hp in range(2):
                dve.tensor_tensor(kk[:, hp, :], kk[:, hp, :], ce[:, hp, :], ALU.mult).then_inc(V_.h, V_.one(f"kkn{hp}"))
            for d in range(2):
                dve.wait_ge(A_.h, A_.at(f"sw1{d}"))
                dve.tensor_scalar(lw, lw, -float(np.exp(-0.5)), None, ALU.mult).then_inc(V_.h, V_.one(f"lw{d}"))
                dve.wait_ge(me.h, me.m)
                for hp in range(2):
                    dve.tensor_tensor_scan(ci[:, hp, :], C("not_first"), lw[:, hp, :], 0.0,
                                                                   ALU.mult, ALU.add).then_inc(V_.h, V_.one(f"scan{hp}{d}"))
                dve.wait_ge(me.h, me.m)
                if d == 0:
                    dve.tensor_tensor(ce, ci, lw, ALU.subtract).then_inc(V_.h, V_.one("excl0"))
                    dve.tensor_copy(kd[:, 0, 0:1], ci[:, 0, 0:1]).then_inc(V_.h, V_.one("incl0"))
                else:
                    tot = chunks_of(ci)[:, :, CH - 1:CH].broadcast_to((P, 2 * NCH, CH))
                    dve.tensor_tensor(chunks_of(ce), tot, chunks_of(ci), ALU.subtract).then_inc(V_.h, V_.one("excl1"))
                    dve.wait_ge(me.h, me.m)
                    dve.tensor_tensor(ci, ce, lw, ALU.add).then_inc(V_.h, V_.one("incl1"))
                dve.wait_ge(A_.h, A_.at(f"ex{d}"))
                dve.wait_ge(me.h, me.m)
                for hp in range(2):
                    dve.scalar_tensor_tensor(zr[:, 2 * d + hp, :, 0, :], by_chunk(ex[:, hp, :]), -1.0,
                                                                  by_chunk(kk[:, hp, :]), ALU.mult, ALU.mult).then_inc(V_.h, V_.one(f"z{hp}{d}"))
                dve.wait_ge(A_.h, A_.at(f"ep{d}"))
                for hp in range(2):
                    dve.tensor_tensor(zr[:, 2 * d + hp, :, 1, :], by_chunk(ce[:, hp, :]),
                                                           by_chunk(r[:, hp, :]), ALU.mult).then_inc(V_.h, V_.one(f"r{hp}{d}"))
                dve.wait_ge(A_.h, A_.at(f"a1{d}"))
                dve.tensor_tensor(lw, kk, av, ALU.mult).then_inc(V_.h, V_.one(f"b1{d}"))
                dve.wait_ge(me.h, me.m)
                dve.wait_ge(A_.h, A_.at(f"en{d}"))
                dve.tensor_tensor(bt[:, 2 * d:2 * d + 2, :], lw, ex, ALU.mult).then_inc(V_.h, V_.one(f"b{d}"))
                for hp in range(2):
                    dve.tensor_scalar(kd[:, hp, :], av[:, hp, :], Q1(l, "k_a", hp),
                                                            scal[l][:, 42 + hp:43 + hp], ALU.mult, ALU.add).then_inc(V_.h, V_.one(f"ka{hp}{d}"))
                dve.wait_ge(me.h, me.m)
                dve.tensor_tensor(kd, kd, k, ALU.mult).then_inc(V_.h, V_.one(f"kd{d}"))
                dve.wait_ge(me.h, me.m)
                dve.tensor_tensor(kt[:, 2 * d:2 * d + 2, :], kd, ex, ALU.mult).then_inc(V_.h, V_.one(f"k{d}"))
                for hp in range(2):
                    dve.scalar_tensor_tensor(av[:, hp, :], r[:, hp, :], Q1(l, "r_k", hp),
                                                                   kd[:, hp, :], ALU.mult, ALU.mult).then_inc(V_.h, V_.one(f"rk{hp}{d}"))
                dve.wait_ge(P_.h, P_.at(f"bonus{d}"))
                dve.tensor_tensor(av, v3(banks[:, 0:1024], 2), v, ALU.mult).then_inc(V_.h, V_.one(f"bv{d}"))
                dve.wait_ge(me.h, me.m)
                dve.wait_ge(A_.h, A_.at(f"pc{d}"))
                if d == 0:
                    dve.tensor_tensor(bon, av, gg[:, 0:2, :], ALU.mult).then_inc(V_.h, V_.one("bg0"))
                else:
                    dve.tensor_tensor(av, av, gg[:, 2:4, :], ALU.mult).then_inc(V_.h, V_.one("bg1"))
                    dve.wait_ge(me.h, me.m)
                    dve.tensor_tensor(bon, bon, av, ALU.add).then_inc(V_.h, V_.one("badd1"))
        end_phase()

        gb = Arena(tmp_at)
        lo = v3(us[:, 6:10, :].rearrange("p a b -> p (a b)"), 4)
        take = lambda: gb.take(512, 8)
        DT, DD, LL, MB, AK, MK, BS, KS, VS, D2, D2T, D4, D4T, E1, E2, DI, N1, GG_, TI = (take() for _ in range(19))
        X = gb.take(512, 2)
        lo8 = [v3(lo[:, i, :], 8) for i in range(4)]
        NTb, N2, INT_ = lo8[0], lo8[1], lo8[2]
        RH, UU = v3(lo[:, 3, 0:256], 4), v3(lo[:, 3, 256:512], 4)
        D8, E3, E4 = D2T, E1, E2
        b8 = lambda i: v3(bank(i), 8)
        b4 = lambda i: v3(bank(i)[:, 0:256], 4)
        eye = C("eye64").rearrange("p (o t) -> p o t", o=1).broadcast_to((P, 8, CH))
        Y = us
        pn, vn, an = [], ["x0"], []
        for g in range(NCH // 2):
            pn += [f"{x}_{g}" for x in ("gram", "p1", "p2", "p3", "p4", "p5", "p6", "p7", "p8")]
            vn += [f"{x}_{g}" for x in ("dt0", "mb0", "dt1", "mb1", "ak0", "mk0", "ak1", "mk1", "d", "l", "e1", "d2", "d4", "e2",
                                        "e3", "e4", "nt", "int", "n2", "g")]
            an += [f"{x}_{g}" for x in ("bs", "ks", "d2t", "d4t", "vs", "d8", "di", "n", "ti")]
            for j in range(2):
                pn += [f"{x}_{g}{j}" for x in ("rhs", "u", "dx", "y")]
                vn += [f"{x}_{g}{j}" for x in ("u", "xa", "xb")]
                an += [f"{x}_{g}{j}" for x in ("rhs", "y0", "y1")]
        P_, V_, A_ = Steps(S("rc_pe"), pn), Steps(S("rc_dve"), vn), Steps(S("rc_act"), an)
        hs = [slice(0, 64), slice(64, 128)]
        mod = Modulation([(0, 16, 48), (1, 0, 48)]) if l == 0 else None
        fill = dict(gram=2, p1=2, p2=2, p3=2, p4=2, p5=1, p6=1, p7=1, p8=1, rhs0=1, u0=1, y0=1, rhs1=1, u1=1, y1=1)
        whole = {}
        h_at = 0
        for g in range(NCH // 2):
            for name, n in fill.items():
                whole[g, name] = [h // 2 for h in range(h_at, h_at + n) if h % 2]
                h_at += n

        def fill_pe(pe, name):
            if mod:
                for _ in range(fill[name]):
                    mod.half(pe)

        def fill_act(act, g, name):
            if mod:
                for m in whole[g, name]:
                    mod.copy(act, m)

        if mod:
            assert h_at == 2 * mod.n

            @block.sync
            def _(sp):
                load_parts(sp, mod.n)

        @block.tensor
        def _(pe):
            def products(out, left, right):
                for i in range(8):
                    for h in hs:
                        mm = pe.matmul(out[h, i, :], left[h, i, :], right[h, i, :], start=True, stop=True)
                return mm

            for g in range(NCH // 2):
                if g:
                    pe.wait_ge(A_.h, A_.at(f"y1_{g - 1}1"))
                    pe.wait_ge(V_.h, V_.at(f"xb_{g - 1}1"))
                for j in range(2):
                    for q in range(4):
                        c = CHUNKS[q // 2][2 * g + j]
                        cs = slice(c * CH, (c + 1) * CH)
                        i = 4 * j + q
                        for h in hs:
                            z_r = zr[h, q, c, :, :].rearrange("p w t -> p (w t)")
                            pe.matmul(bank(j)[h, q * 128:(q + 1) * 128], bt[h, q, cs], z_r, start=True, stop=True)
                            pe.matmul(bank(2 + j)[h, q * 128:(q + 1) * 128], kt[h, q, cs], z_r, start=True, stop=True)
                            pe.matmul(b8(4)[h, i, :], zr[h, q, c, 0, :], bt[h, q, cs], start=True, stop=True)
                            pe.matmul(b8(5)[h, i, :], bt[h, q, cs], eye[h, 0, :], start=True, stop=True)
                            mm = pe.matmul(b8(6)[h, i, :], kt[h, q, cs], eye[h, 0, :], start=True, stop=True)
                mm.then_inc(P_.h, P_.one(f"gram_{g}"))
                fill_pe(pe, "gram")
                pe.wait_ge(V_.h, V_.at(f"e1_{g}"))
                products(b8(0), DT, DD)
                products(b8(1), DD, DT).then_inc(P_.h, P_.one(f"p1_{g}"))
                fill_pe(pe, "p1")
                pe.wait_ge(V_.h, V_.at(f"d2_{g}"))
                pe.wait_ge(A_.h, A_.at(f"d2t_{g}"))
                products(b8(2), D2T, D2)
                products(b8(3), D2, D2T)
                for i in range(8):
                    c = CHUNKS[i % 4 // 2][2 * g + i // 4]
                    for h in hs:
                        pe.matmul(b8(5)[h, i, :], us[h, 4 + i % 2, c * CH:(c + 1) * CH], eye[h, 0, :], start=True, stop=True)
                products(b8(4), D2, E1).then_inc(P_.h, P_.one(f"p2_{g}"))
                fill_pe(pe, "p2")
                pe.wait_ge(V_.h, V_.at(f"e2_{g}"))
                pe.wait_ge(A_.h, A_.at(f"d4t_{g}"))
                products(b8(0), D4T, D4)
                products(b8(1), D4, E2).then_inc(P_.h, P_.one(f"p3_{g}"))
                fill_pe(pe, "p3")
                pe.wait_ge(V_.h, V_.at(f"e3_{g}"))
                pe.wait_ge(A_.h, A_.at(f"d8_{g}"))
                products(b8(2), D8, E3).then_inc(P_.h, P_.one(f"p4_{g}"))
                fill_pe(pe, "p4")
                pe.wait_ge(V_.h, V_.at(f"e4_{g}"))
                products(b8(3), E4, eye)
                products(b8(0), LL, E4)
                products(b8(1), E4, LL).then_inc(P_.h, P_.one(f"p5_{g}"))
                fill_pe(pe, "p5")
                pe.wait_ge(V_.h, V_.at(f"int_{g}"))
                pe.wait_ge(A_.h, A_.at(f"n_{g}"))
                products(b8(2), NTb, N1).then_inc(P_.h, P_.one(f"p6_{g}"))
                fill_pe(pe, "p6")
                pe.wait_ge(V_.h, V_.at(f"n2_{g}"))
                products(b8(3), N2, INT_).then_inc(P_.h, P_.one(f"p7_{g}"))
                fill_pe(pe, "p7")
                pe.wait_ge(V_.h, V_.at(f"g_{g}"))
                products(b8(4), DI, GG_).then_inc(P_.h, P_.one(f"p8_{g}"))
                fill_pe(pe, "p8")
                for j in range(2):
                    old = v3(X[:, j, :], 4)
                    if j or g:
                        pe.wait_ge(V_.h, V_.at(f"xb_{g if j else g - 1}{1 - j}"))
                    else:
                        pe.wait_ge(V_.h, V_.at("x0"))
                    at_c = [CHUNKS[q // 2][2 * g + j] for q in range(4)]
                    for q in range(4):
                        i = 4 * j + q
                        for h in hs:
                            pe.matmul(b4(5)[h, q, :], zr[h, q, at_c[q], 0, :], old[h, q, :], start=True, stop=False)
                            mm = pe.matmul(b4(5)[h, q, :], AK[h, i, :], VS[h, i, :], start=False, stop=True)
                    mm.then_inc(P_.h, P_.one(f"rhs_{g}{j}"))
                    fill_pe(pe, f"rhs{j}")
                    pe.wait_ge(A_.h, A_.at(f"ti_{g}"))
                    pe.wait_ge(A_.h, A_.at(f"rhs_{g}{j}"))
                    for q in range(4):
                        for h in hs:
                            mm = pe.matmul(b4(6)[h, q, :], TI[h, 4 * j + q, :], RH[h, q, :], start=True, stop=True)
                    mm.then_inc(P_.h, P_.one(f"u_{g}{j}"))
                    fill_pe(pe, f"u{j}")
                    pe.wait_ge(V_.h, V_.at(f"u_{g}{j}"))
                    for q in range(4):
                        i = 4 * j + q
                        for h in hs:
                            pe.matmul(b4(4)[h, q, :], BS[h, i, :], UU[h, q, :], start=True, stop=False)
                            mm = pe.matmul(b4(4)[h, q, :], KS[h, i, :], VS[h, i, :], start=False, stop=True)
                    mm.then_inc(P_.h, P_.one(f"dx_{g}{j}"))
                    for q in range(4):
                        i = 4 * j + q
                        for h in hs:
                            pe.matmul(b4(j)[h, q, :], old[h, q, :], zr[h, q, at_c[q], 1, :], start=True, stop=False)
                            pe.matmul(b4(j)[h, q, :], UU[h, q, :], MB[h, i, :], start=False, stop=False)
                            mm = pe.matmul(b4(j)[h, q, :], VS[h, i, :], MK[h, i, :], start=False, stop=True)
                    mm.then_inc(P_.h, P_.one(f"y_{g}{j}"))
                    fill_pe(pe, f"y{j}")
            if mod:
                mod.last(pe)

        @block.scalar
        def _(act):
            for g in range(NCH // 2):
                act.wait_ge(P_.h, P_.at(f"gram_{g}"))
                for name, b, o in (("bs", 5, BS), ("ks", 6, KS)):
                    act.activation(o, b8(b), ACT.Copy).then_inc(A_.h, A_.one(f"{name}_{g}"))
                fill_act(act, g, "gram")
                stages = ["p1", "p2", "p3", "p4", "p5", "p6", "p7", "p8"]
                for name, after, b, o in (("d2t", "p1", 1, D2T), ("d4t", "p2", 3, D4T), ("vs", "p2", 5, VS), ("d8", "p3", 0, D8),
                                          ("di", "p5", 3, DI), ("n", "p5", 1, N1), ("ti", "p8", 4, TI)):
                    while stages[0] != after:
                        fill_act(act, g, stages.pop(0))
                    act.wait_ge(P_.h, P_.at(f"{after}_{g}"))
                    act.activation(o, b8(b), ACT.Copy).then_inc(A_.h, A_.one(f"{name}_{g}"))
                for name in stages:
                    fill_act(act, g, name)
                for j in range(2):
                    act.wait_ge(P_.h, P_.at(f"rhs_{g}{j}"))
                    act.activation(RH, b4(5), ACT.Copy).then_inc(A_.h, A_.one(f"rhs_{g}{j}"))
                    fill_act(act, g, f"rhs{j}")
                    fill_act(act, g, f"u{j}")
                    act.wait_ge(P_.h, P_.at(f"y_{g}{j}"))
                    for d in range(2):
                        c = CHUNKS[d][2 * g + j]
                        act.activation(Y[:, 2 * d:2 * d + 2, c * CH:(c + 1) * CH],
                                                               b4(j)[:, 2 * d:2 * d + 2, :], ACT.Copy).then_inc(A_.h, A_.one(f"y{d}_{g}{j}"))
                    fill_act(act, g, f"y{j}")

        @block.vector
        def _(dve):
            dve.memset(X[:, :, :], 0.0).then_inc(V_.h, V_.one("x0"))
            mzr = C("mask_zr").rearrange("p (q w t) -> p q w t", q=4, w=2)
            mdt = v3(C("mask_dt"), 4)
            zr_of = lambda b: bank(b).rearrange("p (q w t) -> p q w t", q=4, w=2)
            mult = lambda o, a, b: dve.tensor_tensor(o, a, b, ALU.mult)
            add = lambda o, a, b: dve.tensor_tensor(o, a, b, ALU.add)
            for g in range(NCH // 2):
                dve.wait_ge(P_.h, P_.at(f"gram_{g}"))
                for j in range(2):
                    s = slice(4 * j, 4 * j + 4)
                    mult(DT[:, s, :], zr_of(j)[:, :, 0, :], mdt).then_inc(V_.h, V_.one(f"dt{j}_{g}"))
                    mult(MB[:, s, :], zr_of(j)[:, :, 1, :], mzr[:, :, 1, :]).then_inc(V_.h, V_.one(f"mb{j}_{g}"))
                for j in range(2):
                    s = slice(4 * j, 4 * j + 4)
                    mult(AK[:, s, :], zr_of(2 + j)[:, :, 0, :], mzr[:, :, 0, :]).then_inc(V_.h, V_.one(f"ak{j}_{g}"))
                    mult(MK[:, s, :], zr_of(2 + j)[:, :, 1, :], mzr[:, :, 1, :]).then_inc(V_.h, V_.one(f"mk{j}_{g}"))
                both = lambda a: a.rearrange("p (j q) t -> p j (q t)", j=2)
                for name, o in (("d", DD), ("l", LL)):
                    m = C(f"mask_{name}").rearrange("p (j n) -> p j n", j=1).broadcast_to((P, 2, 4 * CH))
                    mult(both(o), both(b8(4)), m).then_inc(V_.h, V_.one(f"{name}_{g}"))
                dve.wait_ge(V_.s.h, V_.s.m)
                add(E1, DT, eye).then_inc(V_.h, V_.one(f"e1_{g}"))
                dve.wait_ge(P_.h, P_.at(f"p1_{g}"))
                dve.tensor_copy(D2, b8(0)).then_inc(V_.h, V_.one(f"d2_{g}"))
                dve.wait_ge(P_.h, P_.at(f"p2_{g}"))
                dve.tensor_copy(D4, b8(2)).then_inc(V_.h, V_.one(f"d4_{g}"))
                add(E2, b8(4), E1).then_inc(V_.h, V_.one(f"e2_{g}"))
                dve.wait_ge(P_.h, P_.at(f"p3_{g}"))
                dve.wait_ge(V_.s.h, V_.s.m)
                add(E3, b8(1), E2).then_inc(V_.h, V_.one(f"e3_{g}"))
                dve.wait_ge(P_.h, P_.at(f"p4_{g}"))
                dve.wait_ge(V_.s.h, V_.s.m)
                add(E4, b8(2), E3).then_inc(V_.h, V_.one(f"e4_{g}"))
                dve.wait_ge(P_.h, P_.at(f"p5_{g}"))
                dve.tensor_copy(NTb, b8(0)).then_inc(V_.h, V_.one(f"nt_{g}"))
                add(INT_, b8(0), eye).then_inc(V_.h, V_.one(f"int_{g}"))
                dve.wait_ge(P_.h, P_.at(f"p6_{g}"))
                dve.tensor_copy(N2, b8(2)).then_inc(V_.h, V_.one(f"n2_{g}"))
                dve.wait_ge(P_.h, P_.at(f"p7_{g}"))
                dve.wait_ge(V_.s.h, V_.s.m)
                add(GG_, b8(3), INT_).then_inc(V_.h, V_.one(f"g_{g}"))
                for j in range(2):
                    old, new = v3(X[:, j, :], 4), v3(X[:, 1 - j, :], 4)
                    dve.wait_ge(P_.h, P_.at(f"u_{g}{j}"))
                    dve.tensor_copy(UU, b4(6)).then_inc(V_.h, V_.one(f"u_{g}{j}"))
                    dve.wait_ge(P_.h, P_.at(f"dx_{g}{j}"))
                    dve.wait_ge(V_.s.h, V_.s.m)
                    add(new, b4(4), old).then_inc(V_.h, V_.one(f"xa_{g}{j}"))
                    dve.wait_ge(V_.s.h, V_.s.m)
                    for d in range(2):
                        c = CHUNKS[d][2 * g + j]
                        o = new[:, 2 * d:2 * d + 2, :]
                        ins = mult(o, o, pc[:, 2 * d:2 * d + 2, c:c + 1].broadcast_to((P, 2, CH)))
                        if d:
                            ins.then_inc(V_.h, V_.one(f"xb_{g}{j}"))
            if mod:
                mod.store(dve)
        end_phase()

        fb = Arena(tmp_at)
        dv, sq, sd = fb.take(4 * T, 4), fb.take(4 * T, 4), fb.take(4 * T, 4)
        names = [f"q{q}" for q in range(4)]
        P_, A_ = Steps(S("gn_pe"), ["m" + n for n in names] + ["v" + n for n in names]), \
            Steps(S("gn_act"), ["s" + n for n in names] + ["r" + n for n in names])
        V_ = Steps(S("gn_dve"), ["d" + n for n in names] + [x + n for n in names for x in "ingb"] + ["sum0", "sum1", "o0", "o1"])

        @block.tensor
        def _(pe):
            for q in range(4):
                pe.matmul(bank(q), C("head_sum"), Y[:, q, :], start=True, stop=True).then_inc(P_.h, P_.one(f"mq{q}"))
            for q in range(4):
                pe.wait_ge(A_.h, A_.at(f"sq{q}"))
                pe.matmul(bank(4 + q), C("head_sum"), sq[:, q, :], start=True, stop=True).then_inc(P_.h, P_.one(f"vq{q}"))

        @block.scalar
        def _(act):
            for q in range(4):
                act.wait_ge(V_.h, V_.at(f"dq{q}"))
                act.activation(sq[:, q, :], dv[:, q, :], ACT.Square).then_inc(A_.h, A_.one(f"sq{q}"))
            for q in range(4):
                act.wait_ge(P_.h, P_.at(f"vq{q}"))
                act.activation(sd[:, q, :], bank(4 + q), ACT.Sqrt, bias=eps(EPS_GN), scale=1.0 / DH).then_inc(A_.h, A_.one(f"rq{q}"))

        @block.vector
        def _(dve):
            for q in range(4):
                dve.wait_ge(P_.h, P_.at(f"mq{q}"))
                dve.scalar_tensor_tensor(dv[:, q, :], bank(q), -1.0 / DH, Y[:, q, :], ALU.mult, ALU.add).then_inc(V_.h, V_.one(f"dq{q}"))
            for q in range(4):
                dve.wait_ge(A_.h, A_.at(f"rq{q}"))
                dve.reciprocal(sd[:, q, :], sd[:, q, :]).then_inc(V_.h, V_.one(f"iq{q}"))
                dve.wait_ge(V_.s.h, V_.s.m)
                dve.tensor_tensor(dv[:, q, :], dv[:, q, :], sd[:, q, :], ALU.mult).then_inc(V_.h, V_.one(f"nq{q}"))
                dve.wait_ge(V_.s.h, V_.s.m)
                dve.tensor_scalar(dv[:, q, :], dv[:, q, :], Q1(l, "gn_g", q % 2), Q1(l, "gn_b", q % 2),
                                                    ALU.mult, ALU.add).then_inc(V_.h, V_.one(f"gq{q}"))
                dve.wait_ge(V_.s.h, V_.s.m)
                dve.tensor_tensor(dv[:, q, :], dv[:, q, :], gg[:, q, :], ALU.mult).then_inc(V_.h, V_.one(f"bq{q}"))
            dve.wait_ge(V_.s.h, V_.s.m)
            for hp in range(2):
                dve.tensor_tensor(dv[:, hp, :], dv[:, hp, :], dv[:, 2 + hp, :], ALU.add).then_inc(V_.h, V_.one(f"sum{hp}"))
            dve.wait_ge(V_.s.h, V_.s.m)
            for hp in range(2):
                dve.tensor_tensor(mixT[:, 4 + hp, :], dv[:, hp, :], bon[:, hp, :], ALU.add).then_inc(V_.h, V_.one(f"o{hp}"))
        end_phase()

    def experts(l):
        a = Arena()
        key, gate = a.take(2 * N_EXP, 2), a.take(2 * N_EXP, 2)
        htok = a.take(2 * D, 2)
        at = a.at
        rt = a.take(KT * N_EXP, KT)
        W = lambda: a.take(2 * N_EXP, 2)
        lg, v1, o1, v2, o2, l2, sel = (W() for _ in range(7))
        st = [a.take(2, 2) for _ in range(8)]
        cnt = a.take(2)
        rin = S("router_loaded")

        @block.scalar
        def _(act):
            act.dma_start(rt, router_in[:, :].rearrange("p (k e) -> p k e", e=N_EXP)).then_inc(rin.h, 16)
        V_ = Steps(S("route_dve"), ["lg"] + [f"{x}0" for x in ("m", "v", "w", "x", "o")] + ["l2"] +
                   [f"{x}1" for x in ("m", "v", "w", "x", "o")] + ["dif", "sel", "one", "inv", "g2", "s0", "s1", "s2",
                                                                 "key0", "key1", "cnt0", "cnt1", "passes"])
        A_ = Steps(S("route_act"), ["t0", "e", "t1"])
        P_ = Steps(S("route_pe"), ["lg", "t0", "t1", "pos"])
        iota = con[:, CON["iota"][0]:CON["iota"][1]]

        @block.tensor
        def _(pe):
            pe.wait_ge(rin.h, 16)
            for tt in range(2):
                for k in range(KT):
                    mm = pe.matmul(bank(0)[:, tt * 8:tt * 8 + 8], hT[:, k, CTX + tt * P:CTX + (tt + 1) * P], rt[:, k, :],
                                   start=k == 0, stop=k == KT - 1)
            mm.then_inc(P_.h, P_.one("lg"))
            for tt in range(2):
                for k in range(KT):
                    b = 2 + 2 * tt + k // 4
                    mm = pe.transpose(bank(b)[:, (k % 4) * P:(k % 4 + 1) * P], hT[:, k, CTX + tt * P:CTX + (tt + 1) * P],
                                      C("ident"))
                mm.then_inc(P_.h, P_.one(f"t{tt}"))
            pe.wait_ge(V_.h, V_.at("sel"))
            pe.matmul(bank(1)[:, 0:8], C("before"), sel[:, 0, :], start=True, stop=True)
            pe.matmul(bank(1)[:, 8:16], C("ones"), sel[:, 0, :], start=True, stop=False)
            pe.matmul(bank(1)[:, 8:16], C("before"), sel[:, 1, :], start=False, stop=True)
            pe.matmul(bank(1)[:, 16:24], C("ones"), sel[:, 0, :], start=True, stop=False)
            pe.matmul(bank(1)[:, 16:24], C("ones"), sel[:, 1, :], start=False, stop=True).then_inc(P_.h, P_.one("pos"))

        @block.scalar
        def _(act):
            act.wait_ge(P_.h, P_.at("t0"))
            act.activation(htok[:, 0, :], banks[:, 2 * 512:4 * 512], ACT.Copy).then_inc(A_.h, A_.one("t0"))
            act.wait_ge(V_.h, V_.at("dif"))
            act.activation(st[3], st[2], ACT.Exp).then_inc(A_.h, A_.one("e"))
            act.wait_ge(P_.h, P_.at("t1"))
            act.activation(htok[:, 1, :], banks[:, 4 * 512:6 * 512], ACT.Copy).then_inc(A_.h, A_.one("t1"))

        @block.vector
        def _(dve):
            wide = lambda s: s.broadcast_to((P, 2, N_EXP))
            it = iota.rearrange("p (o e) -> p o e", o=1).broadcast_to((P, 2, N_EXP))
            dve.wait_ge(P_.h, P_.at("lg"))
            dve.tensor_copy(lg, v3(bank(0)[:, 0:16], 2)).then_inc(V_.h, V_.one("lg"))

            def pick(i, src, v, o):
                dve.wait_ge(V_.h, V_.s.m)
                dve.tensor_reduce(st[i], src, AX.X, ALU.max).then_inc(V_.h, V_.one(f"m{i}"))
                dve.wait_ge(V_.h, V_.s.m)
                dve.tensor_tensor(v, src, wide(st[i]), ALU.is_equal).then_inc(V_.h, V_.one(f"v{i}"))
                dve.wait_ge(V_.h, V_.s.m)
                dve.scalar_tensor_tensor(v, v, -100.0, it, ALU.mult, ALU.add).then_inc(V_.h, V_.one(f"w{i}"))
                dve.wait_ge(V_.h, V_.s.m)
                dve.tensor_reduce(st[4 + i], v, AX.X, ALU.min).then_inc(V_.h, V_.one(f"x{i}"))
                dve.wait_ge(V_.h, V_.s.m)
                dve.tensor_tensor(o, v, wide(st[4 + i]), ALU.is_equal).then_inc(V_.h, V_.one(f"o{i}"))
            pick(0, lg, v1, o1)
            dve.wait_ge(V_.h, V_.s.m)
            dve.scalar_tensor_tensor(l2, o1, NEG, lg, ALU.mult, ALU.add).then_inc(V_.h, V_.one("l2"))
            pick(1, l2, v2, o2)
            dve.wait_ge(V_.h, V_.s.m)
            dve.tensor_tensor(st[2], st[1], st[0], ALU.subtract).then_inc(V_.h, V_.one("dif"))
            dve.tensor_tensor(sel, o1, o2, ALU.add).then_inc(V_.h, V_.one("sel"))
            dve.wait_ge(A_.h, A_.at("e"))
            dve.tensor_scalar(st[6], st[3], 1.0, None, ALU.add).then_inc(V_.h, V_.one("one"))
            dve.wait_ge(V_.h, V_.s.m)
            dve.reciprocal(st[6], st[6]).then_inc(V_.h, V_.one("inv"))
            dve.wait_ge(V_.h, V_.s.m)
            dve.tensor_tensor(st[7], st[3], st[6], ALU.mult).then_inc(V_.h, V_.one("g2"))
            dve.wait_ge(V_.h, V_.s.m)
            dve.tensor_tensor(v1, o1, wide(st[6]), ALU.mult).then_inc(V_.h, V_.one("s0"))
            dve.tensor_tensor(v2, o2, wide(st[7]), ALU.mult).then_inc(V_.h, V_.one("s1"))
            dve.wait_ge(V_.h, V_.s.m)
            dve.tensor_tensor(gate, v1, v2, ALU.add).then_inc(V_.h, V_.one("s2"))
            dve.wait_ge(P_.h, P_.at("pos"))
            dve.scalar_tensor_tensor(key, v3(bank(1)[:, 0:16], 2), 1.0, sel, ALU.add, ALU.mult)\
                .then_inc(V_.h, V_.one("key0"))
            dve.wait_ge(V_.h, V_.s.m)
            dve.tensor_scalar(key, key, 1.0, None, ALU.subtract).then_inc(V_.h, V_.one("key1"))
            dve.tensor_reduce(cnt[:, 0:1], bank(1)[:, 16:24], AX.X, ALU.max).then_inc(V_.h, V_.one("cnt0"))
            dve.wait_ge(V_.h, V_.s.m)
            dve.tensor_scalar(cnt[:, 1:2], cnt[:, 0:1], P + 0.5, 1.0, ALU.is_gt, ALU.add).then_inc(V_.h, V_.one("cnt1"))
            dve.wait_ge(V_.h, V_.s.m)
            dve.tensor_copy(passes[:, :], cnt[:, 1:2]).then_inc(V_.h, V_.one("passes"))
        end_phase()

        a = Arena(at)
        sg, hid = a.take(2 * 256, 2), a.take(2 * 256, 2)
        xg_high, xg_low = ([v3(b, KT) for b in (a.take_split(KT * P), a.take_split(KT * P))] for _ in range(2))
        hid_high, hid_low = (a.take_split(2 * 256, 2) for _ in range(2))
        high = a.take_split(3 * PART, 3)
        pick_, send = ([v3(b, 2) for b in (a.take(2 * P), a.take(2 * P))] for _ in range(2))
        sent = [a.take(LAT) for _ in range(2)]
        ysb = a.take(D)
        work = [S(f"x_loaded_{i}") for i in range(RING)]
        x_loaded = work[:]
        names = ("x_used", "x_silu", "x_hidden", "x_picked", "x_gathered", "x_copied", "x_turned", "x_turned_copied",
                 "x_summed", "x_scattered", "x_added", "x_weight_high", "x_weight_low", "x_gathered_high",
                 "x_hidden_plain", "x_hidden_turned", "x_hidden_high")
        x_used, si, ac, picked, gathered, xcop, turned, tcop, summed, scat, added, wh_ok, wl_ok, xh_ok, hp, ht, hh = (
            S(n) for n in names)
        work += [S(n) for n in names]
        met, go = S("pass_met"), S("pass_go")
        N, n_units = N_EXP * FFE_UNITS, FFE_UNITS
        base = stream["put"] - stream["skew"]
        trips = (n_units - 2) // 2
        gate_bank, up_bank = (lambda U: bank(U % 2)), (lambda U: bank(2 + U % 2))
        gate_of = lambda U: 3 * U if U else 1
        up_of = lambda U: 3 * U + 1 if U else 2
        down_of = lambda U: 3 * U + 5 if U < N - 1 else 3 * N
        assert trips * 2 + 2 == n_units and 3 * n_units % RING == 0

        def passes_of(eng):
            return eng.value_load(passes[0:1, 0:1], min_val=1, max_val=2)

        def leave(eng, p):
            eng.drain().then_inc(met.h, 1)
            eng.wait_ge(go.h, 1)

        @block.gpsimd
        def _(pool):
            with pool.Fori(0, passes_of(pool)) as p:
                pool.wait_ge(met.h, 4)
                for s in work + [met]:
                    pool.sem_clear(s.h)
                pool.drain().then_inc(go.h, 1)

        @block.sync
        def _(sp):
            sp.wait_ge(S("phase_met").h, 4 * phase["n"])
            sp.wait_ge(used.h, stream["put"])
            with sp.Fori(0, passes_of(sp)) as p:
                def load(n, i=None, wait_for=None):
                    if wait_for is not None:
                        sp.wait_ge(x_used.h, wait_for)
                    src = parts[base + n, :, :] if i is None else \
                        parts[bass.ds(i * RING + (base + n), 1), :, :].rearrange("a p n -> p (a n)")
                    sp.dma_start(slots[:, n % RING, :], src).then_inc(x_loaded[n % RING].h, 16)
                for n in range(2):
                    load(n)
                for e in range(N_EXP):
                    n0 = 2 + 3 * n_units * e
                    for n in range(n0, n0 + 3):
                        load(n, None, n - RING + 1 if n >= RING else None)
                    with sp.Fori(0, trips) as i:
                        for n in range(n0 + 3, n0 + 9):
                            load(n, i, i * RING + (n - RING + 1))
                    for n in range(n0 + 3 * (n_units - 1), n0 + 3 * n_units - (2 if e == N_EXP - 1 else 0)):
                        load(n, None, n - RING + 1)
                leave(sp, p)

        def over_units(eng, e, body, static_part):
            body(e * n_units, 0, 1)
            static_part(e)
            with eng.Fori(0, trips) as i:
                for j in range(2):
                    body(e * n_units + 1 + j, i, trips)
            body((e + 1) * n_units - 1, 0, 1)

        @block.tensor
        def _(pe):
            with pe.Fori(0, passes_of(pe)) as p:
                def take(n, i):
                    pe.wait_ge(wl_ok.h, i * RING + (n + 1))
                    return high[:, n % 3, :], low_slots[:, n % RING, :]

                def product(U, n, i, which):
                    e = (U // n_units) % 2
                    wh, wl = (v3(w, KT) for w in take(n, i))
                    if which == 0:
                        pe.wait_ge(ac.h, i * 2 + (U + 1))
                    for k in range(KT):
                        for g, (x, w) in enumerate(((xg_high[e], wh), (xg_high[e], wl), (xg_low[e], wh))):
                            mm = pe.matmul((gate_bank(U), up_bank(U))[which][:, 0:256], x[:, k, :], w[:, k, :],
                                           start=k == 0 and g == 0, stop=k == KT - 1 and g == 2)
                    mm.then_inc(x_used.h, 1)

                def turn(U, i):
                    pe.wait_ge(hp.h, i * 2 + (U + 1))
                    for j in range(2):
                        mm = pe.transpose(gate_bank(U)[:, 256 + j * P:256 + (j + 1) * P], hid[:, U % 2, j * P:(j + 1) * P],
                                          C("ident"))
                    mm.then_inc(ht.h, 1)

                def down(U, n, i, times):
                    u = U % n_units
                    wh, wl = (v3(w, 2) for w in take(n, i))
                    pe.wait_ge(ac.h, i * 2 + (U + 3))
                    if u == 0 and U:
                        pe.wait_ge(summed.h, U // n_units)
                    for j in range(2):
                        for half in range(2):
                            for g, (h, w) in enumerate(((hid_high, wh), (hid_high, wl), (hid_low, wh))):
                                mm = pe.matmul(bank(4 + half), h[:, U % 2, j * P:(j + 1) * P],
                                               w[:, j, half * 512:(half + 1) * 512],
                                               start=times == 1 and u == 0 and j == 0 and g == 0,
                                               stop=times == 1 and u > 0 and j == 1 and g == 2, skip_group_check=True)
                    mm.then_inc(x_used.h, 1)

                def gather(e):
                    pe.wait_ge(picked.h, e + 1)
                    if e >= 2:
                        pe.wait_ge(added.h, 4 * (e - 1))
                    for k in range(KT):
                        for tt in range(2):
                            mm = pe.matmul(bank(6 + k // 4)[:, (k % 4) * P:(k % 4 + 1) * P], htok[:, tt, k * P:(k + 1) * P],
                                           pick_[e % 2][:, tt, :], start=tt == 0, stop=tt == 1)
                    mm.then_inc(gathered.h, 1)
                    pe.wait_ge(xcop.h, e + 1)
                    for tt in range(2):
                        mm = pe.transpose(bank(6)[:, tt * P:(tt + 1) * P], send[e % 2][:, tt, :], C("ident"))
                    mm.then_inc(turned.h, 1)

                def scatter(e):
                    pe.wait_ge(summed.h, e + 1)
                    pe.wait_ge(tcop.h, min(e + 2, N_EXP))
                    for f in range(4):
                        if f >= 2:
                            pe.wait_ge(added.h, 4 * e + f - 1)
                        for m in range(2 * f, 2 * f + 2):
                            mm = pe.matmul(bank(6 + f % 2)[:, (m % 2) * LAT:(m % 2 + 1) * LAT], ysb[:, m * P:(m + 1) * P],
                                           sent[e % 2], start=True, stop=True)
                        mm.then_inc(scat.h, 1)

                gather(0)
                product(0, 0, 0, 0)
                product(0, 1, 0, 1)

                def body(U, i, times):
                    n = 2 + 3 * U
                    if U < N - 1:
                        product(U + 1, n, i, 0)
                        turn(U, i)
                        product(U + 1, n + 1, i, 1)
                        down(U, n + 2, i, times)
                    else:
                        turn(U, i)
                        down(U, n, i, times)

                def own_part(e):
                    if e:
                        scatter(e - 1)
                    if e + 1 < N_EXP:
                        gather(e + 1)
                for e in range(N_EXP):
                    over_units(pe, e, body, own_part)
                scatter(N_EXP - 1)
                leave(pe, p)

        @block.scalar
        def _(act):
            with act.Fori(0, passes_of(act)) as p:
                def split(m, i):
                    if m < 3 * N:
                        act.wait_ge(x_loaded[m % RING].h, i * 16 + 16 * (m // RING + 1))
                        if m >= 3:
                            act.wait_ge(x_used.h, i * RING + (m - 2))
                        act.activation(high[:, m % 3, :], slots[:, m % RING, :], ACT.Copy).then_inc(wh_ok.h, 1)

                def gathered_out(e):
                    act.wait_ge(gathered.h, e + 1)
                    act.activation(xg_high[e % 2].rearrange("p k s -> p (k s)"), banks[:, 6 * 512:8 * 512], ACT.Copy)\
                        .then_inc(xh_ok.h, 1)
                    act.wait_ge(turned.h, e + 1)
                    act.activation(sent[e % 2], bank(6)[:, 0:LAT], ACT.Copy).then_inc(tcop.h, 1)

                def sums_out(e):
                    act.wait_ge(x_used.h, down_of(n_units * (e + 1) - 1))
                    if e:
                        act.wait_ge(scat.h, 4 * e)
                    act.activation(ysb, banks[:, 4 * 512:6 * 512], ACT.Copy).then_inc(summed.h, 1)

                def body(U, i, times):
                    act.wait_ge(x_used.h, i * RING + gate_of(U))
                    act.wait_ge(ac.h, i * 2 + (U + 1))
                    act.activation(sg[:, U % 2, :], gate_bank(U)[:, 0:256], ACT.Silu).then_inc(si.h, 1)
                    split(3 * U + 3, i)
                    if U and U % n_units == 0 and times == 1:
                        sums_out(U // n_units - 1)
                    split(3 * U + 4, i)
                    act.wait_ge(ht.h, i * 2 + (U + 1))
                    act.activation(hid_high[:, U % 2, :], gate_bank(U)[:, 256:512], ACT.Copy).then_inc(hh.h, 1)
                    split(3 * U + 5, i)

                def own_part(e):
                    if e + 1 < N_EXP:
                        gathered_out(e + 1)
                gathered_out(0)
                for m in range(3):
                    split(m, 0)
                for e in range(N_EXP):
                    over_units(act, e, body, own_part)
                sums_out(N_EXP - 1)
                leave(act, p)

        @block.vector
        def _(dve):
            keyed = S("key_moved")
            with dve.Fori(0, passes_of(dve)) as p:
                def choose(e):
                    for o, by_gate in ((pick_, False), (send, True)):
                        for tt in range(2):
                            kc, gc = key[:, tt, e:e + 1], gate[:, tt, e:e + 1]
                            if by_gate:
                                ins = dve.tensor_scalar(o[e % 2][:, tt, :], C("slot"), kc, gc, ALU.is_equal, ALU.mult)
                            else:
                                ins = dve.tensor_scalar(o[e % 2][:, tt, :], C("slot"), kc, None, ALU.is_equal)
                    ins.then_inc(picked.h, 1)

                def add(e):
                    for f in range(4):
                        dve.wait_ge(scat.h, 4 * e + f + 1)
                        for m in range(2 * f, 2 * f + 2):
                            xs = xT[:, m, CTX:T]
                            ins = dve.scalar_tensor_tensor(xs, bank(6 + f % 2)[:, (m % 2) * LAT:(m % 2 + 1) * LAT],
                                                           modc(l, 40 + m, 1), xs, ALU.mult, ALU.add)
                        ins.then_inc(added.h, 1)

                for j in range(2):
                    dve.memset(hid[:, j, :], 0.0).then_inc(ac.h, 1)

                def split(m, i):
                    if m < 3 * N:
                        dve.wait_ge(wh_ok.h, i * RING + (m + 1))
                        dve.tensor_tensor(low_slots[:, m % RING, :], slots[:, m % RING, :], high[:, m % 3, :].bitcast(F32),
                                          ALU.subtract).then_inc(wl_ok.h, 1)

                def gathered_low(e):
                    dve.wait_ge(xh_ok.h, e + 1)
                    dve.tensor_tensor(xg_low[e % 2].rearrange("p k s -> p (k s)"), banks[:, 6 * 512:8 * 512],
                                      xg_high[e % 2].rearrange("p k s -> p (k s)").bitcast(F32), ALU.subtract)\
                        .then_inc(xcop.h, 1)
                choose(0)
                gathered_low(0)
                for m in range(3):
                    split(m, 0)

                def body(U, i, times):
                    dve.wait_ge(x_used.h, i * RING + up_of(U))
                    dve.wait_ge(si.h, i * 2 + (U + 1))
                    dve.tensor_tensor(hid[:, U % 2, :], up_bank(U)[:, 0:256], sg[:, U % 2, :], ALU.mult).then_inc(hp.h, 1)
                    split(3 * U + 3, i)
                    split(3 * U + 4, i)
                    dve.wait_ge(hh.h, i * 2 + (U + 1))
                    dve.tensor_tensor(hid_low[:, U % 2, :], gate_bank(U)[:, 256:512], hid_high[:, U % 2, :].bitcast(F32),
                                      ALU.subtract).then_inc(ac.h, 1)
                    split(3 * U + 5, i)

                def own_part(e):
                    if e + 1 < N_EXP:
                        choose(e + 1)
                    if e:
                        add(e - 1)
                    if e + 1 < N_EXP:
                        gathered_low(e + 1)
                for e in range(N_EXP):
                    over_units(dve, e, body, own_part)
                add(N_EXP - 1)
                dve.tensor_scalar(key, key, float(P), None, ALU.subtract).then_inc(picked.h, 1)
                leave(dve, p)
        stream["skew"] -= 3 * N
        end_phase()

        @block.sync
        def _(sp):
            sp.wait_ge(S("phase_met").h, 4 * phase["n"])

    def mixer_inputs(l):
        ctx_out = l < DEPTH - 1
        first = 0 if ctx_out else CTX
        a = Arena()
        us = a.take(10 * T, 10)
        glu = a.take(2 * 2 * (CTX + 2 * CV_PAD)).rearrange("p (i s t) -> p i s t", i=2, s=2)
        q, k, v = a.take(4 * T, 4), a.take(4 * T, 4), a.take(4 * T, 4)
        bias = a.take(2 * NA_H * LAT, 2 * NA_H)
        at = a.at
        gate = a.take(2 * T, 2)
        rw_tiles = [dict(part=6 + t // 2, j=t % 2, cols=(0, T), owner="dve") for t in range(10)]
        tiles = [dict(part=t // 2, j=t % 2, cols=(first, T), owner="act") for t in range(4)]
        tiles += [dict(part=2 + t // 2, j=t % 2, cols=(0, T), owner="act") for t in range(4)]
        tiles += [dict(part=4 + p, tok=t, cols=(0, T), owner="act") for p in range(2) for t in range(4)]
        tiles += rw_tiles
        tiles += [dict(part=11, j=t, cols=(first, T), owner="act") for t in range(2)]
        tiles += [dict(part=12, j=t, cols=(first, T), owner="dve") for t in range(2)]
        tile_done, free, next_high, next_low = project(tiles, "h", (0, T), a.take_split(HIGHS * PART, HIGHS))
        own_part, sig, b_in, b_ok = S("shift_own"), S("conv_gate"), S("bias_loaded"), S("bias_masked")

        @block.scalar
        def _(act):
            act.dma_start(bias, bias_in[l, :, :].rearrange("p (q k) -> p q k", k=LAT)).then_inc(b_in.h, 16)
            for t in range(len(tiles)):
                bk = bank(t % 8)
                act.wait_ge(*tile_done(t))
                if t < 4:
                    act.activation(q[:, t, first:T], bk[:, 0:T - first], ACT.Copy, scale=DH ** -0.5).then_inc(free["act"].h, free["act"].one())
                elif t < 8:
                    act.activation(k[:, t - 4, :], bk, ACT.Copy).then_inc(free["act"].h, free["act"].one())
                elif t < 16:
                    p, tok = divmod(t - 8, 4)
                    act.activation(v[:, tok, p * UNIT:(p + 1) * UNIT], bk[:, 0:UNIT], ACT.Copy).then_inc(free["act"].h, free["act"].one())
                elif t < 26:
                    act.activation(us[:, t - 16, :], bk, ACT.Copy, scale=scal[l][:, 32 + t - 16:33 + t - 16]).then_inc(own_part.h, own_part.one())
                elif t < 28:
                    act.activation(gate[:, t - 26, first:T], bk[:, 0:T - first], ACT.Sigmoid).then_inc(free["act"].h, free["act"].one())
                next_high(act, t)

        @block.vector
        def _(dve):
            own_pad = S("conv_pad")
            for s in range(2):
                dve.memset(glu[:, :, s, 0:CV_PAD], 0.0).then_inc(own_pad.h, own_pad.one())
                dve.memset(glu[:, :, s, CV_PAD + CTX:], 0.0).then_inc(own_pad.h, own_pad.one())
            dve.wait_ge(b_in.h, 16 * (l + 1))
            for h in range(2):
                bh = bias[:, h * NA_H:(h + 1) * NA_H, :].rearrange("p h (r c) -> p (h r) c", c=64)
                for i, (name, op) in enumerate((("win", ALU.mult), ("out_win", ALU.add))):
                    dve.wait_ge(b_ok.h, b_ok.at(2 * h + i))
                    m = C(name).rearrange("p (o k) -> p o k", o=1).broadcast_to((P, NA_H * 4, 64))
                    dve.tensor_tensor(bh, bh, m, op).then_inc(b_ok.h, b_ok.one())
            side = S("shift_side")
            for t in range(16):
                next_low(dve, t)
            for t in range(16, 26):
                i = t - 16
                dve.wait_ge(own_part.h, own_part.at(i + 1))
                u3, p3 = (x.rearrange("p (s t) -> p s t", s=2) for x in (us[:, i, :], bank(t % 8)))
                dve.scalar_tensor_tensor(u3[:, :, 1:CTX], p3[:, :, 0:CTX - 1], Q1(l, "mu_prev", i), u3[:, :, 1:CTX],
                                                  ALU.mult, ALU.add).then_inc(side.h, side.one())
                dve.wait_ge(side.h, side.at(i + 1))
                dve.scalar_tensor_tensor(u3[:, :, 0:CTX - 1], p3[:, :, 1:CTX], Q1(l, "mu_next", i),
                                                         u3[:, :, 0:CTX - 1], ALU.mult, ALU.add).then_inc(free["dve"].h, free["dve"].one())
                next_low(dve, t)
            for t in range(28, 30):
                i = t - 28
                dve.wait_ge(*tile_done(t))
                dve.wait_ge(free["act"].h, free["act"].at(18))
                ns = (T - first) // CTX
                dve.tensor_tensor(glu[:, i, 2 - ns:2, CV_PAD:CV_PAD + CTX],
                                                  bank(t % 8)[:, 0:T - first].rearrange("p (s t) -> p s t", s=ns),
                                                  gate[:, i, first:T].rearrange("p (s t) -> p s t", s=ns), ALU.mult).then_inc(free["dve"].h, free["dve"].one())
        end_phase()
        units = []
        for h in range(NA_H):
            for t in range(2):
                units.append((h // 2, h % 2, CTX + t * P, [(CTX, T), (0, CTX)], [2, 3, 0, 1], bias[:, t * NA_H + h, :], CTX))
        k_same, v_cols = (lambda tile: tile), (lambda tile, half: tile * P + half * DH)
        taps = Taps(l, glu, 0 if ctx_out else 1, at)
        attention(units, q, k, v, 1.0, LAT, k_same, v_cols, taps.at, taps)
        if ctx_out:
            units = [(h // 2, h % 2, t * P, [(0, CTX)], [0, 1], None, 0) for h in range(NA_H) for t in range(2)]
            attention(units, q, k, v, 1.0, CTX, k_same, v_cols, taps.at)
        conformer(l, taps, 0 if ctx_out else 1)
        recurrence(l, us, 10 * T)

    def second_mixers(l):
        a = Arena()
        qk = a.take(5 * LAT, 5)
        v = a.take(2 * P, 2)
        sv, su, cb, cc = (a.take(2 * LAT, 2) for _ in range(4))
        cx = a.take(2 * (LAT + 2), 2)
        qn, sq, sd = a.take(5 * LAT, 5), a.take(7 * LAT, 7), a.take(6 * LAT, 6)
        vnt, sgw, sgb, cv = a.take(2 * 2 * P, 2), a.take(4 * P, 4), a.take(P), a.take(2 * LAT, 2)
        at = a.at
        lat = (CTX, T)
        tiles = [dict(part=t // 2, j=t % 2, cols=lat, owner="act") for t in range(4)]
        tiles += [dict(part=2, j=0, cols=lat, owner="act")]
        tiles += [dict(part=2, tok=2 + t, cols=lat, owner="act") for t in range(2)]
        tiles += [dict(part=3 + t // 2, j=t % 2, cols=lat, owner="act") for t in range(8)]
        tiles += [dict(part=7, j=t, cols=lat, owner="dve") for t in range(2)]
        tile_done, free, next_high, next_low = project(tiles, "h", lat, Arena(at).take_split(3 * PART, 3))
        s_in = S("gating_loaded")

        @block.scalar
        def _(act):
            act.dma_start(sgw, sgw_in[l, :, :].rearrange("p (h n) -> p h n", h=4)).then_inc(s_in.h, 16)
            act.dma_start(sgb[0:4, :], sgb_in[l, :, :]).then_inc(s_in.h, 16)
            for t in range(15):
                act.wait_ge(*tile_done(t))
                bk = bank(t % 8)
                if t < 5:
                    o = qk[:, t, :]
                elif t < 7:
                    o = v[:, t - 5, :]
                else:
                    o = (sv, su, cb, cc)[(t - 7) // 2][:, (t - 7) % 2, :]
                at_ = P if 5 <= t < 7 else 0
                act.activation(o, bk[:, at_:LAT], ACT.Copy).then_inc(free["act"].h, free["act"].one())
                next_high(act, t)

        @block.vector
        def _(dve):
            pad = S("conv_pad")
            dve.memset(cx[:, :, 0:1], 0.0).then_inc(pad.h, pad.one())
            dve.memset(cx[:, :, LAT + 1:LAT + 2], 0.0).then_inc(pad.h, pad.one())
            for t in range(15):
                next_low(dve, t)
            for i in range(2):
                dve.wait_ge(*tile_done(15 + i))
                dve.wait_ge(free["act"].h, free["act"].at(15))
                dve.tensor_tensor(cx[:, i, 1:LAT + 1], bank((15 + i) % 8)[:, 0:LAT], cc[:, i, :], ALU.mult).then_inc(free["dve"].h, free["dve"].one())
        end_phase()

        sA, sP, sV = S("m2_act"), S("m2_pe"), S("m2_dve")
        A_ = Steps(sA, [f"sq{t}" for t in range(7)] + [f"rt{t}" for t in range(6)] + ["tn0", "tn1"])
        P_ = Steps(sP, [f"ms{t}" for t in range(6)] + [f"sw{t}" for t in range(5)] + ["vt", "mixed"])
        V_ = Steps(sV, ["c00", "c01", "c10", "c11", "c20", "c21", "cm0", "cm1"] + [f"i{t}" for t in range(6)] +
                   [f"n{t}" for t in range(7)] + [f"{x}{t}" for t in range(5) for x in ("sin", "cos", "rot")] + ["g0", "g1"])
        bk = lambda t: bank(t)[:, 0:LAT]

        @block.scalar
        def _(act):
            for t in range(7):
                act.activation(sq[:, t, :], qk[:, t, :] if t < 5 else sv[:, t - 5, :], ACT.Square).then_inc(A_.h, A_.one(f"sq{t}"))
            for t in range(6):
                act.wait_ge(P_.h, P_.at(f"ms{t}"))
                act.activation(sd[:, t, :], bk(t), ACT.Sqrt, bias=eps(EPS_RMS),
                                                 scale=1.0 / DH if t < 5 else 1.0).then_inc(A_.h, A_.one(f"rt{t}"))
            act.wait_ge(P_.h, P_.at("vt"))
            for c in range(2):
                act.activation(vnt[:, c, :], bank(6)[:, c * 256:(c + 1) * 256], ACT.Copy).then_inc(A_.h, A_.one(f"tn{c}"))

        @block.tensor
        def _(pe):
            for t in range(5):
                pe.wait_ge(A_.h, A_.at(f"sq{t}"))
                pe.matmul(bk(t), C("head_sum"), sq[:, t, :], start=True, stop=True).then_inc(P_.h, P_.one(f"ms{t}"))
            pe.wait_ge(A_.h, A_.at("sq6"))
            for i in range(2):
                mm = pe.matmul(bk(5), C("mean_cv"), sq[:, 5 + i, :], start=i == 0, stop=i == 1)
            mm.then_inc(P_.h, P_.one("ms5"))
            for t in range(5):
                pe.wait_ge(V_.h, V_.at(f"n{t}"))
                pe.matmul(bk(t), C("swap"), qn[:, t, :],
                                            start=True, stop=True).then_inc(P_.h, P_.one(f"sw{t}"))
            pe.wait_ge(V_.h, V_.at("n6"))
            for c in range(2):
                for i in range(2):
                    mm = pe.transpose(bank(6)[:, c * 256 + i * P:c * 256 + (i + 1) * P], sq[:, 5 + i, c * P:(c + 1) * P],
                                      C("ident"))
            mm.then_inc(P_.h, P_.one("vt"))
            pe.wait_ge(A_.h, A_.at("tn1"))
            pe.wait_ge(s_in.h, 32 * (l + 1))
            for h in range(4):
                hs = slice((h % 2) * DH, (h % 2) * DH + DH)
                for c in range(2):
                    o = bank(7)[hs, (h // 2) * LAT + c * P:(h // 2) * LAT + (c + 1) * P]
                    pe.matmul(o, vnt[:, c, h * DH:(h + 1) * DH], sgw[:, h, :], start=True, stop=False)
                    lo = CON["sel"][0] + h * P
                    mm = pe.matmul(o, con[0:4, lo:lo + DH], sgb[0:4, :], start=False, stop=True)
            mm.then_inc(P_.h, P_.one("mixed"))

        @block.vector
        def _(dve):
            for tap in range(3):
                dve.wait_ge(sV.h, sV.m)
                for i in range(2):
                    w, x = Q2(l, "conv_w", 2 * tap + i), cx[:, i, tap:tap + LAT]
                    ins = dve.tensor_scalar(cv[:, i, :], x, w, None, ALU.mult) if tap == 0 else \
                        dve.scalar_tensor_tensor(cv[:, i, :], x, w, cv[:, i, :], ALU.mult, ALU.add)
                    ins.then_inc(V_.h, V_.one(f"c{tap}{i}"))
            dve.wait_ge(sV.h, sV.m)
            for i in range(2):
                dve.tensor_tensor(mixT[:, 6 + i, CTX:T], cv[:, i, :], cb[:, i, :], ALU.mult).then_inc(V_.h, V_.one(f"cm{i}"))
            for t in range(6):
                dve.wait_ge(A_.h, A_.at(f"rt{t}"))
                dve.reciprocal(sd[:, t, :], sd[:, t, :]).then_inc(V_.h, V_.one(f"i{t}"))
            dve.wait_ge(sV.h, sV.m)
            for t in range(5):
                dve.scalar_tensor_tensor(qn[:, t, :], qk[:, t, :], Q2(l, "q_g" if t < 4 else "k_g", 0),
                                                          sd[:, t, :], ALU.mult, ALU.mult).then_inc(V_.h, V_.one(f"n{t}"))
            dve.wait_ge(P_.h, P_.at("ms5"))
            for i in range(2):
                dve.scalar_tensor_tensor(sq[:, 5 + i, :], sv[:, i, :], Q2(l, "sg_g", i), sd[:, 5, :],
                                                              ALU.mult, ALU.mult).then_inc(V_.h, V_.one(f"n{5 + i}"))
            for t in range(5):
                dve.wait_ge(P_.h, P_.at(f"sw{t}"))
                dve.tensor_tensor(qk[:, t, :], bk(t), C("sin"),
                                                     ALU.mult).then_inc(V_.h, V_.one(f"sin{t}"))
                dve.tensor_tensor(qn[:, t, :], qn[:, t, :], C("cos"), ALU.mult).then_inc(V_.h, V_.one(f"cos{t}"))
                dve.wait_ge(sV.h, sV.m)
                dve.tensor_tensor(qk[:, t, :], qk[:, t, :], qn[:, t, :], ALU.add).then_inc(V_.h, V_.one(f"rot{t}"))
            dve.wait_ge(P_.h, P_.at("mixed"))
            for i in range(2):
                dve.tensor_tensor(mixT[:, 4 + i, CTX:T], bank(7)[:, i * LAT:(i + 1) * LAT], su[:, i, :],
                                                   ALU.mult).then_inc(V_.h, V_.one(f"g{i}"))
        end_phase()
        units = [(j, g, t * P, [(0, LAT)], [0, 1], None, CTX) for j in range(4) for g in range(2) for t in range(2)]
        attention(units, qk, qk, v, DH ** -0.5, LAT, lambda tile: 4, lambda tile, half: half * DH, at)

    ready, late = S("inputs_loaded"), S("tokens_loaded")

    @block.scalar
    def _(act):
        act.dma_start(ct[:, :], ct_in[:, :]).then_inc(ready.h, 16)
        act.dma_start(con[:, :], con_in[:, :]).then_inc(ready.h, 16)
        for l in range(DEPTH):
            act.dma_start(par1[l][:, :], par1_in[l, :, :]).then_inc(ready.h, 16)
        act.dma_start(x_buf[:, :], xt_in[:, :]).then_inc(late.h, 16)
        for l in range(DEPTH):
            act.dma_start(par2[l][:, :], par2_in[l, :, :]).then_inc(late.h, 16)
        act.wait_ge(ready.h, 16 * 4)
        act.activation(ct[:, :], ct[:, :], ACT.Silu).then_inc(S("condition").h, S("condition").one())
    end_phase()

    def gated(l_gate, s):
        def put(dve, m, acc):
            cols = xT[:, m, s * CTX:(s + 1) * CTX]
            if l_gate:
                ins = dve.scalar_tensor_tensor(cols, acc, modc(l_gate - 1, 40 + m, s), cols, ALU.mult, ALU.add)
            else:
                ins = dve.tensor_tensor(cols, acc, cols, ALU.add)
            ins.then_inc(S("residual").h, S("residual").one())
        return put

    modulation([(0, 0, 16)], late)
    for l in range(DEPTH):
        ctx_out = l < DEPTH - 1
        cols = (0, T) if ctx_out else (CTX, T)
        norm(xT, hT, (0, T), gain1(l), lambda t, s: modc(l, t, s), "1")
        mixer_inputs(l)
        out_project(cols, lambda t, s: modc(l, 16 + t, s))
        norm(xT, hT, cols, gain2(l), lambda t, s: modc(l, 24 + t, s), "2")
        if l % 2 == 0:
            feed_forward("silu", FF_UNITS, CTX, gated(l + 1, 1))
            if ctx_out:
                stream["skew"] += 3 * FF_UNITS
                feed_forward("silu", FF_UNITS, 0, gated(l + 1, 0))
        else:
            experts(l)
    lat = (CTX, T)
    norm(xT, xT, lat, lambda k, s: Q1(0, "final_g", k), None, "final")
    for l in range(DEPTH):
        norm(xT, hT, lat, lambda k, s, l=l: Q2(l, "norm1_g", k), None, "1")
        second_mixers(l)
        out_project(lat, None)
        norm(xT, hT, lat, lambda k, s, l=l: Q2(l, "norm2_g", k), None, "2")
        feed_forward("conv", FF_UNITS, CTX, gated(False, 1),
                     taps=lambda tap, t, l=l: Q2(l, "ffn_w", 44 * tap + t))

    @block.scalar
    def _(act):
        stored = S("output_stored")
        act.dma_start(out[:, :].rearrange("p (k t) -> p k t", k=KT), xT[:, :, CTX:T]).then_inc(stored.h, 16)
        act.wait_ge(stored.h, 16)
    assert stream["put"] == stream["got"]
    ctx.close()
    return stream["got"] - stream["skew"]


def cols_of(w):
    n = w.shape[1] // UNIT
    return w.reshape(KT, P, n, UNIT).transpose(2, 1, 0, 3).reshape(n, P, PART)


def rows_of(w):
    n = w.shape[0] // UNIT
    return w.reshape(n, 2, P, D).transpose(0, 2, 1, 3).reshape(n, P, PART)


def ff_parts(gate, up, down):
    n = len(gate)
    out = [gate[0], up[0]]
    for u in range(1, n):
        out += [gate[u], up[u], down[u - 1]]
    return out + [down[n - 1]]


def columns(v):
    return np.asarray(v).reshape(-1, P).T


def kernel(**i):
    import concourse.bacc as bacc
    from concourse.bass_utils import run_bass_kernel_spmd as run

    i = {k: np.asarray(v) for k, v in i.items()}
    parts = []
    mod = [list(cols_of(w)) for w in i["mod_w"]]
    parts += mod[0][:8]
    for l in range(DEPTH):
        w = i["w_in"][l]
        o_cv = 3 * NA_W + RW_IN
        parts += list(cols_of(w[:, :o_cv])) + list(cols_of(w[:, o_cv + 256:])) + list(cols_of(w[:, o_cv:o_cv + 256]))
        if l == 0:
            parts += mod[0][8:] + mod[1]
        parts += list(cols_of(i["w_out"][l]))
        if l % 2 == 0:
            j = l // 2
            parts += ff_parts(cols_of(i["ffn_w_gate"][j]), cols_of(i["ffn_w_up"][j]), rows_of(i["ffn_w_down"][j]))
        else:
            j = l // 2
            parts += ff_parts([p for e in range(N_EXP) for p in cols_of(i["moe_w_gate"][j, e])],
                              [p for e in range(N_EXP) for p in cols_of(i["moe_w_up"][j, e])],
                              [p for e in range(N_EXP) for p in rows_of(i["moe_w_down"][j, e])])
    for l in range(DEPTH):
        w = i["w_in_2"][l]
        heads = [h * DH + f for t in range(4) for h in (t, t + 4) for f in range(DH)]
        q, kv, su, sv, rest = w[:, :512][:, heads], w[:, 512:768], w[:, 768:1024], w[:, 1024:1280], w[:, 1280:]
        parts += list(cols_of(np.concatenate([q, kv, sv, su, rest], 1)))
        wo = i["w_out_2"][l]
        parts += list(cols_of(np.concatenate([wo[:512][heads], wo[512:]], 0)))
        up = i["ffn_w_up_2"][l]
        parts += ff_parts(cols_of(up[:, :D_FF]), cols_of(up[:, D_FF:]), rows_of(i["ffn_w_down_2"][l]))
    n_parts = len(parts)
    xt = np.concatenate([i["ctx"][0], i["x"][0]], 0).T.reshape(KT, P, T).transpose(1, 0, 2).reshape(P, KT * T)
    ct = np.stack([i["c_ctx"], i["c"][0]], 1).reshape(KT, P, 2).transpose(1, 0, 2).reshape(P, KT * 2)
    par1, par2, lora, gate2, bias = [], [], [], [], []
    qr, qc = np.arange(LAT) // 64, np.arange(LAT) % 64
    r_at = qr[None, :] - qr[:, None] + 7
    c_at = qc[None, :] - qc[:, None] + 15
    near = (c_at >= 0) & (c_at <= 30)
    for l in range(DEPTH):
        vec = dict(norm1_g="norm1_g", norm2_g="norm2_g", mod_b="mod_b", mu_prev="rw_mu_prev", mu_next="rw_mu_next",
                   w0="rw_w0", a0="rw_a0", k_k="rw_k_k", k_a="rw_k_a", r_k="rw_r_k", gn_g="rw_gn_g", gn_b="rw_gn_b",
                   cv_b="cv_dw_b", cv_g="cv_ln_g", cv_beta="cv_ln_b", cv_w="cv_dw_w")
        par1.append(np.concatenate([columns(i["final_g"] if n == "final_g" else i[vec[n]][l]) for n in P1], 1))
        q_g, k_g = (np.concatenate([i[n][l]] * 2) for n in ("q_norm_g_2", "k_norm_g_2"))
        par2.append(np.concatenate([columns(v) for v in (i["norm1_g_2"][l], i["norm2_g_2"][l], q_g, k_g, i["sg_norm_g_2"][l],
                                                         i["conv_w_2"][l], i["ffn_conv_w_2"][l])], 1))
        lora.append(np.concatenate([i["rw_w2"][l], i["rw_a2"][l]], 1).transpose(1, 0, 2).reshape(P, 512))
        gate2.append(i["rw_g2"][l].transpose(1, 0, 2).reshape(P, 512))
        b = i["na_rpb"][l][:, r_at, np.clip(c_at, 0, 30)]
        b = np.where(near, b, np.float32(0))
        bias.append(b.reshape(NA_H, 2, P, LAT).transpose(2, 1, 0, 3).reshape(P, -1))
    router = i["moe_router"][0].reshape(KT, P, N_EXP).transpose(1, 0, 2).reshape(P, KT * N_EXP)
    sgw = i["sg_w_2"].transpose(0, 3, 1, 2).reshape(DEPTH, P, 4 * P)
    arrays = {
        "parts": np.stack(parts), "xt": xt, "ct": ct, "con": constants(), "par1": np.stack(par1), "par2": np.stack(par2),
        "lora": np.stack(lora), "gate2": np.stack(gate2), "router": router, "bias": np.stack(bias), "sgw": sgw,
        "sgb": i["sg_b_2"],
    }
    nc = bacc.Bacc("TRN2", target_bir_lowering=False, num_devices=1)
    args = []
    for name, a in arrays.items():
        arrays[name] = np.ascontiguousarray(a)
        args.append(nc.dram_tensor(name, a.shape, F32, kind="ExternalInput").ap())
    args.append(nc.dram_tensor("out", (P, KT * LAT), F32, kind="ExternalOutput").ap())
    assert build(nc, *args) == n_parts
    got = run(nc, [arrays], core_ids=[0]).results[0]["out"]
    return got.reshape(P, KT, LAT).transpose(2, 1, 0).reshape(1, LAT, D)
```
